# Optimizing a Trainium2 kernel written in Bass

```python
import math
import jax, jax.numpy as jnp
from jax import lax
import numpy as np

D_MODEL = 1024
BATCH = 1
SEQ = 1024
DEPTH = 1

CHUNK = 64
Q_BLOCK = 128
MEM_LEN = 256
MIX_WIDTH = D_MODEL
FOX_WIDTH = MIX_WIDTH // 2
FOX_HEADS = 8
FOX_HEAD_DIM = FOX_WIDTH // FOX_HEADS
GLA_WIDTH = MIX_WIDTH - FOX_WIDTH
GLA_HEADS = 4
GLA_VAL_DIM = GLA_WIDTH // GLA_HEADS
GLA_KEY_DIM = GLA_VAL_DIM // 2
GLA_QK = GLA_HEADS * GLA_KEY_DIM
GLA_GATE_RANK = 16
GLA_GATE_NORM = 16.0
MEM_HEADS = 4
MEM_HEAD_DIM = D_MODEL // MEM_HEADS
D_FF = 128 * (-(-8 * D_MODEL // (3 * 128)))
RMS_EPS = 1e-6

OFF_FQ = 0
OFF_FK = OFF_FQ + FOX_WIDTH
OFF_FV = OFF_FK + FOX_WIDTH
OFF_FF = OFF_FV + FOX_WIDTH
OFF_GQ = OFF_FF + FOX_HEADS
OFF_GK = OFF_GQ + GLA_QK
OFF_GV = OFF_GK + GLA_QK
OFF_GG = OFF_GV + GLA_WIDTH
OFF_GR = OFF_GG + GLA_GATE_RANK
IN_WIDTH = OFF_GR + GLA_WIDTH

kernel_name = 'hybrid_fox_gla_macaron_memory_layer'

F32 = jnp.float32

def rms_norm(x, g):
    xf = x.astype(F32)
    y = xf * lax.rsqrt(jnp.mean(xf * xf, axis=-1, keepdims=True) + RMS_EPS)
    return (y * g.astype(F32)).astype(x.dtype)

def head_rms_norm(o, g):
    B, S, H, d = o.shape
    y = o * lax.rsqrt(jnp.mean(o * o, axis=-1, keepdims=True) + RMS_EPS)
    return (y * g.astype(F32).reshape(H, d)).reshape(B, S, H * d)

def swiglu(h, w_gate, w_up, w_down):
    return (jax.nn.silu(h @ w_gate) * (h @ w_up)) @ w_down

def forgetting_attention(q, k, v, log_f):
    B, S, H, dh = q.shape
    qf = (q.astype(F32) * (dh ** -0.5)).transpose(0, 2, 1, 3)
    kf = k.astype(F32).transpose(0, 2, 1, 3)
    vf = v.astype(F32).transpose(0, 2, 1, 3)
    c = jnp.cumsum(log_f, axis=1).transpose(0, 2, 1)
    outs = []
    for i in range(S // Q_BLOCK):
        q0 = i * Q_BLOCK
        L = q0 + Q_BLOCK
        s = jnp.einsum('bhqd,bhkd->bhqk', qf[:, :, q0:L], kf[:, :, :L])
        s = s + c[:, :, q0:L, None] - c[:, :, None, :L]
        mask = jnp.arange(L)[None, :] <= (q0 + jnp.arange(Q_BLOCK))[:, None]
        p = jax.nn.softmax(jnp.where(mask, s, -jnp.inf), axis=-1)
        outs.append(jnp.einsum('bhqk,bhkd->bhqd', p, vf[:, :, :L]))
    return jnp.concatenate(outs, axis=2).transpose(0, 2, 1, 3)

def gla_chunked(q, k, v, log_a):
    B, S, H, dk = q.shape
    dv = v.shape[-1]
    N = S // CHUNK

    def to_chunks(t):
        return t.astype(F32).reshape(B, N, CHUNK, H, t.shape[-1]).transpose(0, 3, 1, 2, 4)

    qc = to_chunks(q) * (dk ** -0.5)
    kc = to_chunks(k)
    vc = to_chunks(v)
    b = jnp.cumsum(to_chunks(log_a), axis=3)
    b_last = b[:, :, :, -1:, :]
    q_dec = qc * jnp.exp(b)
    k_inv = kc * jnp.exp(-b)
    causal = jnp.tril(jnp.ones((CHUNK, CHUNK), dtype=bool))
    att = jnp.where(causal, jnp.einsum('bhncd,bhnsd->bhncs', q_dec, k_inv), 0.0)
    o_intra = jnp.einsum('bhncs,bhnse->bhnce', att, vc)
    kv = jnp.einsum('bhncd,bhnce->bhnde', kc * jnp.exp(b_last - b), vc)
    decay = jnp.exp(b_last[:, :, :, 0, :])

    def step(state, inp):
        dec, kv_n = inp
        return dec[..., None] * state + kv_n, state

    s0 = jnp.zeros((B, H, dk, dv), F32)
    _, s_prev = lax.scan(step, s0, (jnp.moveaxis(decay, 2, 0), jnp.moveaxis(kv, 2, 0)))
    s_prev = jnp.moveaxis(s_prev, 0, 2)
    o = o_intra + jnp.einsum('bhncd,bhnde->bhnce', q_dec, s_prev)
    return o.transpose(0, 2, 3, 1, 4).reshape(B, S, H, dv)

def hybrid_mixer(h, w_in, b_f, w_g2, b_g, g_fox_out, g_gla_out, w_out):
    B, S, _ = h.shape
    z = h @ w_in
    fq = z[..., OFF_FQ:OFF_FK].reshape(B, S, FOX_HEADS, FOX_HEAD_DIM)
    fk = z[..., OFF_FK:OFF_FV].reshape(B, S, FOX_HEADS, FOX_HEAD_DIM)
    fv = z[..., OFF_FV:OFF_FF].reshape(B, S, FOX_HEADS, FOX_HEAD_DIM)
    log_f = jax.nn.log_sigmoid((z[..., OFF_FF:OFF_GQ] + b_f).astype(F32))
    o_fox = head_rms_norm(forgetting_attention(fq, fk, fv, log_f), g_fox_out)
    gq = z[..., OFF_GQ:OFF_GK].reshape(B, S, GLA_HEADS, GLA_KEY_DIM)
    gk = z[..., OFF_GK:OFF_GV].reshape(B, S, GLA_HEADS, GLA_KEY_DIM)
    gv = z[..., OFF_GV:OFF_GG].reshape(B, S, GLA_HEADS, GLA_VAL_DIM)
    gate = (z[..., OFF_GG:OFF_GR] @ w_g2 + b_g).astype(F32)
    log_a = (jax.nn.log_sigmoid(gate) / GLA_GATE_NORM).reshape(B, S, GLA_HEADS, GLA_KEY_DIM)
    o_gla = head_rms_norm(gla_chunked(gq, gk, gv, log_a), g_gla_out)
    o_gla = o_gla * jax.nn.silu(z[..., OFF_GR:IN_WIDTH].astype(F32))
    o = jnp.concatenate([o_fox, o_gla], axis=-1).astype(h.dtype)
    return o @ w_out

def memory_cross_attention(h, m, w_q, w_kv, w_o):
    B, S, _ = h.shape
    M = m.shape[1]
    q = (h @ w_q).reshape(B, S, MEM_HEADS, MEM_HEAD_DIM).astype(F32)
    kv = (m @ w_kv).reshape(B, M, 2, MEM_HEADS, MEM_HEAD_DIM).astype(F32)
    s = jnp.einsum('bqhd,bkhd->bhqk', q, kv[:, :, 0]) * (MEM_HEAD_DIM ** -0.5)
    p = jax.nn.softmax(s, axis=-1)
    o = jnp.einsum('bhqk,bkhd->bqhd', p, kv[:, :, 1]).reshape(B, S, MEM_HEADS * MEM_HEAD_DIM)
    return o.astype(h.dtype) @ w_o

def setup_inputs(seed: int = 0) -> dict:
    key = jax.random.key(seed)
    ks = iter(jax.random.split(key, 32))

    def normal(shape, scale):
        return jax.random.normal(next(ks), shape, F32) * scale

    def gain(n):
        return 1.0 + normal((DEPTH, n), 0.1)

    Ld = DEPTH
    return {
        'x': normal((BATCH, SEQ, D_MODEL), 1.0),
        'mem': normal((BATCH, MEM_LEN, D_MODEL), 1.0),
        'g_ff1_pre': gain(D_MODEL),
        'w_ff1_gate': normal((Ld, D_MODEL, D_FF), D_MODEL ** -0.5),
        'w_ff1_up': normal((Ld, D_MODEL, D_FF), D_MODEL ** -0.5),
        'w_ff1_down': normal((Ld, D_FF, D_MODEL), D_FF ** -0.5),
        'g_ff1_post': gain(D_MODEL),
        'g_mix_pre': gain(D_MODEL),
        'w_mix_in': normal((Ld, D_MODEL, IN_WIDTH), D_MODEL ** -0.5),
        'b_fox_f': 2.0 + normal((Ld, FOX_HEADS), 0.5),
        'w_gla_g2': normal((Ld, GLA_GATE_RANK, GLA_QK), GLA_GATE_RANK ** -0.5),
        'b_gla_g': normal((Ld, GLA_QK), 0.1),
        'g_fox_out': gain(FOX_WIDTH),
        'g_gla_out': gain(GLA_WIDTH),
        'w_mix_out': normal((Ld, MIX_WIDTH, D_MODEL), MIX_WIDTH ** -0.5),
        'g_mix_post': gain(D_MODEL),
        'g_mem_pre': gain(D_MODEL),
        'g_mem_src': gain(D_MODEL),
        'w_mem_q': normal((Ld, D_MODEL, MEM_HEADS * MEM_HEAD_DIM), D_MODEL ** -0.5),
        'w_mem_kv': normal((Ld, D_MODEL, 2 * MEM_HEADS * MEM_HEAD_DIM), D_MODEL ** -0.5),
        'w_mem_o': normal((Ld, MEM_HEADS * MEM_HEAD_DIM, D_MODEL), (MEM_HEADS * MEM_HEAD_DIM) ** -0.5),
        'g_mem_post': gain(D_MODEL),
        'g_ff2_pre': gain(D_MODEL),
        'w_ff2_gate': normal((Ld, D_MODEL, D_FF), D_MODEL ** -0.5),
        'w_ff2_up': normal((Ld, D_MODEL, D_FF), D_MODEL ** -0.5),
        'w_ff2_down': normal((Ld, D_FF, D_MODEL), D_FF ** -0.5),
        'g_ff2_post': gain(D_MODEL),
        'g_final': 1.0 + normal((D_MODEL,), 0.1),
    }

def reference(x, mem, g_ff1_pre, w_ff1_gate, w_ff1_up, w_ff1_down, g_ff1_post,
              g_mix_pre, w_mix_in, b_fox_f, w_gla_g2, b_gla_g, g_fox_out, g_gla_out,
              w_mix_out, g_mix_post, g_mem_pre, g_mem_src, w_mem_q, w_mem_kv, w_mem_o,
              g_mem_post, g_ff2_pre, w_ff2_gate, w_ff2_up, w_ff2_down, g_ff2_post, g_final):
    for l in range(DEPTH):
        y = swiglu(rms_norm(x, g_ff1_pre[l]), w_ff1_gate[l], w_ff1_up[l], w_ff1_down[l])
        x = x + 0.5 * rms_norm(y, g_ff1_post[l])
        y = hybrid_mixer(rms_norm(x, g_mix_pre[l]), w_mix_in[l], b_fox_f[l], w_gla_g2[l],
                         b_gla_g[l], g_fox_out[l], g_gla_out[l], w_mix_out[l])
        x = x + rms_norm(y, g_mix_post[l])
        y = memory_cross_attention(rms_norm(x, g_mem_pre[l]), rms_norm(mem, g_mem_src[l]),
                                   w_mem_q[l], w_mem_kv[l], w_mem_o[l])
        x = x + rms_norm(y, g_mem_post[l])
        y = swiglu(rms_norm(x, g_ff2_pre[l]), w_ff2_gate[l], w_ff2_up[l], w_ff2_down[l])
        x = x + 0.5 * rms_norm(y, g_ff2_post[l])
    return rms_norm(x, g_final)


_drawn_inputs = setup_inputs


def setup_inputs(seed=0):
    import zlib

    import numpy as np

    out = dict(_drawn_inputs(seed))
    spreads = {}
    factors = {'b_gla_g': 3.568}
    for name, (base, spread) in spreads.items():
        noise = np.random.default_rng([zlib.crc32(name.encode()), seed]).standard_normal(out[name].shape)
        drawn = base * np.exp(spread * noise) if base else spread * noise
        out[name] = __import__('jax').numpy.asarray(drawn.astype(out[name].dtype))
    for name, factor in factors.items():
        out[name] = (out[name] * factor).astype(out[name].dtype)
    return out
```

```python
import concourse.bass as bass
from concourse import mybir
from contextlib import ExitStack

F32 = mybir.dt.float32
F32R = mybir.dt.float32r
BF16 = mybir.dt.bfloat16
ALU = mybir.AluOpType
ACT = mybir.ActivationFunctionType
AX = mybir.AxisListType
ds = bass.ds

P = 128
D = 1024
T = 1024
HT = 512
KT = D // P
NT = T // P
D_FF = 2816
FC = D_FF // P
MEM = 256
EPS = 1e-6

FOX_H, FOX_D = 8, 64
OFF_FQ, OFF_FK, OFF_FV, OFF_FF = 0, 512, 1024, 1536
OFF_GQ = OFF_FF + FOX_H
OFF_GK = OFF_GQ + 256
OFF_GV = OFF_GK + 256
OFF_GG = OFF_GV + 512
RANK = 16
OFF_GR = OFF_GG + RANK
GLA_C = 64
NC = T // GLA_C
FOX_PAIRS, GLA_PAIRS, MEM_H = FOX_H // 2, 2, 4

N_G_MIX, N_U_MIX, M_MIX = FC, FC, FC
N_G_FOX, N_U_FOX = N_G_MIX + 1, N_U_MIX
N_G_GLA, N_U_GLA, M_GLA = N_G_FOX + FOX_PAIRS, N_U_FOX + 2 * FOX_PAIRS, M_MIX + FOX_PAIRS
N_G_MEM, N_U_MEM, M_MEM = N_G_GLA + 3 * GLA_PAIRS, N_U_GLA + 3 * GLA_PAIRS, M_GLA + 2 * GLA_PAIRS
N_G_FF2, N_U_FF2, M_FF2 = N_G_MEM + 12, N_U_MEM + 12, M_MEM + 8
G, U, A, B = range(4)
RING = 4


def build_layer(nc, x, mem, g_ff1_pre, w_ff1_gate, w_ff1_up, w_ff1_down, g_ff1_post,
                g_mix_pre, w_mix_in, b_fox_f, w_gla_g2, b_gla_g, g_fox_out, g_gla_out,
                w_mix_out, g_mix_post, g_mem_pre, g_mem_src, w_mem_q, w_mem_kv, w_mem_o,
                g_mem_post, g_ff2_pre, w_ff2_gate, w_ff2_up, w_ff2_down, g_ff2_post, g_final, out):
    ctx = ExitStack()
    with ctx:
        def sb(name, shape, dt=F32, where=None):
            return (where or ctx).enter_context(nc.sbuf_tensor(name, shape, dt))

        def sem(name):
            return ctx.enter_context(nc.semaphore(name))

        x_hi = sb("x_hi", [P, KT, T], F32R)
        x_lo = sb("x_lo", [P, KT, T], F32R)
        y = sb("y", [P, KT, T])
        raw = sb("raw", [P, 3, D])
        w_hi = sb("w_hi", [P, 3, D], F32R)
        w_lo = sb("w_lo", [P, 3, D], F32R)
        h_hi, h_lo = [sb("h_hi", [P, T], F32R)], [sb("h_lo", [P, T], F32R)]
        rs = sb("rs", [P, T])
        sq = sb("sq", [P, 2, HT])
        sq_sum = sb("sq_sum", [P, HT])
        x_new = sb("x_new", [P, 2, HT])
        diag = sb("diag", [P, HT])
        ident = sb("ident", [P, P])
        ones = sb("ones", [P, P])
        ident_r = sb("ident_r", [P, P], F32R)
        mean4 = sb("mean4", [P, 16])
        rms4 = sb("rms4", [P, 16])
        rms8 = sb("rms8", [P, NT])
        minus_half = sb("minus_half", [P, 16])
        inv_d = sb("inv_d", [P, 2])
        gains = sb("gains", [P, 11, KT])
        GAIN = {n: i for i, n in enumerate(
            ["ff1_pre", "ff1_post", "mix_pre", "mix_post", "mem_pre", "mem_post", "ff2_pre", "ff2_post",
             "final", "mem_src"])}
        head_gains = gains[:, 10, :].rearrange("p (a k) -> p a k", a=2)
        w_g2 = sb("w_g2", [32, 256])
        b_f = sb("b_f", [40, 1])
        ps = ctx.enter_context(nc.psum_tensor("ps", [P, 8, HT], F32))
        c_rows = nc.dram_tensor("c_rows", [2, FOX_H, T], F32, kind="Internal").ap()

        with ExitStack() as s:
            h_hi.append(sb("h_hi_ff", [P, T], F32R, where=s))
            h_lo.append(sb("h_lo_ff", [P, T], F32R, where=s))
            gate = sb("gate", [P, 2, HT], where=s)
            gate_act = sb("gate_act", [P, 2, HT], where=s)
            hidden = sb("hidden", [P, 2, HT], where=s)
            out_rows = sb("out_rows", [P, 2, D], where=s)
        with ExitStack() as s:
            gate_low = sb("gate_low", [32, T], where=s)
            tri_blk = sb("tri_blk", [P, P], where=s)
            tri_suf = sb("tri_suf", [P, P], where=s)
            ident_b = sb("ident_b", [P, P], BF16, where=s)
            neg_mask = sb("neg_mask", [P, P], BF16, where=s)
            with ExitStack() as f:
                q_head = [sb(f"q_head{i}", [66, T], where=f) for i in range(2)]
                k_head = [sb(f"k_head{i}", [66, T], where=f) for i in range(2)]
                v_rows = sb("v_rows", [P, NT, P], where=f)
                probs = sb("probs", [P, 2, T], where=f)
                v_t = probs[:, 0, :]
                probs_t = sb("probs_t", [P, 2, NT, P], where=f)
                o_rows = sb("o_rows", [P, NT, 2, FOX_D], where=f)
                row_sum = sb("row_sum", [P, NT, 2], where=f)
                row_inv = sb("row_inv", [P, NT, 2], where=f)
                neg_max = sb("neg_max", [P, NT, 2], where=f)
                o_sq = sb("o_sq", [P, NT, 2], where=f)
                o_junk = sb("o_junk", [P, FOX_D], where=f)
            with ExitStack() as f:
                tri_wide = sb("tri_wide", [P, T], where=f)
                forget = sb("forget", [40, T], where=f)
                forget_a = sb("forget_a", [40, T], where=f)
                lf_rows = sb("lf_rows", [P, NT, FOX_H], where=f)
                c_sb = sb("c_sb", [FOX_H, 2, T], where=f)
            with ExitStack() as f:
                la = sb("la", [P, NT, P], where=f)
                e_b = sb("e_b", [P, T], where=f)
                e_nb = sb("e_nb", [P, T], where=f)
                e_suf = sb("e_suf", [P, NT, P], where=f)
                q_dec = sb("q_dec", [P, T], where=f)
                k_inv = sb("k_inv", [P, T], where=f)
                k_dec = sb("k_dec", [P, NT, P], where=f)
                gv_rows = sb("gv_rows", [P, NT, P], where=f)
                states = sb("states", [P, NC, P], where=f)
                decay = sb("decay", [P, NC], where=f)
                gate_a = e_nb
                gv_t = e_nb
                o_gla = e_nb
                att_t = e_suf
                o_gla_sq = la
                r_act = e_b
        with ExitStack() as s:
            mem_k = sb("mem_k", [P, KT, MEM], where=s)
            mem_v = sb("mem_v", [P, 2, D], where=s)
            q_mem = sb("q_mem", [P, 2, T], where=s)
            mem_stat = sb("mem_stat", [P, 4], where=s)
            with ExitStack() as f:
                mem_rows = sb("mem_rows", [P, 2, D], where=f)
                memt_hi = sb("memt_hi", [P, KT, MEM], F32R, where=f)
                memt_lo = sb("memt_lo", [P, KT, MEM], F32R, where=f)
                mem_vt = x_new[:, :, 0:MEM]
            with ExitStack() as f:
                h_hi.append(sb("h_hi_mem", [P, T], F32R, where=f))
                h_lo.append(sb("h_lo_mem", [P, T], F32R, where=f))
                mem_vh = sb("mem_vh", [P, 2, MEM], where=f)
                mem_p = sb("mem_p", [P, 4, MEM], where=f)
                mem_pt = sb("mem_pt", [P, 2, HT], where=f)
                mem_max = sb("mem_max", [P, NT], where=f)
                mem_sum = sb("mem_sum", [P, NT], where=f)
                mem_inv = sb("mem_inv", [P, NT], where=f)

        const_ready = sem("const_ready")
        passed = sem("passed")
        gains_in = sem("gains_in")
        gains_t = sem("gains_t")
        x_in = [sem("x_in_0"), sem("x_in_1")]
        raw_in = [sem(f"raw_in_{s}") for s in "guab"]
        small_in = sem("small_in")
        small_zero = sem("small_zero")
        w_scaled = [sem(f"w_scaled_{s}") for s in "gu"]
        w_hi_done = [sem(f"w_hi_done_{s}") for s in "guab"]
        w_ready = [sem(f"w_ready_{s}") for s in "guab"]
        gemm_done = [sem("gemm_done_g"), sem("gemm_done_u")]
        gemm_read = [sem("gemm_read_g"), sem("gemm_read_u")]
        down_done = sem("down_done")
        down_read = sem("down_read")
        silu_done = sem("silu_done")
        gate_scaled = sem("gate_scaled")
        h_hi_done = sem("h_hi_done")
        h_ready = sem("h_ready")
        y_zero = sem("y_zero")
        sq_done, sq_added = sem("sq_done"), sem("sq_added")
        stat_done, mean_done = sem("stat_done"), sem("mean_done")
        pow_done, diag_done, spread_done = sem("pow_done"), sem("diag_done"), sem("spread_done")
        x_old = sem("x_old")
        x_new_done, x_hi_done, x_ready = sem("x_new_done"), sem("x_hi_done"), sem("x_ready")
        rs_ready = sem("rs_ready")
        out_t = sem("out_t")
        out_sent = [sem("out_sent_even"), sem("out_sent_odd")]
        out_read = [sem("out_read_act"), sem("out_read_dve")]
        ff_step = sem("ff_step")
        c_sent = sem("c_sent")
        c_in = sem("c_in")
        head_ones = sem("head_ones")
        v_t_done, v_rows_done = sem("v_t_done"), sem("v_rows_done")
        score_done, max_done, exp_done = sem("score_done"), sem("max_done"), sem("exp_done")
        pt_lo, pt_hi, pt_lo_read, pt_hi_read = sem("pt_lo"), sem("pt_hi"), sem("pt_lo_read"), sem("pt_hi_read")
        o_done, o_read, o_sq_done = sem("o_done"), sem("o_read"), sem("o_sq_done")
        o_mean, o_pow, o_norm, o_t = sem("o_mean"), sem("o_pow"), sem("o_norm"), sem("o_t")
        g_step = {n: sem("gla_" + n) for n in (
            "consts", "gate", "logsig", "la", "b", "suf", "eb", "esuf", "decay", "kt", "kdec", "kinv",
            "vt", "vrows", "att", "att_read", "att_mask", "kv", "state", "o", "o_copy", "osq", "stat",
            "mean", "pow", "diag", "spread", "silu", "onorm", "h", "qdec", "logdone", "zero")}
        m_step = {n: sem("mem_" + n) for n in (
            "in", "sq", "mean", "pow", "norm", "t", "hi", "ready", "vt", "vrows", "vh",
            "score", "max", "exp", "scaled", "pt", "pt_read", "o")}

        GEMM_BANK = {G: 0, U: 2}

        def wait(eng, semaphore, value):
            if not (isinstance(value, int) and value <= 0):
                eng.wait_ge(semaphore, value)

        def plain(eng):
            eng.sem_inc(passed, 1)

        def raw_tile(slot):
            return raw[:, slot, :] if slot < 2 else raw[:, 2, (slot - A) * HT:(slot - A + 1) * HT]

        def hi_tile(slot):
            return w_hi[:, slot, :] if slot < 2 else w_hi[:, 2, (slot - A) * HT:(slot - A + 1) * HT]

        def lo_tile(slot):
            return w_lo[:, slot, :] if slot < 2 else w_lo[:, 2, (slot - A) * HT:(slot - A + 1) * HT]

        def f32(ap):
            return ap.bitcast(F32)

        def half(t):
            return slice(t * HT, (t + 1) * HT)

        def stat_event(stage, kind, t):
            return t if stage == 0 else 2 + 4 * (stage - 1) + 2 * kind + t

        def stat_bank(kind, t):
            return 7 if kind == 0 else 6 + t

        def kv_psum(rows, n):
            c = n // 2 % 4
            return ps[rows, (2 if n < 8 else 0) + n % 2, c * P:(c + 1) * P]

        def sq_event(stage, kind, i):
            return i if stage == 0 else 16 + 32 * (stage - 1) + 16 * kind + i

        FF = {1: dict(nG=0, nU=0, m=0, s=0, pre="ff1_pre", gate=w_ff1_gate, up=w_ff1_up, down=w_ff1_down),
              2: dict(nG=N_G_FF2, nU=N_U_FF2, m=M_FF2, s=2 * FC, pre="ff2_pre",
                      gate=w_ff2_gate, up=w_ff2_up, down=w_ff2_down)}
        POST = {1: "ff1_post", 2: "mix_post", 3: "mem_post", 4: "ff2_post"}
        LAST_M = {1: FC - 1, 2: M_MEM - 1, 3: M_FF2 - 1, 4: M_FF2 + FC - 1}

        def cols(w, c0):
            return w[0].rearrange("(k p) n -> p k n", p=P)[:, :, c0]

        def slot3(ap):
            return ap.rearrange("p (k c) -> p k c", c=P)

        block = ctx.enter_context(nc.Block())

        @block.sync
        def _(sp):
            def load(slot, n, src):
                wait(sp, w_ready[slot], n)
                dst = raw_tile(slot) if slot >= A else slot3(raw_tile(slot))
                sp.dma_start(dst, src).then_inc(raw_in[slot], 16)

            def load_down(slot, m, w, row0):
                load(slot, m, w[0][ds(row0, P), (slot - A) * HT:(slot - A + 1) * HT])

            for j in range(NT):
                sp.dma_start(y[:, j, :], x[0][j * P:(j + 1) * P, :]).then_inc(x_in[j // 4], 16)
                if j == 3:
                    load(G, 0, cols(w_ff1_gate, ds(0, P)))
                    load(U, 0, cols(w_ff1_up, ds(0, P)))

            def ff(which, tail):
                f = FF[which]

                def chunk(c, after_g):
                    if not (isinstance(c, int) and c == FC - 1):
                        load(U, f["nU"] + c + 1, cols(f["up"], ds((c + 1) * P, P)))
                    load_down(B, f["m"] + c, f["down"], c * P)
                    if after_g:
                        load(G, f["nG"] + c + 2, cols(f["gate"], ds((c + 2) * P, P)))
                    if not (isinstance(c, int) and c == FC - 1):
                        load_down(A, f["m"] + c + 1, f["down"], (c + 1) * P)

                load_down(A, f["m"], f["down"], 0)
                load(G, f["nG"] + 1, cols(f["gate"], ds(P, P)))
                chunk(0, True)
                with sp.Fori(0, (FC - 4) // 2) as i:
                    chunk(i * 2 + 1, True)
                    chunk(i * 2 + 2, True)
                chunk(FC - 3, True)
                chunk(FC - 2, False)
                chunk(FC - 1, False)

            ff(1, None)
            sp.dma_start(w_g2[0:RANK, :], w_gla_g2[0]).then_inc(small_in, 16)
            wait(sp, w_ready[G], N_G_MIX)
            sp.wait_ge(small_zero, 1)
            small = slot3(raw_tile(G))
            sp.dma_start(small[:, :, 0:RANK], cols(w_mix_in, slice(OFF_GG, OFF_GG + RANK))).then_inc(small_in, 16)
            sp.dma_start(small[:, :, 32:40], cols(w_mix_in, slice(OFF_FF, OFF_FF + FOX_H))).then_inc(raw_in[G], 16)
            sp.dma_start(w_g2[RANK:RANK + 1, :], b_gla_g).then_inc(small_in, 16)
            sp.dma_start(b_f[32:40, :], b_fox_f.rearrange("a h -> h a")).then_inc(small_in, 16)
            sp.wait_ge(ff_step, 11)
            sp.dma_start(c_rows.rearrange("a h t -> h a t"), c_sb[:, :, :]).then_inc(c_sent, 16)
            sp.wait_ge(c_sent, 16)
            sp.wait_ge(head_ones, 1)
            with sp.Fori(0, FOX_PAIRS) as p:
                load(U, 2 * p + N_U_FOX, cols(w_mix_in, ds(p * P + OFF_FQ, P)))
                load(G, p + N_G_FOX, cols(w_mix_in, ds(p * P + OFF_FK, P)))
                load(U, 2 * p + (N_U_FOX + 1), cols(w_mix_in, ds(p * P + OFF_FV, P)))
                sp.wait_ge(gemm_done[U], 4 * p + (2 * N_U_FOX + 2))
                for i in range(2):
                    sp.dma_start(q_head[i][64:65, :], c_rows[0, ds(2 * p + i, 1), :]).then_inc(c_in, 16)
                    sp.dma_start(k_head[i][65:66, :], c_rows[1, ds(2 * p + i, 1), :]).then_inc(c_in, 16)
                load_down(A, p + M_MIX, w_mix_out, p * P)
                load_down(B, p + M_MIX, w_mix_out, p * P)
            with sp.Fori(0, GLA_PAIRS) as g:
                load(G, 3 * g + N_G_GLA, cols(w_mix_in, ds(g * P + OFF_GQ, P)))
                load(U, 3 * g + N_U_GLA, cols(w_mix_in, ds(g * P + OFF_GK, P)))
                for i in range(2):
                    load(G, 3 * g + (N_G_GLA + 1 + i), cols(w_mix_in, ds(g * 2 * P + (i * P + OFF_GV), P)))
                    load(U, 3 * g + (N_U_GLA + 1 + i), cols(w_mix_in, ds(g * 2 * P + (i * P + OFF_GR), P)))
                    for s in (A, B):
                        load_down(s, 2 * g + (M_GLA + i), w_mix_out, g * 2 * P + (i * P + 512))

            load(G, N_G_MEM, cols(w_mem_q, slice(0, P)))
            load(U, N_U_MEM, cols(w_mem_q, slice(P, 2 * P)))
            sp.wait_ge(down_read, 16 * (M_MEM - 1) + (RING + 1))
            sp.dma_start(mem_rows[:, :, :], mem[0].rearrange("(j p) d -> p j d", p=P)).then_inc(m_step["in"], 16)
            with sp.Fori(0, 8) as i:
                load(G, i + (N_G_MEM + 1), cols(w_mem_kv, ds(i * 2 * P, P)))
                load(U, i + (N_U_MEM + 1), cols(w_mem_kv, ds(i * 2 * P + P, P)))

            load(G, N_G_MEM + 9, cols(w_mem_q, slice(2 * P, 3 * P)))
            load(U, N_U_MEM + 9, cols(w_mem_q, slice(3 * P, 4 * P)))

            def mem_head(h, next_g, next_u):
                for i in range(2):
                    for s in (A, B):
                        load_down(s, 2 * h + (M_MEM + i), w_mem_o, h * 2 * P + i * P)
                    if i == 0 and next_g is not None:
                        load(G, h + (N_G_MEM + 10), next_g)
                        load(U, h + (N_U_MEM + 10), next_u)

            with sp.Fori(0, MEM_H - 2) as h:
                mem_head(h, cols(w_mem_q, ds(h * 2 * P + 4 * P, P)), cols(w_mem_q, ds(h * 2 * P + 5 * P, P)))
            mem_head(MEM_H - 2, cols(w_ff2_gate, ds(0, P)), cols(w_ff2_up, ds(0, P)))
            mem_head(MEM_H - 1, None, None)

            ff(2, None)

            for j in range(NT):
                for r in out_read:
                    sp.wait_ge(r, j + 1)
                sp.dma_start(out[0][j * P:(j + 1) * P, :], out_rows[:, j % 2, :]).then_inc(out_sent[j % 2], 16)
            for done in out_sent:
                sp.wait_ge(done, 16 * NT // 2)

        @block.gpsimd
        def _(pool):
            gp = nc.gpsimd

            def scale(slot, n, gain):
                pool.wait_ge(raw_in[slot], 16 * n + 16)
                w = slot3(raw_tile(slot))
                gp.tensor_tensor(w, w, gains[:, GAIN[gain], :].unsqueeze(2).to_broadcast([P, KT, P]),
                                 ALU.mult).then_inc(w_scaled[slot], 1)

            def add_squares(stage, kind, t):
                wait(pool, stat_done, stat_event(stage, kind, t))
                for d in range(KT):
                    e = sq_event(stage, kind, t * KT + d)
                    pool.wait_ge(sq_done, e + 1)
                    if d == 0:
                        gp.tensor_copy(sq_sum[:, :], sq[:, e % 2, :]).then_inc(sq_added, 1)
                    else:
                        pool.wait_ge(sq_added, e)
                        gp.tensor_tensor(sq_sum[:, :], sq_sum[:, :], sq[:, e % 2, :], ALU.add).then_inc(sq_added, 1)

            def inverse_root(stage, kind, t):
                e = stat_event(stage, kind, t)
                pool.wait_ge(mean_done, e + 1)
                dst = rms8[:, 4 * t:4 * t + 4] if (stage, kind) == (4, 1) else rms4[:, 0:4]
                gp.tensor_tensor(dst, mean4[:, 0:4], minus_half[:, 0:4], ALU.pow).then_inc(pow_done, 1)

            def zero_y(stage):
                pool.wait_ge(x_new_done, 16 * stage + 16)
                for d in range(KT):
                    gp.memset(y[:, d, :], 0.0).then_inc(y_zero, 1)

            def norms(stage, first_scale=None):
                if stage > 0:
                    for t in range(2):
                        add_squares(stage, 0, t)
                        inverse_root(stage, 0, t)
                for t in range(2):
                    add_squares(stage, 1, t)
                    inverse_root(stage, 1, t)

            gp.memset(ident[:, :], 0.0)
            gp.memset(ones[:, :], 1.0)
            gp.memset(minus_half[:, :], -0.5)
            gp.memset(inv_d[:, 0:1], 1.0 / D)
            gp.memset(inv_d[:, 1:2], 1.0 / P)
            pool.drain()
            gp.affine_select(out=ident[:, :], in_=ident[:, :], compare_op=ALU.not_equal, fill=1.0, base=0,
                             pattern=[[-1, P]], channel_multiplier=1)
            pool.drain().then_inc(const_ready, 1)

            def ff(which):
                f = FF[which]

                def chunk(c, nxt_u, nxt_g):
                    if nxt_g:
                        scale(G, f["nG"] + c + 1, f["pre"])
                    for t in range(2):
                        pool.wait_ge(silu_done, f["s"] + 2 * c + (t + 1))
                        gp.tensor_tensor(gate_act[:, t, :], gate_act[:, t, :], rs[:, half(t)],
                                         ALU.mult).then_inc(gate_scaled, 1)
                    if nxt_u:
                        scale(U, f["nU"] + c + 1, f["pre"])

                chunk(0, True, True)
                with pool.Fori(0, (FC - 2) // 2) as i:
                    chunk(i * 2 + 1, True, True)
                    chunk(i * 2 + 2, True, True)
                chunk(FC - 1, False, False)

            pool.wait_ge(const_ready, 2)
            scale(G, 0, "ff1_pre")
            scale(U, 0, "ff1_pre")
            norms(0)
            zero_y(0)
            ff(1)

            pool.wait_ge(w_ready[G], N_G_MIX)
            gp.memset(raw_tile(G), 0.0).then_inc(small_zero, 1)
            pool.wait_ge(small_in, 16 * 4)
            scale(G, N_G_MIX, "mix_pre")
            norms(1)
            gp.memset(gate_low[:, :], 1.0).then_inc(g_step["consts"], 1)
            gp.memset(tri_wide[:, :], 1.0)
            gp.memset(tri_blk[:, :], 1.0 / 16)
            gp.memset(tri_suf[:, :], 1.0 / 16)
            gp.memset(ident_b[:, :], 0.0)
            gp.memset(neg_mask[:, :], 0.0)
            pool.drain()
            gp.affine_select(out=tri_wide[:, 0:P], in_=tri_wide[:, 0:P], compare_op=ALU.is_ge, fill=0.0, base=0,
                             pattern=[[1, P]], channel_multiplier=-1)
            gp.affine_select(out=tri_blk[:, :], in_=tri_blk[:, :], compare_op=ALU.is_ge, fill=0.0, base=0,
                             pattern=[[1, P]], channel_multiplier=-1)
            gp.affine_select(out=tri_suf[:, :], in_=tri_suf[:, :], compare_op=ALU.is_gt, fill=0.0, base=0,
                             pattern=[[-1, P]], channel_multiplier=1)
            gp.affine_select(out=ident_b[:, :], in_=ident_b[:, :], compare_op=ALU.not_equal, fill=1.0, base=0,
                             pattern=[[-1, P]], channel_multiplier=1)
            gp.affine_select(out=neg_mask[:, :], in_=neg_mask[:, :], compare_op=ALU.is_ge, fill=-1e30, base=0,
                             pattern=[[-1, P]], channel_multiplier=1)
            pool.drain()
            gp.memset(tri_blk[0:GLA_C, GLA_C:P], 0.0)
            gp.memset(tri_suf[GLA_C:P, 0:GLA_C], 0.0)
            pool.drain().then_inc(g_step["consts"], 1)
            zero_y(1)
            pool.wait_ge(c_sent, 16)
            pool.drain()
            for i in range(2):
                gp.memset(q_head[i][64:66, :], 1.0)
                gp.memset(k_head[i][64:66, :], 1.0)
            pool.drain().then_inc(head_ones, 1)
            with pool.Fori(0, FOX_PAIRS) as p:
                scale(U, 2 * p + N_U_FOX, "mix_pre")
                scale(G, p + N_G_FOX, "mix_pre")
                scale(U, 2 * p + (N_U_FOX + 1), "mix_pre")
                pool.wait_ge(o_mean, p + 1)
                gp.tensor_tensor(rms4[:, :], mean4[:, :], minus_half[:, :], ALU.pow).then_inc(o_pow, 1)
            with pool.Fori(0, GLA_PAIRS) as g:
                scale(G, 3 * g + N_G_GLA, "mix_pre")
                scale(U, 3 * g + N_U_GLA, "mix_pre")
                pool.wait_ge(g_step["kdec"], 2 * g + 2)
                plain(pool)
                gp.memset(att_t[:, :, :], 0.0).then_inc(g_step["zero"], 1)
                for i in range(2):
                    scale(G, 3 * g + (N_G_GLA + 1 + i), "mix_pre")
                    scale(U, 3 * g + (N_U_GLA + 1 + i), "mix_pre")
                    pool.wait_ge(g_step["att_read"], 8 * g + (4 * i + 4))
                    plain(pool)
                    for r in range(2):
                        pool.drain()
                        part = att_t[r * GLA_C:(r + 1) * GLA_C, :, r * GLA_C:(r + 1) * GLA_C]
                        gp.affine_select(out=part, in_=part, compare_op=ALU.is_ge, fill=0.0, base=0,
                                         pattern=[[0, NT], [1, GLA_C]],
                                         channel_multiplier=-1).then_inc(g_step["att_mask"], 1)
                    pool.drain()
                    for t in range(2):
                        pool.wait_ge(g_step["mean"], 4 * g + (2 * i + t + 1))
                        gp.tensor_tensor(rms4[:, 0:4], mean4[:, 0:4], minus_half[:, 0:4],
                                         ALU.pow).then_inc(g_step["pow"], 1)

            scale(G, N_G_MEM, "mem_pre")
            scale(U, N_U_MEM, "mem_pre")
            norms(2)
            scale(G, N_G_MEM + 1, "mem_src")
            scale(U, N_U_MEM + 1, "mem_src")
            zero_y(2)
            pool.wait_ge(m_step["mean"], 1)
            gp.tensor_tensor(mem_stat[:, 2:4], mem_stat[:, 0:2], minus_half[:, 0:2], ALU.pow).then_inc(m_step["pow"], 1)
            with pool.Fori(1, 8) as i:
                scale(G, i + (N_G_MEM + 1), "mem_src")
                scale(U, i + (N_U_MEM + 1), "mem_src")

            def mem_head(h, more):
                if more:
                    scale(G, h + (N_G_MEM + 9), "mem_pre")
                    scale(U, h + (N_U_MEM + 9), "mem_pre")
                pool.wait_ge(m_step["vrows"], 16)
                wait(pool, m_step["o"], 4 * h)
                gp.tensor_copy(mem_vh[:, :, :], mem_v[:, :, ds(h * MEM, MEM)]).then_inc(m_step["vh"], 1)

            mem_head(0, True)
            with pool.Fori(1, MEM_H - 1) as h:
                mem_head(h, True)
            mem_head(MEM_H - 1, False)

            scale(G, N_G_FF2, "ff2_pre")
            scale(U, N_U_FF2, "ff2_pre")
            norms(3)
            zero_y(3)
            ff(2)
            norms(4)

        @block.scalar
        def _(act):
            sc = nc.scalar
            gain_rows = sq[:, 0, 0:P]
            for name, src in (("ff1_pre", g_ff1_pre), ("ff1_post", g_ff1_post), ("mix_pre", g_mix_pre),
                              ("mix_post", g_mix_post), ("mem_pre", g_mem_pre), ("mem_post", g_mem_post),
                              ("ff2_pre", g_ff2_pre), ("ff2_post", g_ff2_post), ("mem_src", g_mem_src),
                              ("final", g_final.unsqueeze(0))):
                r = GAIN[name] * KT
                act.dma_start(gain_rows[r:r + KT, :], src[0].rearrange("(k p) -> k p", p=P)).then_inc(gains_in, 16)
            for i, src in enumerate((g_fox_out, g_gla_out)):
                r = (10 + i // 2) * KT + 4 * i
                act.dma_start(gain_rows[r:r + 4, :], src[0].rearrange("(k p) -> k p", p=P)).then_inc(gains_in, 16)

            def free_of(slot, n, eng):
                if slot < A:
                    wait(eng, gemm_done[slot], 2 * n)
                else:
                    wait(eng, down_done, 16 * n)

            def split_hi(slot, n, early=False):
                if slot < A:
                    act.wait_ge(w_scaled[slot], n + 1)
                else:
                    act.wait_ge(raw_in[slot], 16 * n + 16)
                if early:
                    act.wait_ge(down_done, 16 * n - 8)
                else:
                    free_of(slot, n, act)
                sc.activation(hi_tile(slot), raw_tile(slot), ACT.Copy).then_inc(w_hi_done[slot], 1)

            def square(e, src):
                wait(act, sq_added, e - 1)
                sc.activation(sq[:, e % 2, :], src, ACT.Square).then_inc(sq_done, 1)

            def y_squares(stage):
                m = LAST_M[stage]
                for i in range(16):
                    act.wait_ge(down_read, 16 * m + i + 1 + RING)
                    square(sq_event(stage, 0, i), y[:, i % 8, half(i // 8)])

            def new_x(stage, i):
                act.wait_ge(x_new_done, 16 * stage + i + 1)
                t, d = divmod(i, 8)
                if stage < 4:
                    sc.activation(x_hi[:, d, half(t)], x_new[:, i % 2, :], ACT.Copy).then_inc(x_hi_done, 1)
                else:
                    sc.activation(y[:, d, half(t)], x_new[:, i % 2, :], ACT.Copy,
                                  scale=gains[:, GAIN["final"], d:d + 1]).then_inc(x_hi_done, 1)
                square(sq_event(stage, 1, i), x_new[:, i % 2, :])

            def keep_rs(stage, t):
                act.wait_ge(spread_done, stat_event(stage, 1, t) + 1)
                sc.activation(rs[:, half(t)], ps[:, 6 + t, :], ACT.Copy).then_inc(rs_ready, 1)

            def norms(stage):
                if stage > 0:
                    y_squares(stage)
                for i in range(16):
                    new_x(stage, i)
                    if i == 11 and stage < 4:
                        keep_rs(stage, 0)
                if stage < 4:
                    keep_rs(stage, 1)

            def ff(which):
                f = FF[which]

                def chunk(c, parity, first=False, last=False):
                    nG, nU, m = f["nG"] + c, f["nU"] + c, f["m"] + c
                    if not first:
                        split_hi(U, nU)
                    for t in range(2):
                        act.wait_ge(gemm_read[G], 2 * nG + (t + 1))
                        if not first:
                            act.wait_ge(gemm_read[U], 2 * nU + (t - 1))
                        sc.activation(gate_act[:, t, :], gate[:, t, :], ACT.Silu).then_inc(silu_done, 1)
                        if t == 0 and not first:
                            split_hi(B, m - 1)
                    if not last:
                        split_hi(G, nG + 1)
                    split_hi(A, m, early=not first)
                    for t in range(2):
                        act.wait_ge(gemm_read[U], 2 * nU + (t + 1))
                        sc.activation(h_hi[parity][:, half(t)], hidden[:, t, :], ACT.Copy).then_inc(h_hi_done, 1)

                chunk(0, 0, first=True)
                with act.Fori(0, (FC - 2) // 2) as i:
                    chunk(i * 2 + 1, 1)
                    chunk(i * 2 + 2, 0)
                chunk(FC - 1, 1, last=True)
                split_hi(B, f["m"] + FC - 1)

            split_hi(G, 0)
            split_hi(U, 0)
            norms(0)
            ff(1)
            split_hi(G, N_G_MIX)
            norms(1)
            row = slice(32, 40)
            act.wait_ge(ff_step, 2)
            sc.activation(forget_a[row, :], forget[row, :], ACT.Abs).then_inc(ff_step, 1)
            act.wait_ge(ff_step, 3)
            sc.activation(forget_a[row, :], forget_a[row, :], ACT.Exp, scale=-1.0).then_inc(ff_step, 1)
            act.wait_ge(ff_step, 4)
            sc.activation(forget_a[row, :], forget_a[row, :], ACT.Ln, bias=1.0).then_inc(ff_step, 1)

            def attend_fox(p):
                for i in range(2):
                    act.wait_ge(v_t_done, 2 * p + (i + 1))
                    sc.activation(v_rows[:, 4 * i:4 * i + 4, :].rearrange("p a b -> p (a b)"), ps[:, 4 + i, :],
                                  ACT.Copy).then_inc(v_rows_done, 1)
                for a in range(19):
                    hh, b = divmod(a, 8)
                    if a < 16:
                        act.wait_ge(max_done, 16 * p + (a + 1))
                        if a >= 2:
                            act.wait_ge(pt_lo, 16 * p + (a - 1))
                        if a >= 6 and (a - 2) % 8 >= 4:
                            act.wait_ge(pt_hi, 8 * p + 4 * ((a - 2) // 8) + ((a - 2) % 8 - 3))
                        L = (b + 1) * P
                        bank = 2 * (a % 2)
                        sc.activation(probs[:, a % 2, 0:L],
                                      ps[:, bank:bank + 2, :].rearrange("p a b -> p (a b)")[:, 0:L], ACT.Exp,
                                      bias=neg_max[:, b, hh:hh + 1], scale=1.0,
                                      accum_out=row_sum[:, b, hh:hh + 1]).then_inc(exp_done, 1)
                    if 1 <= a <= 16 and (a - 1) % 8 >= 4:
                        h1, b1 = divmod(a - 1, 8)
                        act.wait_ge(pt_hi, 8 * p + (4 * h1 + b1 - 3))
                        if a - 1 >= 2:
                            act.wait_ge(o_done, 16 * p + (a - 2))
                        sc.activation(probs_t[:, (a - 1) % 2, 4:b1 + 1, :].rearrange("p a b -> p (a b)"),
                                      ps[:, 5, 0:(b1 - 3) * P], ACT.Copy).then_inc(pt_hi_read, 1)
                    if a >= 3:
                        h3, b3 = divmod(a - 3, 8)
                        act.wait_ge(o_read, 16 * p + (a - 2))
                        if a > 3:
                            act.wait_ge(o_sq_done, 16 * p + (a - 3))
                        sc.activation(o_junk[:, :], o_rows[:, b3, h3, :], ACT.Square,
                                      accum_out=o_sq[:, b3, h3:h3 + 1]).then_inc(o_sq_done, 1)

            with act.Fori(0, FOX_PAIRS) as p:
                split_hi(U, 2 * p + N_U_FOX)
                split_hi(G, p + N_G_FOX)
                split_hi(U, 2 * p + (N_U_FOX + 1))
                attend_fox(p)
                split_hi(A, p + M_MIX)
                split_hi(B, p + M_MIX)
                for t in range(2):
                    act.wait_ge(o_t, 2 * p + (t + 1))
                    act.wait_ge(down_done, 16 * p + 16 * M_MIX)
                    plain(act)
                    sc.activation(h_hi[0][:, half(t)], ps[:, 4 + t, :], ACT.Copy,
                                  scale=head_gains[:, 0, ds(p, 1)]).then_inc(h_hi_done, 1)

            with act.Fori(0, GLA_PAIRS) as g:
                st = g_step
                split_hi(G, 3 * g + N_G_GLA)
                split_hi(U, 3 * g + N_U_GLA)
                for i in range(2):
                    la_h = gate_a[:, half(i)]
                    act.wait_ge(st["gate"], 2 * g + (i + 1))
                    sc.activation(la_h, ps[:, 4 + i, :], ACT.Abs).then_inc(st["logsig"], 1)
                    act.wait_ge(st["logsig"], 6 * g + (3 * i + 1))
                    sc.activation(la_h, la_h, ACT.Exp, scale=-1.0).then_inc(st["logsig"], 1)
                    act.wait_ge(st["logsig"], 6 * g + (3 * i + 2))
                    sc.activation(la_h, la_h, ACT.Ln, bias=1.0).then_inc(st["logsig"], 1)
                for i in range(2):
                    act.wait_ge(st["b"], 2 * g + (i + 1))
                    sc.activation(e_b[:, half(i)], ps[:, 4 + i, :], ACT.Exp).then_inc(st["eb"], 1)
                    sc.activation(e_nb[:, half(i)], ps[:, 4 + i, :], ACT.Exp, scale=-1.0).then_inc(st["eb"], 1)
                for i in range(2):
                    act.wait_ge(st["suf"], 2 * g + (i + 1))
                    sc.activation(e_suf[:, 4 * i:4 * i + 4, :].rearrange("p a b -> p (a b)"), ps[:, 6 + i, :],
                                  ACT.Exp).then_inc(st["esuf"], 1)
                for hd in range(2):
                    split_hi(G, 3 * g + (N_G_GLA + 1 + hd))
                    split_hi(U, 3 * g + (N_U_GLA + 1 + hd))
                    for i in range(2):
                        act.wait_ge(st["vt"], 4 * g + (2 * hd + i + 1))
                        sc.activation(gv_rows[:, 4 * i:4 * i + 4, :].rearrange("p a b -> p (a b)"), ps[:, 4 + i, :],
                                      ACT.Copy).then_inc(st["vrows"], 1)
                    for t in range(2):
                        act.wait_ge(gemm_read[U], 6 * g + (2 * N_U_GLA + 2 + 2 * hd + t + 1))
                        sc.activation(r_act[:, half(t)], r_act[:, half(t)], ACT.Silu).then_inc(st["silu"], 1)
                    for t in range(2):
                        act.wait_ge(st["o"], 4 * g + (2 * hd + t + 1))
                        sc.activation(o_gla[:, half(t)], ps[:, 4 + t, :], ACT.Copy).then_inc(st["o_copy"], 1)
                        sc.activation(o_gla_sq[:, 4 * t:4 * t + 4, :].rearrange("p a b -> p (a b)"), ps[:, 4 + t, :],
                                      ACT.Square).then_inc(st["osq"], 1)
                    split_hi(A, 2 * g + (M_GLA + hd))
                    split_hi(B, 2 * g + (M_GLA + hd))
                    for t in range(2):
                        act.wait_ge(st["h"], 4 * g + (2 * hd + t + 1))
                        sc.activation(h_hi[0][:, half(t)], x_new[:, t, :], ACT.Copy).then_inc(h_hi_done, 1)

            split_hi(G, N_G_MEM)
            split_hi(U, N_U_MEM)
            norms(2)
            for s, nn in ((G, N_G_MEM), (U, N_U_MEM)):
                split_hi(s, nn + 1)
            ms = m_step
            act.wait_ge(ms["in"], 16)
            for j in range(2):
                act.wait_ge(x_ready, 16 * 3) if j == 0 else act.wait_ge(ms["sq"], 1)
                sc.activation(x_new[:, :, :].rearrange("p a b -> p (a b)"), mem_rows[:, j, :], ACT.Square,
                              accum_out=mem_stat[:, j:j + 1]).then_inc(ms["sq"], 1)
            for k in range(KT // 2):
                act.wait_ge(ms["t"], k + 1)
                sc.activation(memt_hi[:, 2 * k:2 * k + 2, :].rearrange("p a b -> p (a b)"), ps[:, 4 + k % 2, :],
                              ACT.Copy).then_inc(ms["hi"], 1)
            with act.Fori(0, 4) as i:
                for s, nn in ((G, N_G_MEM), (U, N_U_MEM)):
                    act.wait_ge(gemm_done[s], 2 * i + (2 * nn + 4))
                    plain(act)
                    for r in range(2):
                        sc.activation(mem_k[:, ds(2 * i + s, 1), r * P:(r + 1) * P], ps[:, GEMM_BANK[s], r * P:(r + 1) * P],
                                      ACT.Copy, scale=1.0 / 16).then_inc(gemm_read[s], 1)
                    split_hi(s, i + (nn + 2))
            with act.Fori(0, 4) as i:
                for s, nn in ((G, N_G_MEM), (U, N_U_MEM)):
                    split_hi(s, i + (nn + 6))
                for s, nn in ((G, N_G_MEM), (U, N_U_MEM)):
                    act.wait_ge(ms["vt"], 2 * i + (s + 1))
                    plain(act)
                    for r in range(2):
                        sc.activation(mem_v[:, r, ds(i * 2 * P + s * P, P)], ps[:, 4 + s, r * P:(r + 1) * P],
                                      ACT.Copy).then_inc(ms["vrows"], 1)

            def mem_head(h, more):
                for j in range(NT):
                    act.wait_ge(ms["max"], 8 * h + (j + 1))
                    if j >= 4:
                        act.wait_ge(ms["pt"], 2 * h + 1)
                    sc.activation(mem_p[:, j % 4, :], ps[:, j % 4, 0:MEM], ACT.Exp, bias=mem_max[:, j:j + 1],
                                  scale=1.0, accum_out=mem_sum[:, j:j + 1]).then_inc(ms["exp"], 1)
                    if j % 4 == 3:
                        t = j // 4
                        act.wait_ge(ms["pt"], 2 * h + (t + 1))
                        if t:
                            act.wait_ge(ms["o"], 4 * h + 2)
                        for blk in range(2):
                            sc.activation(mem_pt[:, blk, :], ps[:, 4 + blk, :], ACT.Copy).then_inc(ms["pt_read"], 1)
                        for c in range(2):
                            act.wait_ge(ms["o"], 4 * h + (2 * t + c + 1))
                            act.wait_ge(down_done, 32 * h + 16 * M_MEM)
                            sc.activation(h_hi[2 * c][:, half(t)], ps[:, 6 + c, :], ACT.Copy).then_inc(h_hi_done, 1)
                if more:
                    split_hi(G, h + (N_G_MEM + 10))
                    split_hi(U, h + (N_U_MEM + 10))
                for c in range(2):
                    split_hi(A, 2 * h + (M_MEM + c))
                    split_hi(B, 2 * h + (M_MEM + c))

            with act.Fori(0, MEM_H - 1) as h:
                mem_head(h, True)
            mem_head(MEM_H - 1, False)

            norms(3)
            ff(2)
            norms(4)
            act.wait_ge(pow_done, 18)
            for j in range(NT):
                act.wait_ge(out_t, 2 * j + 1)
                if j >= 2:
                    act.wait_ge(out_sent[j % 2], 16 * (j // 2))
                sc.activation(out_rows[:, j % 2, 0:HT], ps[:, 2 * (j % 2), :], ACT.Copy,
                              scale=rms8[:, j:j + 1]).then_inc(out_read[0], 1)

        @block.tensor
        def _(pe):
            mm = nc.tensor.matmul

            def product(acc, w, v, first, last):
                mm(acc, w[0], v[0], start=first, stop=False)
                mm(acc, w[0], v[1], start=False, stop=False)
                return mm(acc, w[1], v[0], start=False, stop=last)

            def x_tile(k, t):
                return x_hi[:, k, half(t)], x_lo[:, k, half(t)]

            def w_tile(slot, k):
                return tuple(w[:, slot, k * P:(k + 1) * P] for w in (w_hi, w_lo))

            def gemm(slot, n, t):
                if t == 0:
                    pe.wait_ge(w_ready[slot], n + 1)
                wait(pe, gemm_read[slot], 2 * n + (t - 1))
                for k in range(KT):
                    last = product(ps[:, GEMM_BANK[slot] + t, :], w_tile(slot, k), x_tile(k, t), k == 0, k == KT - 1)
                last.then_inc(gemm_done[slot], 1)

            def down_group(m, h_slot, d, t, k):
                pe.wait_ge(w_ready[A if d < 4 else B], m + 1)
                pe.wait_ge(h_ready, 2 * m + (t + 1))
                pe.wait_ge(down_read, 16 * m + (k + 1))
                w = w_hi[:, 2, d * P:(d + 1) * P], w_lo[:, 2, d * P:(d + 1) * P]
                v = h_hi[h_slot][:, half(t)], h_lo[h_slot][:, half(t)]
                product(ps[:, 4 + k % 4, :], w, v, True, True).then_inc(down_done, 1)

            def down_all(m, h_slot, by_half):
                for k in range(16):
                    d, t = (k % 8, k // 8) if by_half else (k // 2, k % 2)
                    down_group(m, h_slot, d, t, k)

            def statistics(stage, kind, t):
                pe.wait_ge(sq_added, sq_event(stage, kind, 8 * t + 7) + 1)
                for j in range(4):
                    last = mm(ps[:, stat_bank(kind, t), j:j + 1], sq_sum[:, j * P:(j + 1) * P], inv_d[:, 0:1],
                              start=True, stop=True)
                last.then_inc(stat_done, 1)

            def spread(stage, kind, t):
                pe.wait_ge(diag_done, stat_event(stage, kind, t) + 1)
                mm(ps[:, 6 + t, :], ones[:, :], diag[:, :], start=True, stop=True).then_inc(spread_done, 1)

            def old_x(stage, i):
                t, d = divmod(i, 8)
                if i >= 2:
                    pe.wait_ge(x_new_done, 16 * stage + i - 1)
                bank = ps[:, 4 + i % 2, :]
                if stage == 0:
                    if d == 0:
                        pe.wait_ge(x_in[t], 16 * 4)
                    for j in range(4):
                        last = nc.tensor.transpose(bank[:, j * P:(j + 1) * P], y[:, 4 * t + j, d * P:(d + 1) * P], ident[:, :])
                    last.then_inc(x_old, 1)
                else:
                    mm(bank, ident_r[:, :], x_hi[:, d, half(t)], start=True, stop=False)
                    mm(bank, ident_r[:, :], x_lo[:, d, half(t)], start=False, stop=True).then_inc(x_old, 1)

            def norms(stage, first):
                if stage > 0:
                    pe.wait_ge(down_read, 16 * (LAST_M[stage] + 1) + RING)
                    statistics(stage, 0, 0)
                    spread(stage, 0, 0)
                for i in range(2):
                    old_x(stage, i)
                if stage > 0:
                    statistics(stage, 0, 1)
                for i in range(16):
                    if i + 2 < 16:
                        old_x(stage, i + 2)
                    t, k = divmod(i, 8)
                    if first:
                        pe.wait_ge(x_ready, 16 * stage + i + 1)
                    for slot, n in first:
                        if i == 0:
                            pe.wait_ge(w_ready[slot], n + 1)
                        if k == 0:
                            wait(pe, gemm_read[slot], 2 * n + (t - 1))
                        last = product(ps[:, GEMM_BANK[slot] + t, :], w_tile(slot, k), x_tile(k, t),
                                       k == 0, k == KT - 1)
                        if k == KT - 1:
                            last.then_inc(gemm_done[slot], 1)
                    if stage > 0 and i == 2:
                        spread(stage, 0, 1)
                    if i == 8:
                        statistics(stage, 1, 0)
                    if i == 10 and stage < 4:
                        spread(stage, 1, 0)
                statistics(stage, 1, 1)
                if stage < 4:
                    spread(stage, 1, 1)

            def ff(which):
                f = FF[which]

                def chunk(c, parity):
                    m = f["m"] + c - 1
                    for q in range(4):
                        slot, t = (G, U)[q // 2], q % 2
                        gemm(slot, (f["nG"] if slot == G else f["nU"]) + c, t)
                        for k in range(4 * q, 4 * q + 4):
                            down_group(m, 1 - parity, k // 2, k % 2, k)

                with pe.Fori(0, (FC - 2) // 2) as i:
                    chunk(i * 2 + 1, 1)
                    chunk(i * 2 + 2, 0)
                chunk(FC - 1, 1)
                down_all(f["m"] + FC - 1, 1, True)

            pe.wait_ge(const_ready, 1)
            pe.wait_ge(gains_in, 16 * 12)
            nc.tensor.transpose(ps[:, 6, 0:11 * KT], sq[0:11 * KT, 0, 0:P], ident[0:11 * KT, 0:11 * KT]).then_inc(gains_t, 1)
            pe.wait_ge(const_ready, 2)
            norms(0, [(G, 0), (U, 0)])
            ff(1)
            norms(1, [(G, N_G_MIX)])

            pe.wait_ge(ff_step, 6)
            for j in range(NT):
                last = nc.tensor.transpose(ps[:, 4, j * FOX_H:(j + 1) * FOX_H], forget_a[32:40, j * P:(j + 1) * P],
                                           ident[32:40, 32:40])
            last.then_inc(ff_step, 1)
            pe.wait_ge(ff_step, 8)
            pe.wait_ge(g_step["consts"], 2)
            for t in range(2):
                for j in range(4 * t + 4):
                    first_col = max(j * P - t * HT, 0)
                    skip = max(t * HT - j * P, 0)
                    last = mm(ps[0:FOX_H, 2 + t, first_col:HT], lf_rows[:, j, :],
                              tri_wide[:, skip:skip + HT - first_col], start=j == 0, stop=j == 4 * t + 3)
            last.then_inc(ff_step, 1)
            pe.wait_ge(ff_step, 11)

            def scores(p, a):
                hh, b = divmod(a, 8)
                if a >= 2:
                    pe.wait_ge(exp_done, 16 * p + (a - 1))
                width = (b + 1) * P
                q = q_head[hh][0:66, b * P:(b + 1) * P]
                for t in range((width + HT - 1) // HT):
                    w = min(HT, width - t * HT)
                    diagonal = (t + 1) * HT >= width
                    mm(ps[:, 2 * (a % 2) + t, 0:w], q, k_head[hh][0:66, t * HT:t * HT + w], start=True, stop=not diagonal)
                    if diagonal:
                        mm(ps[:, 2 * (a % 2) + t, w - P:w], ident_b[:, :], neg_mask[:, :], start=False,
                           stop=True).then_inc(score_done, 1)

            def transpose_probs(p, a):
                hh, b = divmod(a, 8)
                pe.wait_ge(exp_done, 16 * p + (a + 1))
                for i in range(b // 4 + 1):
                    if i == 0 and a > 0:
                        pe.wait_ge(pt_lo_read, 16 * p + a)
                    if i == 1 and (a > 4):
                        pe.wait_ge(pt_hi_read, 8 * p + (4 * hh + b - 4))
                    for j in range(4 * i, min(4 * i + 4, b + 1)):
                        last = nc.tensor.transpose(ps[:, 4 + i, (j % 4) * P:(j % 4 + 1) * P],
                                                   probs[:, a % 2, j * P:(j + 1) * P], ident[:, :])
                    last.then_inc(pt_hi if i else pt_lo, 1)

            def attend_values(p, a):
                hh, b = divmod(a, 8)
                pe.wait_ge(pt_lo_read, 16 * p + (a + 1))
                if b >= 4:
                    pe.wait_ge(pt_hi_read, 8 * p + (4 * hh + b - 3))
                if a >= 2:
                    pe.wait_ge(o_read, 16 * p + (a - 1))
                for j in range(b + 1):
                    last = mm(ps[:, 6 + a % 2, 0:FOX_D], probs_t[:, a % 2, j, :],
                              v_rows[:, j, hh * FOX_D:(hh + 1) * FOX_D], start=j == 0, stop=j == b)
                last.then_inc(o_done, 1)

            with pe.Fori(0, FOX_PAIRS) as p:
                for slot, n in ((U, 2 * p + N_U_FOX), (G, p + N_G_FOX), (U, 2 * p + (N_U_FOX + 1))):
                    for t in range(2):
                        gemm(slot, n, t)
                pe.wait_ge(gemm_read[U], 4 * p + (2 * N_U_FOX + 4))
                for i in range(2):
                    for j in range(4):
                        last = nc.tensor.transpose(ps[:, 4 + i, j * P:(j + 1) * P],
                                                   v_t[:, (4 * i + j) * P:(4 * i + j + 1) * P], ident[:, :])
                    last.then_inc(v_t_done, 1)
                pe.wait_ge(c_in, 64 * p + 64)
                pe.wait_ge(gemm_read[G], 2 * p + (2 * N_G_FOX + 2))
                for a in range(18):
                    if a < 16:
                        scores(p, a)
                    if a == 1:
                        pe.wait_ge(v_rows_done, 2 * p + 2)
                    if 1 <= a <= 16:
                        transpose_probs(p, a - 1)
                    if a >= 2:
                        attend_values(p, a - 2)
                pe.wait_ge(o_norm, p + 1)
                for i in range(2):
                    for j in range(4):
                        last = nc.tensor.transpose(ps[:, 4 + i, j * P:(j + 1) * P],
                                                   o_rows[:, 4 * i + j, :, :].rearrange("p a b -> p (a b)"), ident[:, :])
                    last.then_inc(o_t, 1)
                pe.wait_ge(h_ready, 2 * p + (2 * M_MIX + 2))
                down_all(p + M_MIX, 0, True)
                pe.wait_ge(down_read, 16 * p + (16 * (M_MIX + 1) + RING))

            st = g_step
            with pe.Fori(0, GLA_PAIRS) as g:
                for i in range(2):
                    for j in range(4):
                        last = mm(ps[:, 4 + i, j * P:(j + 1) * P], gate_low[0:RANK + 1, (4 * i + j) * P:(4 * i + j + 1) * P],
                                  w_g2[0:RANK + 1, ds(g * P, P)], start=True, stop=True)
                    last.then_inc(st["gate"], 1)
                for slot, n in ((G, 3 * g + N_G_GLA), (U, 3 * g + N_U_GLA)):
                    for t in range(2):
                        gemm(slot, n, t)
                pe.wait_ge(st["la"], 2 * g + 2)
                for i in range(2):
                    for j in range(4):
                        last = mm(ps[:, 4 + i, j * P:(j + 1) * P], la[:, 4 * i + j, :], tri_blk[:, :], start=True, stop=True)
                    last.then_inc(st["b"], 1)
                for i in range(2):
                    mm(ps[:, 6 + i, :], tri_suf[:, :], la[:, 4 * i:4 * i + 4, :].rearrange("p a b -> p (a b)"),
                       start=True, stop=True).then_inc(st["suf"], 1)
                pe.wait_ge(st["eb"], 4 * g + 4)
                pe.wait_ge(gemm_read[U], 6 * g + (2 * N_U_GLA + 2))
                for i in range(2):
                    for j in range(4):
                        last = nc.tensor.transpose(ps[:, 4 + i, j * P:(j + 1) * P],
                                                   k_inv[:, (4 * i + j) * P:(4 * i + j + 1) * P], ident[:, :])
                    last.then_inc(st["kt"], 1)
                for hd in range(2):
                    rows = slice(hd * GLA_C, (hd + 1) * GLA_C)
                    for slot, nn in ((G, N_G_GLA), (U, N_U_GLA)):
                        for t in range(2):
                            gemm(slot, 3 * g + (nn + 1 + hd), t)
                    pe.wait_ge(gemm_read[G], 6 * g + (2 * N_G_GLA + 2 * hd + 4))
                    pe.wait_ge(st["kdec"], 2 * g + 2)
                    for i in range(2):
                        for j in range(4):
                            last = nc.tensor.transpose(ps[:, 4 + i, j * P:(j + 1) * P],
                                                       gv_t[:, (4 * i + j) * P:(4 * i + j + 1) * P], ident[:, :])
                        last.then_inc(st["vt"], 1)
                    pe.wait_ge(st["qdec"], g + 1)
                    for i in range(2):
                        for j in range(4 * i, 4 * i + 4):
                            tile = slice(j * P, (j + 1) * P)
                            last = mm(ps[:, i, (j % 4) * P:(j % 4 + 1) * P], k_inv[rows, tile], q_dec[rows, tile],
                                      start=True, stop=True)
                        last.then_inc(st["att"], 1)
                    pe.wait_ge(st["vrows"], 4 * g + (2 * hd + 2))
                    pe.wait_ge(gemm_read[U], 6 * g + (2 * N_U_GLA + 2 * hd + 4))
                    plain(pe)
                    for n in range(NC - 1):
                        r = slice((n % 2) * GLA_C, (n % 2 + 1) * GLA_C)
                        if n == 8:
                            pe.wait_ge(st["att_read"], 8 * g + (4 * hd + 4))
                            plain(pe)
                        last = mm(kv_psum(rows, n), k_dec[r, n // 2, rows],
                                  gv_rows[r, n // 2, :], start=True, stop=True)
                        if n in (7, NC - 2):
                            last.then_inc(st["kv"], 1)
                    pe.wait_ge(st["att_mask"], 4 * g + (2 * hd + 2))
                    pe.wait_ge(st["state"], 4 * g + (2 * hd + 2))
                    for j in range(NT):
                        acc = ps[:, 4 + j // 4, (j % 4) * P:(j % 4 + 1) * P]
                        mm(acc, gv_rows[:, j, :], att_t[:, j, :], start=True, stop=False)
                        for n in (2 * j, 2 * j + 1):
                            if n > 0:
                                last = mm(acc[:, (n % 2) * GLA_C:(n % 2 + 1) * GLA_C], states[rows, n, :],
                                          q_dec[rows, n * GLA_C:(n + 1) * GLA_C], start=False, stop=n % 2 == 1)
                        if j % 4 == 3:
                            last.then_inc(st["o"], 1)
                    for t in range(2):
                        pe.wait_ge(st["osq"], 4 * g + (2 * hd + t + 1))
                        for j in range(4):
                            last = mm(ps[:, 6 + t, j:j + 1], o_gla_sq[:, 4 * t + j, :], inv_d[:, 1:2], start=True, stop=True)
                        last.then_inc(st["stat"], 1)
                    for t in range(2):
                        pe.wait_ge(st["diag"], 4 * g + (2 * hd + t + 1))
                        mm(ps[:, 6 + t, :], ones[:, :], diag[:, :], start=True, stop=True).then_inc(st["spread"], 1)
                    m = 2 * g + (M_GLA + hd)
                    pe.wait_ge(h_ready, 4 * g + (2 * M_GLA + 2 * hd + 2))
                    down_all(m, 0, True)
                    pe.wait_ge(down_read, 32 * g + (16 * (M_GLA + hd + 1) + RING))

            norms(2, [(G, N_G_MEM), (U, N_U_MEM)])

            ms = m_step
            for kk in range(KT // 2):
                if kk == 0:
                    pe.wait_ge(ms["norm"], 2)
                if kk >= 2:
                    pe.wait_ge(ms["ready"], kk - 1)
                for k in range(2):
                    for j in range(2):
                        last = nc.tensor.transpose(ps[:, 4 + kk % 2, (2 * k + j) * P:(2 * k + j + 1) * P],
                                                   mem_rows[:, j, (2 * kk + k) * P:(2 * kk + k + 1) * P], ident[:, :])
                last.then_inc(ms["t"], 1)
            pe.wait_ge(ms["ready"], 4)

            def gemm_mem(slot, n):
                pe.wait_ge(w_ready[slot], n + 1)
                pe.wait_ge(gemm_read[slot], 2 * n)
                for k in range(KT):
                    w, v, acc = w_tile(slot, k), (memt_hi[:, k, :], memt_lo[:, k, :]), ps[:, GEMM_BANK[slot], 0:MEM]
                    mm(acc, w[0], v[0], start=k == 0, stop=False)
                    a = mm(acc, w[0], v[1], start=False, stop=False)
                    b = mm(acc, w[1], v[0], start=False, stop=k == KT - 1)
                a.then_inc(gemm_done[slot], 1)
                b.then_inc(gemm_done[slot], 1)

            with pe.Fori(0, 4) as i:
                for s, nn in ((G, N_G_MEM), (U, N_U_MEM)):
                    gemm_mem(s, i + (nn + 1))
            with pe.Fori(0, 4) as i:
                for s, nn in ((G, N_G_MEM), (U, N_U_MEM)):
                    gemm_mem(s, i + (nn + 5))
                for s, nn in ((G, N_G_MEM), (U, N_U_MEM)):
                    pe.wait_ge(gemm_read[s], 2 * i + (2 * nn + 12))
                    for r in range(2):
                        last = nc.tensor.transpose(ps[:, 4 + s, r * P:(r + 1) * P], mem_vt[:, s, r * P:(r + 1) * P],
                                                   ident[:, :])
                    last.then_inc(ms["vt"], 1)
                pe.wait_ge(ms["vrows"], 4 * i + 4)

            def mem_head(h, more):
                for s, nn in ((G, N_G_MEM), (U, N_U_MEM)):
                    if isinstance(h, int) and h == 0:
                        continue
                    pe.wait_ge(gemm_read[s], 2 * h + (2 * nn + 18))
                for j in range(NT):
                    if j >= 4:
                        pe.wait_ge(ms["exp"], 8 * h + (j - 3))
                    for c in range(2):
                        last = mm(ps[:, j % 4, 0:MEM], q_mem[:, c, j * P:(j + 1) * P], mem_k[:, ds(2 * h + c, 1), :],
                                  start=c == 0, stop=c == 1)
                    last.then_inc(ms["score"], 1)
                for t in range(2):
                    pe.wait_ge(ms["scaled"], 8 * h + (4 * t + 4))
                    if t:
                        pe.wait_ge(ms["pt_read"], 4 * h + 2)
                    for blk in range(2):
                        for j in range(4):
                            last = nc.tensor.transpose(ps[:, 4 + blk, j * P:(j + 1) * P],
                                                       mem_p[:, j, blk * P:(blk + 1) * P], ident[:, :])
                    last.then_inc(ms["pt"], 1)
                    pe.wait_ge(ms["pt_read"], 4 * h + (2 * t + 2))
                    pe.wait_ge(ms["vh"], h + 1)
                    for c in range(2):
                        if t:
                            pe.wait_ge(h_ready, 4 * h + (2 * M_MEM + c + 1))
                        for blk in range(2):
                            last = mm(ps[:, 6 + c, :], mem_vh[:, blk, c * P:(c + 1) * P], mem_pt[:, blk, :],
                                      start=blk == 0, stop=blk == 1)
                        last.then_inc(ms["o"], 1)
                if more:
                    for s, nn in ((G, N_G_MEM), (U, N_U_MEM)):
                        for t in range(2):
                            pe.wait_ge(ms["exp"], 8 * h + 8)
                            gemm(s, h + (nn + 9), t)
                pe.wait_ge(h_ready, 4 * h + (2 * M_MEM + 4))
                for c in range(2):
                    down_all(2 * h + (M_MEM + c), 2 * c, True)
                pe.wait_ge(down_read, 32 * h + (16 * (M_MEM + 2) + RING))

            with pe.Fori(0, MEM_H - 1) as h:
                mem_head(h, True)
            mem_head(MEM_H - 1, False)

            norms(3, [(G, N_G_FF2), (U, N_U_FF2)])
            ff(2)
            norms(4, [])
            pe.wait_ge(x_hi_done, 16 * 5)
            for j in range(NT):
                for b in range(2):
                    if j >= 2:
                        pe.wait_ge(out_read[b], j - 1)
                    for k in range(4):
                        last = nc.tensor.transpose(ps[:, 2 * (j % 2) + b, k * P:(k + 1) * P],
                                                   y[:, 4 * b + k, j * P:(j + 1) * P], ident[:, :])
                    last.then_inc(out_t, 1)

        @block.vector
        def _(dve):
            ve = nc.vector

            def split_lo(slot, n):
                dve.wait_ge(w_hi_done[slot], n + 1)
                ve.tensor_tensor(lo_tile(slot), raw_tile(slot), f32(hi_tile(slot)), ALU.subtract).then_inc(w_ready[slot], 1)

            def add_group(m, d, t, k):
                dve.wait_ge(down_done, 16 * m + (k + 1))
                ve.tensor_tensor(y[:, d, half(t)], y[:, d, half(t)], ps[:, 4 + k % 4, :], ALU.add).then_inc(down_read, 1)

            def add_all(m, by_half):
                for k in range(16):
                    d, t = (k % 8, k // 8) if by_half else (k // 2, k % 2)
                    add_group(m, d, t, k)

            def mean(stage, kind, t):
                e = stat_event(stage, kind, t)
                dve.wait_ge(stat_done, e + 1)
                wait(dve, pow_done, e)
                ve.tensor_scalar(mean4[:, 0:4], ps[:, stat_bank(kind, t), 0:4], EPS, None, ALU.add).then_inc(mean_done, 1)

            def make_diag(stage, kind, t):
                e = stat_event(stage, kind, t)
                dve.wait_ge(pow_done, e + 1)
                wait(dve, spread_done, e)
                ve.tensor_tensor(slot3(diag[:, :]), ident[:, :].unsqueeze(1).to_broadcast([P, 4, P]),
                                 rms4[:, 0:4].unsqueeze(2).to_broadcast([P, 4, P]), ALU.mult).then_inc(diag_done, 1)

            def low_x(stage, i):
                t, d = divmod(i, 8)
                dve.wait_ge(x_hi_done, 16 * stage + i + 1)
                ve.tensor_tensor(x_lo[:, d, half(t)], x_new[:, i % 2, :], f32(x_hi[:, d, half(t)]),
                                 ALU.subtract).then_inc(x_ready, 1)

            def norms(stage):
                if stage > 0:
                    mean(stage, 0, 0)
                    make_diag(stage, 0, 0)
                for i in range(16):
                    t, d = divmod(i, 8)
                    wait(dve, sq_done, sq_event(stage, 1, i) - 1)
                    dve.drain()
                    if stage == 0:
                        dve.wait_ge(x_old, i + 1)
                        ve.tensor_copy(x_new[:, i % 2, :], ps[:, 4 + i % 2, :]).then_inc(x_new_done, 1)
                    else:
                        dve.wait_ge(spread_done, stat_event(stage, 0, t) + 1)
                        ve.scalar_tensor_tensor(out=x_new[:, i % 2, :], in0=y[:, d, half(t)],
                                                scalar=gains[:, GAIN[POST[stage]], d:d + 1], in1=ps[:, 6 + t, :],
                                                op0=ALU.mult, op1=ALU.mult)
                        dve.drain()
                        dve.wait_ge(x_old, 16 * stage + i + 1)
                        ve.tensor_tensor(x_new[:, i % 2, :], x_new[:, i % 2, :], ps[:, 4 + i % 2, :],
                                         ALU.add).then_inc(x_new_done, 1)
                    if stage < 4 and i >= 1:
                        low_x(stage, i - 1)
                    if stage > 0 and i == 1:
                        mean(stage, 0, 1)
                    if stage > 0 and i == 3:
                        make_diag(stage, 0, 1)
                    if i == 9:
                        mean(stage, 1, 0)
                    if i == 11 and stage < 4:
                        make_diag(stage, 1, 0)
                if stage < 4:
                    low_x(stage, 15)
                mean(stage, 1, 1)
                if stage < 4:
                    make_diag(stage, 1, 1)

            def ff(which):
                f = FF[which]

                def chunk(c, parity, first=False, last=False):
                    nG, nU, m = f["nG"] + c, f["nU"] + c, f["m"] + c

                    def scale_gate(t):
                        wait(dve, silu_done, f["s"] + 2 * c + (t - 1))
                        dve.wait_ge(gemm_done[G], 2 * nG + (t + 1))
                        ve.tensor_tensor(gate[:, t, :], ps[:, t, :], rs[:, half(t)], ALU.mult).then_inc(gemm_read[G], 1)

                    def times_up(t):
                        dve.wait_ge(gemm_done[U], 2 * nU + (t + 1))
                        dve.wait_ge(gate_scaled, f["s"] + 2 * c + (t + 1))
                        ve.tensor_tensor(hidden[:, t, :], ps[:, 2 + t, :], gate_act[:, t, :],
                                         ALU.mult).then_inc(gemm_read[U], 1)

                    def low_hidden(t):
                        dve.wait_ge(h_hi_done, 2 * m + (t + 1))
                        ve.tensor_tensor(h_lo[parity][:, half(t)], hidden[:, t, :], f32(h_hi[parity][:, half(t)]),
                                         ALU.subtract).then_inc(h_ready, 1)

                    def add_groups(q):
                        if not first:
                            for k in range(4 * q, 4 * q + 4):
                                add_group(m - 1, k // 2, k % 2, k)

                    if first:
                        for t in range(2):
                            dve.wait_ge(rs_ready, 2 * (0 if which == 1 else 3) + 1 + t)
                            scale_gate(t)
                    else:
                        dve.drain()
                        scale_gate(0)
                        split_lo(U, nU)
                        add_groups(0)
                        split_lo(B, m - 1)
                        scale_gate(1)
                        add_groups(1)
                    if not last:
                        split_lo(G, nG + 1)
                    times_up(0)
                    split_lo(A, m)
                    low_hidden(0)
                    add_groups(2)
                    times_up(1)
                    low_hidden(1)
                    add_groups(3)

                chunk(0, 0, first=True)
                dve.wait_ge(y_zero, 8 * (1 if which == 1 else 4))
                with dve.Fori(0, (FC - 2) // 2) as i:
                    chunk(i * 2 + 1, 1)
                    chunk(i * 2 + 2, 0)
                chunk(FC - 1, 1, last=True)
                split_lo(B, f["m"] + FC - 1)
                dve.drain()
                add_all(f["m"] + FC - 1, True)

            dve.sem_inc(down_read, RING)
            dve.wait_ge(const_ready, 1)
            ve.tensor_copy(ident_r[:, :], ident[:, :])
            dve.wait_ge(gains_t, 1)
            ve.tensor_copy(gains[:, :, :].rearrange("p a k -> p (a k)"), ps[:, 6, 0:11 * KT])
            dve.drain()
            for name in ("ff1_post", "ff2_post"):
                g = gains[:, GAIN[name], :]
                ve.tensor_scalar(g, g, 0.5, None, ALU.mult)
            dve.drain().then_inc(const_ready, 1)
            split_lo(G, 0)
            split_lo(U, 0)
            norms(0)
            ff(1)
            split_lo(G, N_G_MIX)
            norms(1)

            row = slice(32, 40)
            dve.wait_ge(g_step["consts"], 1)
            for t in range(2):
                dve.wait_ge(rs_ready, 3 + t)
                dve.wait_ge(gemm_done[G], 2 * N_G_MIX + t + 1)
                ve.tensor_tensor(gate_low[0:RANK, half(t)], ps[0:RANK, t, :], rs[0:RANK, half(t)], ALU.mult)
                ve.tensor_tensor(forget[row, half(t)], ps[row, t, :], rs[row, half(t)], ALU.mult).then_inc(gemm_read[G], 1)
            dve.drain()
            dve.wait_ge(small_in, 16 * 4)
            for t in range(2):
                ve.tensor_scalar(forget[row, half(t)], forget[row, half(t)], b_f[row, :], None, ALU.add).then_inc(ff_step, 1)
            dve.wait_ge(ff_step, 5)
            ve.scalar_tensor_tensor(out=forget_a[row, :], in0=forget[row, :], scalar=0.0, in1=forget_a[row, :], op0=ALU.min,
                                    op1=ALU.subtract).then_inc(ff_step, 1)
            dve.wait_ge(ff_step, 7)
            ve.tensor_copy(lf_rows[:, :, :].rearrange("p a b -> p (a b)"), ps[:, 4, 0:NT * FOX_H]).then_inc(ff_step, 1)
            dve.wait_ge(ff_step, 9)
            c_psum = ps[0:FOX_H, 2:4, :].rearrange("p a b -> p (a b)")
            ve.tensor_copy(c_sb[:, 0, :], c_psum).then_inc(ff_step, 1)
            ve.tensor_scalar(c_sb[:, 1, :], c_psum, -1.0, None, ALU.mult).then_inc(ff_step, 1)
            dve.wait_ge(head_ones, 1)

            def attend_fox(p):
                for a in range(19):
                    if a < 16:
                        hh, b = divmod(a, 8)
                        dve.wait_ge(score_done, 16 * p + (a + 1))
                        bank = 2 * (a % 2)
                        ve.tensor_reduce(out=neg_max[:, b, hh:hh + 1],
                                         in_=ps[:, bank:bank + 2, :].rearrange("p a b -> p (a b)")[:, 0:(b + 1) * P],
                                         op=ALU.max, axis=AX.X, negate=True).then_inc(max_done, 1)
                    if a >= 3:
                        h3, b3 = divmod(a - 3, 8)
                        ve.reciprocal(row_inv[:, b3, h3:h3 + 1], row_sum[:, b3, h3:h3 + 1])
                    if 1 <= a <= 16:
                        b1 = (a - 1) % 8
                        dve.wait_ge(pt_lo, 16 * p + a)
                        if a >= 3:
                            dve.wait_ge(o_done, 16 * p + (a - 2))
                        n = min(b1 + 1, 4)
                        ve.tensor_copy(probs_t[:, (a - 1) % 2, 0:n, :].rearrange("p a b -> p (a b)"),
                                       ps[:, 4, 0:n * P]).then_inc(pt_lo_read, 1)
                    if a >= 3:
                        dve.drain()
                        dve.wait_ge(o_done, 16 * p + (a - 2))
                        ve.tensor_scalar(o_rows[:, b3, h3, :], ps[:, 6 + (a - 3) % 2, 0:FOX_D], row_inv[:, b3, h3:h3 + 1],
                                         None, ALU.mult).then_inc(o_read, 1)

            with dve.Fori(0, FOX_PAIRS) as p:
                dve.drain()
                split_lo(U, 2 * p + N_U_FOX)
                split_lo(G, p + N_G_FOX)
                for t in range(2):
                    dve.wait_ge(gemm_done[U], 4 * p + (2 * N_U_FOX + t + 1))
                    for i in range(2):
                        r = slice(i * FOX_D, (i + 1) * FOX_D)
                        last = ve.scalar_tensor_tensor(out=q_head[i][0:FOX_D, half(t)], in0=ps[r, 2 + t, :],
                                                       scalar=FOX_D ** -0.5, in1=rs[r, half(t)], op0=ALU.mult, op1=ALU.mult)
                    last.then_inc(gemm_read[U], 1)
                split_lo(U, 2 * p + (N_U_FOX + 1))
                for t in range(2):
                    dve.wait_ge(gemm_done[G], 2 * p + (2 * N_G_FOX + t + 1))
                    for i in range(2):
                        r = slice(i * FOX_D, (i + 1) * FOX_D)
                        last = ve.tensor_tensor(k_head[i][0:FOX_D, half(t)], ps[r, t, :], rs[r, half(t)], ALU.mult)
                    last.then_inc(gemm_read[G], 1)
                for t in range(2):
                    dve.wait_ge(gemm_done[U], 4 * p + (2 * N_U_FOX + 2 + t + 1))
                    ve.tensor_tensor(v_t[:, half(t)], ps[:, 2 + t, :], rs[:, half(t)], ALU.mult).then_inc(gemm_read[U], 1)
                attend_fox(p)
                dve.wait_ge(o_sq_done, 16 * p + 16)
                ve.tensor_scalar(mean4[:, :], o_sq[:, :, :].rearrange("p a b -> p (a b)"), 1.0 / FOX_D, EPS, ALU.mult,
                                 ALU.add).then_inc(o_mean, 1)
                dve.wait_ge(o_pow, p + 1)
                o16 = o_rows[:, :, :, :].rearrange("p a b c -> p (a b) c")
                ve.tensor_tensor(o16, o16, rms4[:, :].unsqueeze(2).to_broadcast([P, 16, FOX_D]), ALU.mult).then_inc(o_norm, 1)
                split_lo(A, p + M_MIX)
                split_lo(B, p + M_MIX)
                for t in range(2):
                    dve.wait_ge(h_hi_done, 2 * p + (2 * M_MIX + t + 1))
                    ve.scalar_tensor_tensor(out=h_lo[0][:, half(t)], in0=ps[:, 4 + t, :], scalar=head_gains[:, 0, ds(p, 1)],
                                            in1=f32(h_hi[0][:, half(t)]), op0=ALU.mult, op1=ALU.subtract).then_inc(h_ready, 1)
                dve.wait_ge(y_zero, 16)
                add_all(p + M_MIX, True)

            st = g_step
            with dve.Fori(0, GLA_PAIRS) as g:
                dve.drain()
                split_lo(G, 3 * g + N_G_GLA)
                split_lo(U, 3 * g + N_U_GLA)
                for i in range(2):
                    dve.wait_ge(st["logsig"], 6 * g + (3 * i + 3))
                    ve.scalar_tensor_tensor(out=la[:, 4 * i:4 * i + 4, :].rearrange("p a b -> p (a b)"), in0=ps[:, 4 + i, :],
                                            scalar=0.0, in1=gate_a[:, half(i)], op0=ALU.min,
                                            op1=ALU.subtract).then_inc(st["la"], 1)
                for t in range(2):
                    dve.wait_ge(gemm_done[G], 6 * g + (2 * N_G_GLA + t + 1))
                    ve.scalar_tensor_tensor(out=q_dec[:, half(t)], in0=ps[:, t, :], scalar=GLA_C ** -0.5,
                                            in1=rs[:, half(t)], op0=ALU.mult, op1=ALU.mult).then_inc(gemm_read[G], 1)
                for t in range(2):
                    dve.wait_ge(gemm_done[U], 6 * g + (2 * N_U_GLA + t + 1))
                    ve.tensor_tensor(k_inv[:, half(t)], ps[:, 2 + t, :], rs[:, half(t)], ALU.mult).then_inc(gemm_read[U], 1)
                for i in range(2):
                    dve.wait_ge(st["kt"], 2 * g + (i + 1))
                    dve.wait_ge(st["esuf"], 2 * g + (i + 1))
                    tiles = slice(4 * i, 4 * i + 4)
                    ve.tensor_tensor(k_dec[:, tiles, :].rearrange("p a b -> p (a b)"), ps[:, 4 + i, :],
                                     e_suf[:, tiles, :].rearrange("p a b -> p (a b)"), ALU.mult).then_inc(st["kdec"], 1)
                dve.drain()
                ve.tensor_tensor(k_inv[:, :], k_inv[:, :], e_nb[:, :], ALU.mult)
                ve.tensor_copy(decay[:, :], e_b[:, :].rearrange("p (n c) -> p n c", c=GLA_C)[:, :, GLA_C - 1])
                ve.tensor_tensor(q_dec[:, :], q_dec[:, :], e_b[:, :], ALU.mult)
                dve.drain().then_inc(st["qdec"], 1)
                dve.wait_ge(st["zero"], g + 1)
                for hd in range(2):
                    rows = slice(hd * GLA_C, (hd + 1) * GLA_C)
                    split_lo(G, 3 * g + (N_G_GLA + 1 + hd))
                    split_lo(U, 3 * g + (N_U_GLA + 1 + hd))
                    for dst, slot, nn in ((gv_t, G, N_G_GLA), (r_act, U, N_U_GLA)):
                        for t in range(2):
                            dve.wait_ge(gemm_done[slot], 6 * g + (2 * nn + 2 * hd + 2 + t + 1))
                            ve.tensor_tensor(dst[:, half(t)], ps[:, GEMM_BANK[slot] + t, :], rs[:, half(t)],
                                             ALU.mult).then_inc(gemm_read[slot], 1)
                    for i in range(2):
                        dve.wait_ge(st["att"], 4 * g + (2 * hd + i + 1))
                        for r in range(2):
                            rr = slice(r * GLA_C, (r + 1) * GLA_C)
                            ve.tensor_copy(att_t[rr, 4 * i:4 * i + 4, rr], slot3(ps[rr, i, :])[:, :, rr]).then_inc(st["att_read"], 1)
                    for n in range(NC - 1):
                        kv = kv_psum(rows, n)
                        if n % 8 == 0:
                            dve.wait_ge(st["kv"], 4 * g + (2 * hd + n // 8 + 1))
                            plain(dve)
                        if n == 0:
                            s_next = ve.tensor_copy(states[rows, 1, :], kv)
                        else:
                            dve.drain()
                            s_next = ve.scalar_tensor_tensor(out=states[rows, n + 1, :], in0=states[rows, n, :],
                                                             scalar=decay[rows, n:n + 1], in1=kv, op0=ALU.mult, op1=ALU.add)
                        if n in (7, NC - 2):
                            s_next.then_inc(st["state"], 1)
                    for t in range(2):
                        dve.wait_ge(st["stat"], 4 * g + (2 * hd + t + 1))
                        ve.tensor_scalar(mean4[:, 0:4], ps[:, 6 + t, 0:4], EPS, None, ALU.add).then_inc(st["mean"], 1)
                        dve.wait_ge(st["pow"], 4 * g + (2 * hd + t + 1))
                        if t:
                            dve.wait_ge(st["spread"], 4 * g + (2 * hd + 1))
                        ve.tensor_tensor(slot3(diag[:, :]), ident[:, :].unsqueeze(1).to_broadcast([P, 4, P]),
                                         rms4[:, 0:4].unsqueeze(2).to_broadcast([P, 4, P]), ALU.mult).then_inc(st["diag"], 1)
                    split_lo(A, 2 * g + (M_GLA + hd))
                    split_lo(B, 2 * g + (M_GLA + hd))
                    for t in range(2):
                        dve.wait_ge(st["spread"], 4 * g + (2 * hd + t + 1))
                        dve.wait_ge(st["o_copy"], 4 * g + (2 * hd + t + 1))
                        ve.scalar_tensor_tensor(out=x_new[:, t, :], in0=o_gla[:, half(t)],
                                                scalar=head_gains[:, 1, ds(2 * g + hd, 1)], in1=ps[:, 6 + t, :],
                                                op0=ALU.mult, op1=ALU.mult)
                        dve.drain()
                        dve.wait_ge(st["silu"], 4 * g + (2 * hd + t + 1))
                        ve.tensor_tensor(x_new[:, t, :], x_new[:, t, :], r_act[:, half(t)], ALU.mult).then_inc(st["h"], 1)
                    for t in range(2):
                        dve.wait_ge(h_hi_done, 4 * g + (2 * M_GLA + 2 * hd + t + 1))
                        ve.tensor_tensor(h_lo[0][:, half(t)], x_new[:, t, :], f32(h_hi[0][:, half(t)]),
                                         ALU.subtract).then_inc(h_ready, 1)
                    add_all(2 * g + (M_GLA + hd), True)

            split_lo(G, N_G_MEM)
            split_lo(U, N_U_MEM)
            norms(2)

            ms = m_step

            def queries(h):
                for t in range(2):
                    for c, (s, nn) in enumerate(((G, N_G_MEM), (U, N_U_MEM))):
                        n = 2 * nn + t + 1 if h is None else 2 * h + (2 * nn + 18 + t + 1)
                        dve.wait_ge(gemm_done[s], n)
                        ve.tensor_tensor(q_mem[:, c, half(t)], ps[:, GEMM_BANK[s] + t, :], rs[:, half(t)],
                                         ALU.mult).then_inc(gemm_read[s], 1)

            dve.wait_ge(rs_ready, 6)
            queries(None)
            for s, nn in ((G, N_G_MEM), (U, N_U_MEM)):
                split_lo(s, nn + 1)
            dve.wait_ge(ms["sq"], 2)
            ve.tensor_scalar(mem_stat[:, 0:2], mem_stat[:, 0:2], 1.0 / D, EPS, ALU.mult, ALU.add).then_inc(ms["mean"], 1)
            dve.wait_ge(ms["pow"], 1)
            for j in range(2):
                ve.tensor_scalar(mem_rows[:, j, :], mem_rows[:, j, :], mem_stat[:, 2 + j:3 + j], None,
                                 ALU.mult).then_inc(ms["norm"], 1)
            for k in range(KT // 2):
                dve.wait_ge(ms["hi"], k + 1)
                part = slice(2 * k, 2 * k + 2)
                ve.tensor_tensor(memt_lo[:, part, :].rearrange("p a b -> p (a b)"), ps[:, 4 + k % 2, :],
                                 f32(memt_hi[:, part, :].rearrange("p a b -> p (a b)")), ALU.subtract).then_inc(ms["ready"], 1)
            with dve.Fori(0, 4) as i:
                for s, nn in ((G, N_G_MEM), (U, N_U_MEM)):
                    split_lo(s, i + (nn + 2))
            with dve.Fori(0, 4) as i:
                for s, nn in ((G, N_G_MEM), (U, N_U_MEM)):
                    dve.wait_ge(gemm_done[s], 2 * i + (2 * nn + 12))
                    for r in range(2):
                        ve.tensor_copy(mem_vt[:, s, r * P:(r + 1) * P],
                                       ps[:, GEMM_BANK[s], r * P:(r + 1) * P]).then_inc(gemm_read[s], 1)
                    split_lo(s, i + (nn + 6))
                dve.wait_ge(ms["vt"], 2 * i + 2)

            def mem_head(h, more):
                def maximum(j):
                    dve.wait_ge(ms["score"], 8 * h + (j + 1))
                    ve.tensor_reduce(out=mem_max[:, j:j + 1], in_=ps[:, j % 4, 0:MEM], op=ALU.max, axis=AX.X,
                                     negate=True).then_inc(ms["max"], 1)

                def divide(j):
                    dve.wait_ge(ms["exp"], 8 * h + (j + 1))
                    ve.reciprocal(mem_inv[:, j:j + 1], mem_sum[:, j:j + 1])
                    dve.drain()
                    ve.tensor_scalar(mem_p[:, j % 4, :], mem_p[:, j % 4, :], mem_inv[:, j:j + 1], None,
                                     ALU.mult).then_inc(ms["scaled"], 1)

                dve.drain()
                for j in range(4):
                    maximum(j)
                for j in range(4):
                    divide(j)
                    maximum(j + 4)
                for j in range(4, 8):
                    if j == 4:
                        for c in range(2):
                            low(h, 0, c)
                    divide(j)
                for c in range(2):
                    low(h, 1, c)
                if more:
                    split_lo(G, h + (N_G_MEM + 10))
                    split_lo(U, h + (N_U_MEM + 10))
                    queries(h)
                for c in range(2):
                    split_lo(A, 2 * h + (M_MEM + c))
                    split_lo(B, 2 * h + (M_MEM + c))
                    dve.wait_ge(y_zero, 24)
                    add_all(2 * h + (M_MEM + c), True)

            def low(h, t, c):
                dve.wait_ge(h_hi_done, 4 * h + (2 * M_MEM + 2 * t + c + 1))
                ve.tensor_tensor(h_lo[2 * c][:, half(t)], ps[:, 6 + c, :], f32(h_hi[2 * c][:, half(t)]),
                                 ALU.subtract).then_inc(h_ready, 1)

            with dve.Fori(0, MEM_H - 1) as h:
                mem_head(h, True)
            mem_head(MEM_H - 1, False)

            norms(3)
            ff(2)
            norms(4)
            for j in range(NT):
                dve.wait_ge(out_t, 2 * j + 2)
                dve.wait_ge(pow_done, 18)
                if j >= 2:
                    dve.wait_ge(out_sent[j % 2], 16 * (j // 2))
                ve.tensor_scalar(out_rows[:, j % 2, HT:D], ps[:, 2 * (j % 2) + 1, :], rms8[:, j:j + 1], None,
                                 ALU.mult).then_inc(out_read[1], 1)


def kernel(**inputs):
    import numpy as np
    import concourse.bacc as bacc
    from concourse.bass_utils import run_bass_kernel_spmd

    nc = bacc.Bacc("TRN2", target_bir_lowering=False, num_devices=1)
    arrays, args = {}, []
    for name in NAMES:
        a = np.ascontiguousarray(inputs[name])
        arrays["in_" + name] = a
        args.append(nc.dram_tensor("in_" + name, a.shape, mybir.dt.from_np(a.dtype), kind="ExternalInput").ap())
    args.append(nc.dram_tensor("out_x", (1, T, D), F32, kind="ExternalOutput").ap())
    build_layer(nc, *args)
    r = run_bass_kernel_spmd(nc, [arrays], core_ids=[0])
    return r.results[0]["out_x"]


NAMES = ["x", "mem", "g_ff1_pre", "w_ff1_gate", "w_ff1_up", "w_ff1_down", "g_ff1_post",
         "g_mix_pre", "w_mix_in", "b_fox_f", "w_gla_g2", "b_gla_g", "g_fox_out", "g_gla_out",
         "w_mix_out", "g_mix_post", "g_mem_pre", "g_mem_src", "w_mem_q", "w_mem_kv", "w_mem_o",
         "g_mem_post", "g_ff2_pre", "w_ff2_gate", "w_ff2_up", "w_ff2_down", "g_ff2_post", "g_final"]
```

```python
import concourse.bass as bass
from concourse import mybir
from contextlib import ExitStack

F32 = mybir.dt.float32
F32R = mybir.dt.float32r
BF16 = mybir.dt.bfloat16
ALU = mybir.AluOpType
ACT = mybir.ActivationFunctionType
AX = mybir.AxisListType
ds = bass.ds

P = 128
D = 1024
T = 1024
HT = 512
KT = D // P
NT = T // P
D_FF = 2816
FC = D_FF // P
MEM = 256
EPS = 1e-6

FOX_H, FOX_D = 8, 64
OFF_FQ, OFF_FK, OFF_FV, OFF_FF = 0, 512, 1024, 1536
OFF_GQ = OFF_FF + FOX_H
OFF_GK = OFF_GQ + 256
OFF_GV = OFF_GK + 256
OFF_GG = OFF_GV + 512
RANK = 16
OFF_GR = OFF_GG + RANK
GLA_C = 64
NC = T // GLA_C
FOX_PAIRS, GLA_PAIRS, MEM_H = FOX_H // 2, 2, 4

N_G_MIX, N_U_MIX, M_MIX = FC, FC, FC
N_G_FOX, N_U_FOX = N_G_MIX + 1, N_U_MIX
N_G_GLA, N_U_GLA, M_GLA = N_G_FOX + FOX_PAIRS, N_U_FOX + 2 * FOX_PAIRS, M_MIX + FOX_PAIRS
N_G_MEM, N_U_MEM, M_MEM = N_G_GLA + 3 * GLA_PAIRS, N_U_GLA + 3 * GLA_PAIRS, M_GLA + 2 * GLA_PAIRS
N_G_FF2, N_U_FF2, M_FF2 = N_G_MEM + 12, N_U_MEM + 12, M_MEM + 8
G, U, A, B = range(4)
RING = 4


def build_layer(nc, x, mem, g_ff1_pre, w_ff1_gate, w_ff1_up, w_ff1_down, g_ff1_post,
                g_mix_pre, w_mix_in, b_fox_f, w_gla_g2, b_gla_g, g_fox_out, g_gla_out,
                w_mix_out, g_mix_post, g_mem_pre, g_mem_src, w_mem_q, w_mem_kv, w_mem_o,
                g_mem_post, g_ff2_pre, w_ff2_gate, w_ff2_up, w_ff2_down, g_ff2_post, g_final, out):
    ctx = ExitStack()
    with ctx:
        def sb(name, shape, dt=F32, where=None):
            return (where or ctx).enter_context(nc.sbuf_tensor(name, shape, dt))

        def sem(name):
            return ctx.enter_context(nc.semaphore(name))

        x_hi = sb("x_hi", [P, KT, T], F32R)
        x_lo = sb("x_lo", [P, KT, T], F32R)
        y = sb("y", [P, KT, T])
        raw = sb("raw", [P, 3, D])
        w_hi = sb("w_hi", [P, 3, D], F32R)
        w_lo = sb("w_lo", [P, 3, D], F32R)
        h_hi, h_lo = [sb("h_hi", [P, T], F32R)], [sb("h_lo", [P, T], F32R)]
        rs = sb("rs", [P, T])
        sq = sb("sq", [P, 4, HT])
        x_new = sb("x_new", [P, 2, HT])
        post_rs = sb("post_rs", [P, T])
        diag = sb("diag", [P, HT])
        ident = sb("ident", [P, P])
        ones = sb("ones", [P, P])
        ident_r = sb("ident_r", [P, P], F32R)
        mean4 = sb("mean4", [P, 16])
        rms4 = sb("rms4", [P, 16])
        rms8 = sb("rms8", [P, NT])
        minus_half = sb("minus_half", [P, 16])
        inv_d = sb("inv_d", [P, 2])
        gains = sb("gains", [P, 11, KT])
        GAIN = {n: i for i, n in enumerate(
            ["ff1_pre", "ff1_post", "mix_pre", "mix_post", "mem_pre", "mem_post", "ff2_pre", "ff2_post",
             "final", "mem_src"])}
        head_gains = gains[:, 10, :].rearrange("p (a k) -> p a k", a=2)
        w_g2 = sb("w_g2", [32, 256])
        b_f = sb("b_f", [40, 1])
        ps = ctx.enter_context(nc.psum_tensor("ps", [P, 8, HT], F32))
        c_rows = nc.dram_tensor("c_rows", [2, FOX_H, T], F32, kind="Internal").ap()

        with ExitStack() as s:
            h_hi.append(sb("h_hi_ff", [P, T], F32R, where=s))
            h_lo.append(sb("h_lo_ff", [P, T], F32R, where=s))
            gate = sb("gate", [P, 2, HT], where=s)
            gate_act = sb("gate_act", [P, 2, HT], where=s)
            hidden = sb("hidden", [P, 2, HT], where=s)
            out_rows = sb("out_rows", [P, 2, D], where=s)
        with ExitStack() as s:
            gate_low = sb("gate_low", [32, T], where=s)
            tri_blk = sb("tri_blk", [P, P], where=s)
            tri_suf = sb("tri_suf", [P, P], where=s)
            ident_b = sb("ident_b", [P, P], BF16, where=s)
            neg_mask = sb("neg_mask", [P, P], BF16, where=s)
            with ExitStack() as f:
                q_head = [sb(f"q_head{i}", [66, T], where=f) for i in range(2)]
                k_head = [sb(f"k_head{i}", [66, T], where=f) for i in range(2)]
                v_rows = sb("v_rows", [P, NT, P], where=f)
                probs = sb("probs", [P, 2, T], where=f)
                v_t = probs[:, 0, :]
                probs_t = sb("probs_t", [P, 2, NT, P], where=f)
                o_rows = x_new[:, :, :].rearrange("p a (t i d) -> p (a t) i d", i=2, d=FOX_D)
                row_sum = sb("row_sum", [P, NT, 2], where=f)
                row_inv = sb("row_inv", [P, NT, 2], where=f)
                neg_max = sb("neg_max", [P, NT, 2], where=f)
                o_sq = sb("o_sq", [P, NT, 2], where=f)
                o_junk = sb("o_junk", [P, FOX_D], where=f)
                lf_rows = sb("lf_rows", [P, NT, FOX_H], where=f)
                tri_wide = v_rows[:, :, :].rearrange("p a b -> p (a b)")
                forget = probs_t[0:40, 0, :, :].rearrange("p a b -> p (a b)")
                forget_a = probs_t[0:40, 1, :, :].rearrange("p a b -> p (a b)")
                c_sb = sq[0:FOX_H, :, :].rearrange("p (s a) t -> p s (a t)", s=2)
            with ExitStack() as f:
                la = sb("la", [P, NT, P], where=f)
                e_b = sb("e_b", [P, T], where=f)
                e_nb = sb("e_nb", [P, T], where=f)
                e_suf = sb("e_suf", [P, NT, P], where=f)
                q_dec = sb("q_dec", [P, T], where=f)
                k_inv = sb("k_inv", [P, T], where=f)
                k_dec = sb("k_dec", [P, NT, P], where=f)
                gv_rows = sb("gv_rows", [P, NT, P], where=f)
                states = sq[:, :, :].rearrange("p a (n c) -> p (a n) c", c=P)
                decay = sb("decay", [P, NC], where=f)
                gate_a = e_nb
                gv_t = e_nb
                o_gla = e_nb
                att_t = e_suf
                o_gla_sq = la
                r_act = e_b
        with ExitStack() as s:
            mem_k = sb("mem_k", [P, KT, MEM], where=s)
            mem_v = sb("mem_v", [P, 2, D], where=s)
            q_mem = sb("q_mem", [P, 2, T], where=s)
            mem_stat = sb("mem_stat", [P, 4], where=s)
            with ExitStack() as f:
                mem_rows = mem_v
                memt_hi = sb("memt_hi", [P, KT, MEM], F32R, where=f)
                memt_lo = sb("memt_lo", [P, KT, MEM], F32R, where=f)
                mem_vt = x_new[:, :, 0:MEM]
            with ExitStack() as f:
                h_hi.append(sb("h_hi_mem", [P, T], F32R, where=f))
                h_lo.append(sb("h_lo_mem", [P, T], F32R, where=f))
                mem_vh = sb("mem_vh", [P, 2, MEM], where=f)
                mem_p = sb("mem_p", [P, 4, MEM], where=f)
                mem_pt = sb("mem_pt", [P, 2, HT], where=f)
                mem_max = sb("mem_max", [P, NT], where=f)
                mem_sum = sb("mem_sum", [P, NT], where=f)
                mem_inv = sb("mem_inv", [P, NT], where=f)

        const_ready = sem("const_ready")
        passed = sem("passed")
        gains_in = sem("gains_in")
        gains_t = sem("gains_t")
        x_in = [sem("x_in_0"), sem("x_in_1")]
        raw_in = [sem(f"raw_in_{s}") for s in "guab"]
        small_in = sem("small_in")
        small_zero = sem("small_zero")
        w_scaled = [sem(f"w_scaled_{s}") for s in "gu"]
        w_hi_done = [sem(f"w_hi_done_{s}") for s in "guab"]
        w_ready = [sem(f"w_ready_{s}") for s in "guab"]
        gemm_done = [sem("gemm_done_g"), sem("gemm_done_u")]
        gemm_read = [sem("gemm_read_g"), sem("gemm_read_u")]
        down_done = sem("down_done")
        down_read = sem("down_read")
        silu_done = sem("silu_done")
        gate_scaled = sem("gate_scaled")
        h_hi_done = sem("h_hi_done")
        h_ready = sem("h_ready")
        y_zero = sem("y_zero")
        sq_done, sq_added, x_sq_added = sem("sq_done"), sem("sq_added"), sem("x_sq_added")
        stat_done, mean_done = sem("stat_done"), sem("mean_done")
        pow_done, diag_done, spread_done = sem("pow_done"), sem("diag_done"), sem("spread_done")
        rs_ready, y_scaled = sem("rs_ready"), sem("y_scaled")
        x_old = sem("x_old")
        x_new_done, x_hi_done, x_ready = sem("x_new_done"), sem("x_hi_done"), sem("x_ready")
        out_t = sem("out_t")
        out_sent = [sem("out_sent_even"), sem("out_sent_odd")]
        out_read = [sem("out_read_act"), sem("out_read_dve")]
        ff_step = sem("ff_step")
        c_sent = sem("c_sent")
        c_in = sem("c_in")
        head_ones = sem("head_ones")
        v_t_done, v_rows_done = sem("v_t_done"), sem("v_rows_done")
        score_done, max_done, exp_done = sem("score_done"), sem("max_done"), sem("exp_done")
        pt_lo, pt_hi, pt_lo_read, pt_hi_read = sem("pt_lo"), sem("pt_hi"), sem("pt_lo_read"), sem("pt_hi_read")
        o_done, o_read, o_sq_done = sem("o_done"), sem("o_read"), sem("o_sq_done")
        o_mean, o_pow, o_norm, o_t = sem("o_mean"), sem("o_pow"), sem("o_norm"), sem("o_t")
        g_step = {n: sem("gla_" + n) for n in (
            "consts", "gate", "logsig", "la", "b", "suf", "eb", "esuf", "decay", "kt", "kdec", "kinv",
            "vt", "vrows", "att", "att_read", "att_mask", "kv", "state", "o", "o_copy", "osq", "stat",
            "mean", "pow", "diag", "spread", "silu", "onorm", "h", "qdec", "logdone", "zero")}
        m_step = {n: sem("mem_" + n) for n in (
            "in", "sq", "mean", "pow", "norm", "t", "hi", "ready", "vt", "vrows", "vh",
            "score", "max", "exp", "scaled", "pt", "pt_read", "o")}

        GEMM_BANK = {G: 0, U: 2}

        def wait(eng, semaphore, value):
            if not (isinstance(value, int) and value <= 0):
                eng.wait_ge(semaphore, value)

        def plain(eng):
            eng.sem_inc(passed, 1)

        def raw_tile(slot):
            return raw[:, slot, :] if slot < 2 else raw[:, 2, (slot - A) * HT:(slot - A + 1) * HT]

        def hi_tile(slot):
            return w_hi[:, slot, :] if slot < 2 else w_hi[:, 2, (slot - A) * HT:(slot - A + 1) * HT]

        def lo_tile(slot):
            return w_lo[:, slot, :] if slot < 2 else w_lo[:, 2, (slot - A) * HT:(slot - A + 1) * HT]

        def f32(ap):
            return ap.bitcast(F32)

        def half(t):
            return slice(t * HT, (t + 1) * HT)

        def stat_event(stage, kind, t):
            return t if stage == 0 else 2 + 4 * (stage - 1) + 2 * kind + t

        def stat_bank(kind, t):
            return t if kind == 0 else 6 + t

        def kv_psum(rows, n):
            c = n // 2 % 4
            return ps[rows, (2 if n < 8 else 0) + n % 2, c * P:(c + 1) * P]

        def sq_event(stage, kind, i):
            return 8 * stat_event(stage, kind, 0) + i

        FF = {1: dict(nG=0, nU=0, m=0, s=0, pre="ff1_pre", gate=w_ff1_gate, up=w_ff1_up, down=w_ff1_down),
              2: dict(nG=N_G_FF2, nU=N_U_FF2, m=M_FF2, s=2 * FC, pre="ff2_pre",
                      gate=w_ff2_gate, up=w_ff2_up, down=w_ff2_down)}
        POST = {1: "ff1_post", 2: "mix_post", 3: "mem_post", 4: "ff2_post"}
        LAST_M = {1: FC - 1, 2: M_MEM - 1, 3: M_FF2 - 1, 4: M_FF2 + FC - 1}

        def cols(w, c0):
            return w[0].rearrange("(k p) n -> p k n", p=P)[:, :, c0]

        def slot3(ap):
            return ap.rearrange("p (k c) -> p k c", c=P)

        block = ctx.enter_context(nc.Block())

        @block.sync
        def _(sp):
            def load(slot, n, src):
                wait(sp, w_ready[slot], n)
                dst = raw_tile(slot) if slot >= A else slot3(raw_tile(slot))
                sp.dma_start(dst, src).then_inc(raw_in[slot], 16)

            def load_down(slot, m, w, row0):
                load(slot, m, w[0][ds(row0, P), (slot - A) * HT:(slot - A + 1) * HT])

            for j in range(NT):
                sp.dma_start(y[:, j, :], x[0][j * P:(j + 1) * P, :]).then_inc(x_in[j // 4], 16)
                if j == 3:
                    load(G, 0, cols(w_ff1_gate, ds(0, P)))
                    load(U, 0, cols(w_ff1_up, ds(0, P)))

            def ff(which, tail):
                f = FF[which]

                def chunk(c, after_g):
                    if not (isinstance(c, int) and c == FC - 1):
                        load(U, f["nU"] + c + 1, cols(f["up"], ds((c + 1) * P, P)))
                    load_down(B, f["m"] + c, f["down"], c * P)
                    if after_g:
                        load(G, f["nG"] + c + 2, cols(f["gate"], ds((c + 2) * P, P)))
                    if not (isinstance(c, int) and c == FC - 1):
                        load_down(A, f["m"] + c + 1, f["down"], (c + 1) * P)

                load_down(A, f["m"], f["down"], 0)
                load(G, f["nG"] + 1, cols(f["gate"], ds(P, P)))
                chunk(0, True)
                with sp.Fori(0, (FC - 4) // 2) as i:
                    chunk(i * 2 + 1, True)
                    chunk(i * 2 + 2, True)
                chunk(FC - 3, True)
                chunk(FC - 2, False)
                chunk(FC - 1, False)

            ff(1, None)
            load(U, N_U_FOX, cols(w_mix_in, slice(OFF_FQ, OFF_FQ + P)))
            sp.dma_start(w_g2[0:RANK, :], w_gla_g2[0]).then_inc(small_in, 16)
            wait(sp, w_ready[G], N_G_MIX)
            sp.wait_ge(small_zero, 1)
            small = slot3(raw_tile(G))
            sp.dma_start(small[:, :, 0:RANK], cols(w_mix_in, slice(OFF_GG, OFF_GG + RANK))).then_inc(small_in, 16)
            sp.dma_start(small[:, :, 32:40], cols(w_mix_in, slice(OFF_FF, OFF_FF + FOX_H))).then_inc(raw_in[G], 16)
            sp.dma_start(w_g2[RANK:RANK + 1, :], b_gla_g).then_inc(small_in, 16)
            sp.dma_start(b_f[32:40, :], b_fox_f.rearrange("a h -> h a")).then_inc(small_in, 16)
            load(G, N_G_FOX, cols(w_mix_in, slice(OFF_FK, OFF_FK + P)))
            load(U, N_U_FOX + 1, cols(w_mix_in, slice(OFF_FV, OFF_FV + P)))
            sp.wait_ge(ff_step, 11)
            sp.dma_start(c_rows.rearrange("a h t -> h a t"), c_sb).then_inc(c_sent, 16)
            sp.wait_ge(c_sent, 16)
            sp.wait_ge(head_ones, 1)

            def load_c(head, i):
                sp.dma_start(q_head[i][64:65, :], c_rows[0, head, :]).then_inc(c_in, 16)
                sp.dma_start(k_head[i][65:66, :], c_rows[1, head, :]).then_inc(c_in, 16)

            for i in range(2):
                load_c(slice(i, i + 1), i)
            with sp.Fori(0, FOX_PAIRS - 1) as p:
                load(U, 2 * p + (N_U_FOX + 2), cols(w_mix_in, ds(p * P + (OFF_FQ + P), P)))
                load(G, p + (N_G_FOX + 1), cols(w_mix_in, ds(p * P + (OFF_FK + P), P)))
                load_down(A, p + M_MIX, w_mix_out, p * P)
                load_down(B, p + M_MIX, w_mix_out, p * P)
                load(U, 2 * p + (N_U_FOX + 3), cols(w_mix_in, ds(p * P + (OFF_FV + P), P)))
                sp.wait_ge(gemm_done[U], 4 * p + (2 * N_U_FOX + 6))
                for i in range(2):
                    load_c(ds(2 * p + (i + 2), 1), i)
            for s in (A, B):
                load_down(s, FOX_PAIRS - 1 + M_MIX, w_mix_out, (FOX_PAIRS - 1) * P)
            with sp.Fori(0, GLA_PAIRS) as g:
                load(G, 3 * g + N_G_GLA, cols(w_mix_in, ds(g * P + OFF_GQ, P)))
                load(U, 3 * g + N_U_GLA, cols(w_mix_in, ds(g * P + OFF_GK, P)))
                for i in range(2):
                    load(G, 3 * g + (N_G_GLA + 1 + i), cols(w_mix_in, ds(g * 2 * P + (i * P + OFF_GV), P)))
                    load(U, 3 * g + (N_U_GLA + 1 + i), cols(w_mix_in, ds(g * 2 * P + (i * P + OFF_GR), P)))
                    for s in (A, B):
                        load_down(s, 2 * g + (M_GLA + i), w_mix_out, g * 2 * P + (i * P + 512))

            load(G, N_G_MEM, cols(w_mem_q, slice(0, P)))
            load(U, N_U_MEM, cols(w_mem_q, slice(P, 2 * P)))
            sp.wait_ge(down_read, 16 * (M_MEM - 1) + (RING + 1))
            sp.dma_start(mem_rows[:, :, :], mem[0].rearrange("(j p) d -> p j d", p=P)).then_inc(m_step["in"], 16)
            with sp.Fori(0, 8) as i:
                load(G, i + (N_G_MEM + 1), cols(w_mem_kv, ds(i * 2 * P, P)))
                load(U, i + (N_U_MEM + 1), cols(w_mem_kv, ds(i * 2 * P + P, P)))

            load(G, N_G_MEM + 9, cols(w_mem_q, slice(2 * P, 3 * P)))
            load(U, N_U_MEM + 9, cols(w_mem_q, slice(3 * P, 4 * P)))

            def mem_head(h, next_g, next_u):
                for i in range(2):
                    for s in (A, B):
                        load_down(s, 2 * h + (M_MEM + i), w_mem_o, h * 2 * P + i * P)
                    if i == 0 and next_g is not None:
                        load(G, h + (N_G_MEM + 10), next_g)
                        load(U, h + (N_U_MEM + 10), next_u)

            with sp.Fori(0, MEM_H - 2) as h:
                mem_head(h, cols(w_mem_q, ds(h * 2 * P + 4 * P, P)), cols(w_mem_q, ds(h * 2 * P + 5 * P, P)))
            mem_head(MEM_H - 2, cols(w_ff2_gate, ds(0, P)), cols(w_ff2_up, ds(0, P)))
            mem_head(MEM_H - 1, None, None)

            ff(2, None)

            for j in range(NT):
                for r in out_read:
                    sp.wait_ge(r, j + 1)
                sp.dma_start(out[0][j * P:(j + 1) * P, :], out_rows[:, j % 2, :]).then_inc(out_sent[j % 2], 16)
            for done in out_sent:
                sp.wait_ge(done, 16 * NT // 2)

        @block.gpsimd
        def _(pool):
            gp = nc.gpsimd

            def scale(slot, n, gain):
                pool.wait_ge(raw_in[slot], 16 * n + 16)
                w = slot3(raw_tile(slot))
                gp.tensor_tensor(w, w, gains[:, GAIN[gain], :].unsqueeze(2).to_broadcast([P, KT, P]),
                                 ALU.mult).then_inc(w_scaled[slot], 1)

            def add_pair(stage, r):
                e = sq_event(stage, 0, 2 * r)
                pool.wait_ge(sq_done, e + 2)
                gp.tensor_tensor(sq[:, e % 4, :], sq[:, e % 4, :], sq[:, e % 4 + 1, :], ALU.add).then_inc(sq_added, 1)

            def inverse_root(stage, kind, t):
                e = stat_event(stage, kind, t)
                pool.wait_ge(mean_done, e + 1)
                dst = rms8[:, 4 * t:4 * t + 4] if (stage, kind) == (4, 1) else rms4[:, 0:4]
                gp.tensor_tensor(dst, mean4[:, 0:4], minus_half[:, 0:4], ALU.pow).then_inc(pow_done, 1)

            def scale_y(stage, i):
                t, d = divmod(i, 8)
                if d == 0:
                    pool.wait_ge(rs_ready, stat_event(stage, 0, t) + 1)
                part = y[:, d, half(t)]
                gp.tensor_tensor(part, part, post_rs[:, half(t)], ALU.mult).then_inc(y_scaled, 1)

            def zero_y(stage):
                pool.wait_ge(x_ready, 16 * stage + 16)
                for d in range(KT):
                    gp.memset(y[:, d, :], 0.0).then_inc(y_zero, 1)

            def norms(stage):
                if stage > 0:
                    for r in range(6):
                        add_pair(stage, r)
                        if r == 3:
                            inverse_root(stage, 0, 0)
                for i in range(16):
                    if stage > 0:
                        scale_y(stage, i)
                        if i < 2:
                            add_pair(stage, 6 + i)
                        if i == 4:
                            inverse_root(stage, 0, 1)
                    if i == 13:
                        inverse_root(stage, 1, 0)
                inverse_root(stage, 1, 1)

            gp.memset(ident[:, :], 0.0)
            gp.memset(ones[:, :], 1.0)
            gp.memset(minus_half[:, :], -0.5)
            gp.memset(inv_d[:, 0:1], 1.0 / D)
            gp.memset(inv_d[:, 1:2], 1.0 / P)
            pool.drain()
            gp.affine_select(out=ident[:, :], in_=ident[:, :], compare_op=ALU.not_equal, fill=1.0, base=0,
                             pattern=[[-1, P]], channel_multiplier=1)
            pool.drain().then_inc(const_ready, 1)

            def ff(which):
                f = FF[which]

                def chunk(c, nxt_u, nxt_g):
                    if nxt_g:
                        scale(G, f["nG"] + c + 1, f["pre"])
                    for t in range(2):
                        pool.wait_ge(silu_done, f["s"] + 2 * c + (t + 1))
                        gp.tensor_tensor(gate_act[:, t, :], gate_act[:, t, :], rs[:, half(t)],
                                         ALU.mult).then_inc(gate_scaled, 1)
                    if nxt_u:
                        scale(U, f["nU"] + c + 1, f["pre"])

                chunk(0, True, True)
                with pool.Fori(0, (FC - 2) // 2) as i:
                    chunk(i * 2 + 1, True, True)
                    chunk(i * 2 + 2, True, True)
                chunk(FC - 1, False, False)

            pool.wait_ge(const_ready, 2)
            scale(G, 0, "ff1_pre")
            scale(U, 0, "ff1_pre")
            norms(0)
            zero_y(0)
            ff(1)

            pool.wait_ge(w_ready[G], N_G_MIX)
            gp.memset(raw_tile(G), 0.0).then_inc(small_zero, 1)
            scale(U, N_U_FOX, "mix_pre")
            pool.wait_ge(small_in, 16 * 4)
            scale(G, N_G_MIX, "mix_pre")
            norms(1)
            gp.memset(gate_low[:, :], 1.0).then_inc(g_step["consts"], 1)
            gp.memset(tri_wide[:, :], 1.0)
            gp.memset(tri_blk[:, :], 1.0 / 16)
            gp.memset(tri_suf[:, :], 1.0 / 16)
            gp.memset(ident_b[:, :], 0.0)
            gp.memset(neg_mask[:, :], 0.0)
            pool.drain()
            gp.affine_select(out=tri_wide[:, 0:P], in_=tri_wide[:, 0:P], compare_op=ALU.is_ge, fill=0.0, base=0,
                             pattern=[[1, P]], channel_multiplier=-1)
            gp.affine_select(out=tri_blk[:, :], in_=tri_blk[:, :], compare_op=ALU.is_ge, fill=0.0, base=0,
                             pattern=[[1, P]], channel_multiplier=-1)
            gp.affine_select(out=tri_suf[:, :], in_=tri_suf[:, :], compare_op=ALU.is_gt, fill=0.0, base=0,
                             pattern=[[-1, P]], channel_multiplier=1)
            gp.affine_select(out=ident_b[:, :], in_=ident_b[:, :], compare_op=ALU.not_equal, fill=1.0, base=0,
                             pattern=[[-1, P]], channel_multiplier=1)
            gp.affine_select(out=neg_mask[:, :], in_=neg_mask[:, :], compare_op=ALU.is_ge, fill=-1e30, base=0,
                             pattern=[[-1, P]], channel_multiplier=1)
            pool.drain()
            gp.memset(tri_blk[0:GLA_C, GLA_C:P], 0.0)
            gp.memset(tri_suf[GLA_C:P, 0:GLA_C], 0.0)
            pool.drain().then_inc(g_step["consts"], 1)
            scale(G, N_G_FOX, "mix_pre")
            scale(U, N_U_FOX + 1, "mix_pre")
            pool.drain()
            for i in range(2):
                gp.memset(q_head[i][64:66, :], 1.0)
                gp.memset(k_head[i][64:66, :], 1.0)
            pool.drain().then_inc(head_ones, 1)
            zero_y(1)

            def fox_root(p):
                pool.wait_ge(o_mean, p + 1)
                gp.tensor_tensor(rms4[:, :], mean4[:, :], minus_half[:, :], ALU.pow).then_inc(o_pow, 1)

            with pool.Fori(0, FOX_PAIRS - 1) as p:
                scale(U, 2 * p + (N_U_FOX + 2), "mix_pre")
                scale(G, p + (N_G_FOX + 1), "mix_pre")
                scale(U, 2 * p + (N_U_FOX + 3), "mix_pre")
                fox_root(p)
            fox_root(FOX_PAIRS - 1)
            with pool.Fori(0, GLA_PAIRS) as g:
                scale(G, 3 * g + N_G_GLA, "mix_pre")
                scale(U, 3 * g + N_U_GLA, "mix_pre")
                pool.wait_ge(g_step["kdec"], 2 * g + 2)
                plain(pool)
                gp.memset(att_t[:, :, :], 0.0).then_inc(g_step["zero"], 1)
                for i in range(2):
                    scale(G, 3 * g + (N_G_GLA + 1 + i), "mix_pre")
                    scale(U, 3 * g + (N_U_GLA + 1 + i), "mix_pre")
                    pool.wait_ge(g_step["att_read"], 8 * g + (4 * i + 4))
                    plain(pool)
                    for r in range(2):
                        pool.drain()
                        part = att_t[r * GLA_C:(r + 1) * GLA_C, :, r * GLA_C:(r + 1) * GLA_C]
                        gp.affine_select(out=part, in_=part, compare_op=ALU.is_ge, fill=0.0, base=0,
                                         pattern=[[0, NT], [1, GLA_C]],
                                         channel_multiplier=-1).then_inc(g_step["att_mask"], 1)
                    pool.drain()
                    for t in range(2):
                        pool.wait_ge(g_step["mean"], 4 * g + (2 * i + t + 1))
                        gp.tensor_tensor(rms4[:, 0:4], mean4[:, 0:4], minus_half[:, 0:4],
                                         ALU.pow).then_inc(g_step["pow"], 1)

            scale(G, N_G_MEM, "mem_pre")
            scale(U, N_U_MEM, "mem_pre")
            norms(2)
            scale(G, N_G_MEM + 1, "mem_src")
            scale(U, N_U_MEM + 1, "mem_src")
            zero_y(2)
            pool.wait_ge(m_step["mean"], 1)
            gp.tensor_tensor(mem_stat[:, 2:4], mem_stat[:, 0:2], minus_half[:, 0:2], ALU.pow).then_inc(m_step["pow"], 1)
            with pool.Fori(1, 8) as i:
                scale(G, i + (N_G_MEM + 1), "mem_src")
                scale(U, i + (N_U_MEM + 1), "mem_src")

            def mem_head(h, more):
                if more:
                    scale(G, h + (N_G_MEM + 9), "mem_pre")
                    scale(U, h + (N_U_MEM + 9), "mem_pre")
                pool.wait_ge(m_step["vrows"], 16)
                wait(pool, m_step["o"], 4 * h)
                gp.tensor_copy(mem_vh[:, :, :], mem_v[:, :, ds(h * MEM, MEM)]).then_inc(m_step["vh"], 1)

            mem_head(0, True)
            with pool.Fori(1, MEM_H - 1) as h:
                mem_head(h, True)
            mem_head(MEM_H - 1, False)

            scale(G, N_G_FF2, "ff2_pre")
            scale(U, N_U_FF2, "ff2_pre")
            norms(3)
            zero_y(3)
            ff(2)
            norms(4)

        @block.scalar
        def _(act):
            sc = nc.scalar
            gain_rows = sq[:, 0, 0:P]
            for name, src in (("ff1_pre", g_ff1_pre), ("ff1_post", g_ff1_post), ("mix_pre", g_mix_pre),
                              ("mix_post", g_mix_post), ("mem_pre", g_mem_pre), ("mem_post", g_mem_post),
                              ("ff2_pre", g_ff2_pre), ("ff2_post", g_ff2_post), ("mem_src", g_mem_src),
                              ("final", g_final.unsqueeze(0))):
                r = GAIN[name] * KT
                act.dma_start(gain_rows[r:r + KT, :], src[0].rearrange("(k p) -> k p", p=P)).then_inc(gains_in, 16)
            for i, src in enumerate((g_fox_out, g_gla_out)):
                r = (10 + i // 2) * KT + 4 * i
                act.dma_start(gain_rows[r:r + 4, :], src[0].rearrange("(k p) -> k p", p=P)).then_inc(gains_in, 16)

            def free_of(slot, n, eng):
                if slot < A:
                    wait(eng, gemm_done[slot], 2 * n)
                else:
                    wait(eng, down_done, 16 * n)

            def split_hi(slot, n, early=False):
                if slot < A:
                    act.wait_ge(w_scaled[slot], n + 1)
                else:
                    act.wait_ge(raw_in[slot], 16 * n + 16)
                if early:
                    act.wait_ge(down_done, 16 * n - 8)
                else:
                    free_of(slot, n, act)
                sc.activation(hi_tile(slot), raw_tile(slot), ACT.Copy).then_inc(w_hi_done[slot], 1)

            def square(e, src):
                wait(act, stat_done, e // 2 - 1)
                sc.activation(sq[:, e % 4, :], src, ACT.Square).then_inc(sq_done, 1)

            def y_squares(stage):
                m = LAST_M[stage]
                for i in range(16):
                    if i == 12:
                        keep_rs(stage, 0, 0)
                    act.wait_ge(down_read, 16 * m + i + 1 + RING)
                    square(sq_event(stage, 0, i), y[:, i % 8, half(i // 8)])

            def new_x(stage, i):
                t, d = divmod(i, 8)
                if stage == 0:
                    act.wait_ge(x_old, i + 1)
                    src = ps[:, 4 + i % 2, :]
                else:
                    act.wait_ge(x_new_done, 16 * (stage - 1) + i + 1)
                    src = x_new[:, i % 2, :]
                if stage < 4:
                    sc.activation(x_hi[:, d, half(t)], src, ACT.Copy).then_inc(x_hi_done, 1)
                else:
                    sc.activation(y[:, d, half(t)], src, ACT.Copy,
                                  scale=gains[:, GAIN["final"], d:d + 1]).then_inc(x_hi_done, 1)
                square(sq_event(stage, 1, i), src)

            def keep_rs(stage, kind, t):
                act.wait_ge(spread_done, stat_event(stage, kind, t) + 1)
                sc.activation((post_rs, rs)[kind][:, half(t)], ps[:, stat_bank(kind, t), :],
                              ACT.Copy).then_inc(rs_ready, 1)

            def norms(stage):
                if stage > 0:
                    y_squares(stage)
                for i in range(16):
                    new_x(stage, i)
                    if stage > 0 and i == 5:
                        keep_rs(stage, 0, 1)
                if stage < 4:
                    keep_rs(stage, 1, 0)
                if stage < 4:
                    keep_rs(stage, 1, 1)

            def ff(which):
                f = FF[which]

                def chunk(c, parity, first=False, last=False):
                    nG, nU, m = f["nG"] + c, f["nU"] + c, f["m"] + c
                    if not first:
                        split_hi(U, nU)
                    for t in range(2):
                        act.wait_ge(gemm_read[G], 2 * nG + (t + 1))
                        if not first:
                            act.wait_ge(gemm_read[U], 2 * nU + (t - 1))
                        sc.activation(gate_act[:, t, :], gate[:, t, :], ACT.Silu).then_inc(silu_done, 1)
                        if t == 0 and not first:
                            split_hi(B, m - 1)
                    if not last:
                        split_hi(G, nG + 1)
                    split_hi(A, m, early=not first)
                    for t in range(2):
                        act.wait_ge(gemm_read[U], 2 * nU + (t + 1))
                        sc.activation(h_hi[parity][:, half(t)], hidden[:, t, :], ACT.Copy).then_inc(h_hi_done, 1)

                chunk(0, 0, first=True)
                with act.Fori(0, (FC - 2) // 2) as i:
                    chunk(i * 2 + 1, 1)
                    chunk(i * 2 + 2, 0)
                chunk(FC - 1, 1, last=True)
                split_hi(B, f["m"] + FC - 1)

            split_hi(G, 0)
            split_hi(U, 0)
            norms(0)
            ff(1)
            split_hi(U, N_U_FOX)
            split_hi(G, N_G_MIX)
            norms(1)
            split_hi(G, N_G_FOX)
            row = slice(32, 40)
            act.wait_ge(ff_step, 2)
            sc.activation(forget_a[row, :], forget[row, :], ACT.Abs).then_inc(ff_step, 1)
            act.wait_ge(ff_step, 3)
            sc.activation(forget_a[row, :], forget_a[row, :], ACT.Exp, scale=-1.0).then_inc(ff_step, 1)
            act.wait_ge(ff_step, 4)
            sc.activation(forget_a[row, :], forget_a[row, :], ACT.Ln, bias=1.0).then_inc(ff_step, 1)
            split_hi(U, N_U_FOX + 1)

            def attend_fox(p, more):
                for i in range(2):
                    act.wait_ge(v_t_done, 2 * p + (i + 1))
                    sc.activation(v_rows[:, 4 * i:4 * i + 4, :].rearrange("p a b -> p (a b)"), ps[:, 4 + i, :],
                                  ACT.Copy).then_inc(v_rows_done, 1)
                splits = {8: (A, p + M_MIX), 10: (B, p + M_MIX)}
                if more:
                    splits[4] = (U, 2 * p + (N_U_FOX + 2))
                    splits[6] = (G, p + (N_G_FOX + 1))
                for a in range(19):
                    if a in splits:
                        split_hi(*splits[a])
                    hh, b = divmod(a, 8)
                    if a < 16:
                        act.wait_ge(max_done, 16 * p + (a + 1))
                        if a >= 2:
                            act.wait_ge(pt_lo, 16 * p + (a - 1))
                        if a >= 6 and (a - 2) % 8 >= 4:
                            act.wait_ge(pt_hi, 8 * p + 4 * ((a - 2) // 8) + ((a - 2) % 8 - 3))
                        L = (b + 1) * P
                        bank = 2 * (a % 2)
                        sc.activation(probs[:, a % 2, 0:L],
                                      ps[:, bank:bank + 2, :].rearrange("p a b -> p (a b)")[:, 0:L], ACT.Exp,
                                      bias=neg_max[:, b, hh:hh + 1], scale=1.0,
                                      accum_out=row_sum[:, b, hh:hh + 1]).then_inc(exp_done, 1)
                    if 1 <= a <= 16 and (a - 1) % 8 >= 4:
                        h1, b1 = divmod(a - 1, 8)
                        act.wait_ge(pt_hi, 8 * p + (4 * h1 + b1 - 3))
                        if a - 1 >= 2:
                            act.wait_ge(o_done, 16 * p + (a - 2))
                        sc.activation(probs_t[:, (a - 1) % 2, 4:b1 + 1, :].rearrange("p a b -> p (a b)"),
                                      ps[:, 5, 0:(b1 - 3) * P], ACT.Copy).then_inc(pt_hi_read, 1)
                    if a >= 3:
                        h3, b3 = divmod(a - 3, 8)
                        act.wait_ge(o_read, 16 * p + (a - 2))
                        if a > 3:
                            act.wait_ge(o_sq_done, 16 * p + (a - 3))
                        sc.activation(o_junk[:, :], o_rows[:, b3, h3, :], ACT.Square,
                                      accum_out=o_sq[:, b3, h3:h3 + 1]).then_inc(o_sq_done, 1)

            def fox_pair(p, more):
                attend_fox(p, more)
                if more:
                    split_hi(U, 2 * p + (N_U_FOX + 3))
                for t in range(2):
                    act.wait_ge(o_t, 2 * p + (t + 1))
                    act.wait_ge(down_done, 16 * p + 16 * M_MIX)
                    plain(act)
                    gain = head_gains[:, 0, ds(p, 1)] if more else head_gains[:, 0, p:p + 1]
                    sc.activation(h_hi[0][:, half(t)], ps[:, 4 + t, :], ACT.Copy, scale=gain).then_inc(h_hi_done, 1)

            with act.Fori(0, FOX_PAIRS - 1) as p:
                fox_pair(p, True)
            fox_pair(FOX_PAIRS - 1, False)

            with act.Fori(0, GLA_PAIRS) as g:
                st = g_step
                split_hi(G, 3 * g + N_G_GLA)
                split_hi(U, 3 * g + N_U_GLA)
                for i in range(2):
                    la_h = gate_a[:, half(i)]
                    act.wait_ge(st["gate"], 2 * g + (i + 1))
                    sc.activation(la_h, ps[:, 4 + i, :], ACT.Abs).then_inc(st["logsig"], 1)
                    act.wait_ge(st["logsig"], 6 * g + (3 * i + 1))
                    sc.activation(la_h, la_h, ACT.Exp, scale=-1.0).then_inc(st["logsig"], 1)
                    act.wait_ge(st["logsig"], 6 * g + (3 * i + 2))
                    sc.activation(la_h, la_h, ACT.Ln, bias=1.0).then_inc(st["logsig"], 1)
                for i in range(2):
                    act.wait_ge(st["b"], 2 * g + (i + 1))
                    sc.activation(e_b[:, half(i)], ps[:, 4 + i, :], ACT.Exp).then_inc(st["eb"], 1)
                    sc.activation(e_nb[:, half(i)], ps[:, 4 + i, :], ACT.Exp, scale=-1.0).then_inc(st["eb"], 1)
                for i in range(2):
                    act.wait_ge(st["suf"], 2 * g + (i + 1))
                    sc.activation(e_suf[:, 4 * i:4 * i + 4, :].rearrange("p a b -> p (a b)"), ps[:, 6 + i, :],
                                  ACT.Exp).then_inc(st["esuf"], 1)
                for hd in range(2):
                    split_hi(G, 3 * g + (N_G_GLA + 1 + hd))
                    split_hi(U, 3 * g + (N_U_GLA + 1 + hd))
                    for i in range(2):
                        act.wait_ge(st["vt"], 4 * g + (2 * hd + i + 1))
                        sc.activation(gv_rows[:, 4 * i:4 * i + 4, :].rearrange("p a b -> p (a b)"), ps[:, 4 + i, :],
                                      ACT.Copy).then_inc(st["vrows"], 1)
                    for t in range(2):
                        act.wait_ge(gemm_read[U], 6 * g + (2 * N_U_GLA + 2 + 2 * hd + t + 1))
                        sc.activation(r_act[:, half(t)], r_act[:, half(t)], ACT.Silu).then_inc(st["silu"], 1)
                    for t in range(2):
                        act.wait_ge(st["o"], 4 * g + (2 * hd + t + 1))
                        sc.activation(o_gla[:, half(t)], ps[:, 4 + t, :], ACT.Copy).then_inc(st["o_copy"], 1)
                        sc.activation(o_gla_sq[:, 4 * t:4 * t + 4, :].rearrange("p a b -> p (a b)"), ps[:, 4 + t, :],
                                      ACT.Square).then_inc(st["osq"], 1)
                    split_hi(A, 2 * g + (M_GLA + hd))
                    split_hi(B, 2 * g + (M_GLA + hd))
                    for t in range(2):
                        act.wait_ge(st["h"], 4 * g + (2 * hd + t + 1))
                        sc.activation(h_hi[0][:, half(t)], x_new[:, t, :], ACT.Copy).then_inc(h_hi_done, 1)

            split_hi(G, N_G_MEM)
            split_hi(U, N_U_MEM)
            norms(2)
            for s, nn in ((G, N_G_MEM), (U, N_U_MEM)):
                split_hi(s, nn + 1)
            ms = m_step
            act.wait_ge(ms["in"], 16)
            for j in range(2):
                act.wait_ge(x_ready, 16 * 3) if j == 0 else act.wait_ge(ms["sq"], 1)
                sc.activation(x_new[:, :, :].rearrange("p a b -> p (a b)"), mem_rows[:, j, :], ACT.Square,
                              accum_out=mem_stat[:, j:j + 1]).then_inc(ms["sq"], 1)
            for k in range(KT // 2):
                act.wait_ge(ms["t"], k + 1)
                sc.activation(memt_hi[:, 2 * k:2 * k + 2, :].rearrange("p a b -> p (a b)"), ps[:, 4 + k % 2, :],
                              ACT.Copy).then_inc(ms["hi"], 1)
            with act.Fori(0, 4) as i:
                for s, nn in ((G, N_G_MEM), (U, N_U_MEM)):
                    act.wait_ge(gemm_done[s], 2 * i + (2 * nn + 4))
                    plain(act)
                    for r in range(2):
                        sc.activation(mem_k[:, ds(2 * i + s, 1), r * P:(r + 1) * P], ps[:, GEMM_BANK[s], r * P:(r + 1) * P],
                                      ACT.Copy, scale=1.0 / 16).then_inc(gemm_read[s], 1)
                    split_hi(s, i + (nn + 2))
            with act.Fori(0, 4) as i:
                for s, nn in ((G, N_G_MEM), (U, N_U_MEM)):
                    split_hi(s, i + (nn + 6))
                for s, nn in ((G, N_G_MEM), (U, N_U_MEM)):
                    act.wait_ge(ms["vt"], 2 * i + (s + 1))
                    plain(act)
                    for r in range(2):
                        sc.activation(mem_v[:, r, ds(i * 2 * P + s * P, P)], ps[:, 4 + s, r * P:(r + 1) * P],
                                      ACT.Copy).then_inc(ms["vrows"], 1)

            def mem_head(h, more):
                for j in range(NT):
                    act.wait_ge(ms["max"], 8 * h + (j + 1))
                    if j >= 4:
                        act.wait_ge(ms["pt"], 2 * h + 1)
                    sc.activation(mem_p[:, j % 4, :], ps[:, j % 4, 0:MEM], ACT.Exp, bias=mem_max[:, j:j + 1],
                                  scale=1.0, accum_out=mem_sum[:, j:j + 1]).then_inc(ms["exp"], 1)
                    if j % 4 == 3:
                        t = j // 4
                        act.wait_ge(ms["pt"], 2 * h + (t + 1))
                        if t:
                            act.wait_ge(ms["o"], 4 * h + 2)
                        for blk in range(2):
                            sc.activation(mem_pt[:, blk, :], ps[:, 4 + blk, :], ACT.Copy).then_inc(ms["pt_read"], 1)
                        for c in range(2):
                            act.wait_ge(ms["o"], 4 * h + (2 * t + c + 1))
                            act.wait_ge(down_done, 32 * h + 16 * M_MEM)
                            sc.activation(h_hi[2 * c][:, half(t)], ps[:, 6 + c, :], ACT.Copy).then_inc(h_hi_done, 1)
                if more:
                    split_hi(G, h + (N_G_MEM + 10))
                    split_hi(U, h + (N_U_MEM + 10))
                for c in range(2):
                    split_hi(A, 2 * h + (M_MEM + c))
                    split_hi(B, 2 * h + (M_MEM + c))

            with act.Fori(0, MEM_H - 1) as h:
                mem_head(h, True)
            mem_head(MEM_H - 1, False)

            norms(3)
            ff(2)
            norms(4)
            act.wait_ge(pow_done, stat_event(4, 1, 1) + 1)
            for j in range(NT):
                act.wait_ge(out_t, 2 * j + 1)
                if j >= 2:
                    act.wait_ge(out_sent[j % 2], 16 * (j // 2))
                sc.activation(out_rows[:, j % 2, 0:HT], ps[:, 2 * (j % 2), :], ACT.Copy,
                              scale=rms8[:, j:j + 1]).then_inc(out_read[0], 1)

        @block.tensor
        def _(pe):
            mm = nc.tensor.matmul

            def product(acc, w, v, first, last):
                mm(acc, w[0], v[0], start=first, stop=False)
                mm(acc, w[0], v[1], start=False, stop=False)
                return mm(acc, w[1], v[0], start=False, stop=last)

            def x_tile(k, t):
                return x_hi[:, k, half(t)], x_lo[:, k, half(t)]

            def w_tile(slot, k):
                return tuple(w[:, slot, k * P:(k + 1) * P] for w in (w_hi, w_lo))

            def gemm(slot, n, t):
                if t == 0:
                    pe.wait_ge(w_ready[slot], n + 1)
                wait(pe, gemm_read[slot], 2 * n + (t - 1))
                for k in range(KT):
                    last = product(ps[:, GEMM_BANK[slot] + t, :], w_tile(slot, k), x_tile(k, t), k == 0, k == KT - 1)
                last.then_inc(gemm_done[slot], 1)

            def down_group(m, h_slot, d, t, k):
                pe.wait_ge(w_ready[A if d < 4 else B], m + 1)
                pe.wait_ge(h_ready, 2 * m + (t + 1))
                pe.wait_ge(down_read, 16 * m + (k + 1))
                w = w_hi[:, 2, d * P:(d + 1) * P], w_lo[:, 2, d * P:(d + 1) * P]
                v = h_hi[h_slot][:, half(t)], h_lo[h_slot][:, half(t)]
                product(ps[:, 4 + k % 4, :], w, v, True, True).then_inc(down_done, 1)

            def add_to_mean(stage, kind, r):
                t, q = divmod(r, 4)
                e = sq_event(stage, kind, 2 * r)
                if kind == 0:
                    pe.wait_ge(sq_added, 8 * (stage - 1) + r + 1)
                else:
                    pe.wait_ge(x_sq_added, 8 * stage + r + 1)
                for j in range(4):
                    last = mm(ps[:, stat_bank(kind, t), 4 * q + j:4 * q + j + 1], sq[:, e % 4, j * P:(j + 1) * P],
                              inv_d[:, 0:1], start=True, stop=True)
                last.then_inc(stat_done, 1)

            def spread(stage, kind, t):
                pe.wait_ge(diag_done, stat_event(stage, kind, t) + 1)
                mm(ps[:, stat_bank(kind, t), :], ones[:, :], diag[:, :], start=True, stop=True).then_inc(spread_done, 1)

            def down_all(m, h_slot, by_half, stage=None):
                for k in range(16):
                    d, t = (k % 8, k // 8) if by_half else (k // 2, k % 2)
                    down_group(m, h_slot, d, t, k)
                    if stage and k >= 9 and k % 2:
                        add_to_mean(stage, 0, (k - 9) // 2)

            def old_x(stage, i):
                t, d = divmod(i, 8)
                if i >= 2:
                    if stage == 0:
                        pe.wait_ge(x_ready, i - 1)
                    else:
                        pe.wait_ge(x_new_done, 16 * (stage - 1) + i - 1)
                bank = ps[:, 4 + i % 2, :]
                if stage == 0:
                    if d == 0:
                        pe.wait_ge(x_in[t], 16 * 4)
                    for j in range(4):
                        last = nc.tensor.transpose(bank[:, j * P:(j + 1) * P], y[:, 4 * t + j, d * P:(d + 1) * P], ident[:, :])
                    last.then_inc(x_old, 1)
                else:
                    mm(bank, ident_r[:, :], x_hi[:, d, half(t)], start=True, stop=False)
                    mm(bank, ident_r[:, :], x_lo[:, d, half(t)], start=False, stop=True).then_inc(x_old, 1)

            def norms(stage, first):
                if stage > 0:
                    pe.wait_ge(down_read, 16 * (LAST_M[stage] + 1) + RING)
                for i in range(2):
                    old_x(stage, i)
                if stage > 0:
                    spread(stage, 0, 0)
                    for r in (4, 5):
                        add_to_mean(stage, 0, r)
                for i in range(16):
                    if i + 2 < 16:
                        old_x(stage, i + 2)
                    t, k = divmod(i, 8)
                    if stage > 0 and i < 2:
                        add_to_mean(stage, 0, 6 + i)
                    if i % 2 and i >= 3:
                        add_to_mean(stage, 1, (i - 3) // 2)
                    if first:
                        pe.wait_ge(x_ready, 16 * stage + i + 1)
                    for slot, n in first:
                        if i == 0:
                            pe.wait_ge(w_ready[slot], n + 1)
                        if k == 0:
                            wait(pe, gemm_read[slot], 2 * n + (t - 1))
                            if stage > 0:
                                pe.wait_ge(rs_ready, stat_event(stage, 0, t) + 1)
                        last = product(ps[:, GEMM_BANK[slot] + t, :], w_tile(slot, k), x_tile(k, t),
                                       k == 0, k == KT - 1)
                        if k == KT - 1:
                            last.then_inc(gemm_done[slot], 1)
                    if stage > 0 and i == 4:
                        spread(stage, 0, 1)
                    if i == 15 and stage < 4:
                        spread(stage, 1, 0)
                add_to_mean(stage, 1, 7)
                if stage < 4:
                    spread(stage, 1, 1)

            def ff(which):
                f = FF[which]

                def chunk(c, parity):
                    m = f["m"] + c - 1
                    for q in range(4):
                        slot, t = (G, U)[q // 2], q % 2
                        gemm(slot, (f["nG"] if slot == G else f["nU"]) + c, t)
                        for k in range(4 * q, 4 * q + 4):
                            down_group(m, 1 - parity, k // 2, k % 2, k)

                with pe.Fori(0, (FC - 2) // 2) as i:
                    chunk(i * 2 + 1, 1)
                    chunk(i * 2 + 2, 0)
                chunk(FC - 1, 1)
                for s in (G, U):
                    pe.wait_ge(gemm_read[s], 2 * (f["nG" if s == G else "nU"] + FC))
                down_all(f["m"] + FC - 1, 1, True, 1 if which == 1 else 4)

            pe.wait_ge(const_ready, 1)
            pe.wait_ge(gains_in, 16 * 12)
            nc.tensor.transpose(ps[:, 6, 0:11 * KT], sq[0:11 * KT, 0, 0:P], ident[0:11 * KT, 0:11 * KT]).then_inc(gains_t, 1)
            pe.wait_ge(const_ready, 2)
            norms(0, [(G, 0), (U, 0)])
            ff(1)
            norms(1, [(G, N_G_MIX), (U, N_U_FOX)])

            for t in range(2):
                gemm(G, N_G_FOX, t)
            pe.wait_ge(ff_step, 6)
            for j in range(NT):
                last = nc.tensor.transpose(ps[:, 4, j * FOX_H:(j + 1) * FOX_H], forget_a[32:40, j * P:(j + 1) * P],
                                           ident[32:40, 32:40])
            last.then_inc(ff_step, 1)
            pe.wait_ge(ff_step, 8)
            pe.wait_ge(g_step["consts"], 2)
            for t in range(2):
                for j in range(4 * t + 4):
                    first_col = max(j * P - t * HT, 0)
                    skip = max(t * HT - j * P, 0)
                    last = mm(ps[0:FOX_H, 6 + t, first_col:HT], lf_rows[:, j, :],
                              tri_wide[:, skip:skip + HT - first_col], start=j == 0, stop=j == 4 * t + 3)
            last.then_inc(ff_step, 1)
            for t in range(2):
                gemm(U, N_U_FOX + 1, t)
            pe.wait_ge(ff_step, 11)

            def scores(p, a):
                hh, b = divmod(a, 8)
                if a >= 2:
                    pe.wait_ge(exp_done, 16 * p + (a - 1))
                width = (b + 1) * P
                q = q_head[hh][0:66, b * P:(b + 1) * P]
                for t in range((width + HT - 1) // HT):
                    w = min(HT, width - t * HT)
                    diagonal = (t + 1) * HT >= width
                    mm(ps[:, 2 * (a % 2) + t, 0:w], q, k_head[hh][0:66, t * HT:t * HT + w], start=True, stop=not diagonal)
                    if diagonal:
                        mm(ps[:, 2 * (a % 2) + t, w - P:w], ident_b[:, :], neg_mask[:, :], start=False,
                           stop=True).then_inc(score_done, 1)

            def transpose_probs(p, a):
                hh, b = divmod(a, 8)
                pe.wait_ge(exp_done, 16 * p + (a + 1))
                for i in range(b // 4 + 1):
                    if i == 0 and a > 0:
                        pe.wait_ge(pt_lo_read, 16 * p + a)
                    if i == 1 and (a > 4):
                        pe.wait_ge(pt_hi_read, 8 * p + (4 * hh + b - 4))
                    for j in range(4 * i, min(4 * i + 4, b + 1)):
                        last = nc.tensor.transpose(ps[:, 4 + i, (j % 4) * P:(j % 4 + 1) * P],
                                                   probs[:, a % 2, j * P:(j + 1) * P], ident[:, :])
                    last.then_inc(pt_hi if i else pt_lo, 1)

            def attend_values(p, a):
                hh, b = divmod(a, 8)
                pe.wait_ge(pt_lo_read, 16 * p + (a + 1))
                if b >= 4:
                    pe.wait_ge(pt_hi_read, 8 * p + (4 * hh + b - 3))
                if a >= 2:
                    pe.wait_ge(o_read, 16 * p + (a - 1))
                for j in range(b + 1):
                    last = mm(ps[:, 6 + a % 2, 0:FOX_D], probs_t[:, a % 2, j, :],
                              v_rows[:, j, hh * FOX_D:(hh + 1) * FOX_D], start=j == 0, stop=j == b)
                last.then_inc(o_done, 1)

            def fox_pair(p, more):
                pe.wait_ge(gemm_read[U], 4 * p + (2 * N_U_FOX + 4))
                for i in range(2):
                    for j in range(4):
                        last = nc.tensor.transpose(ps[:, 4 + i, j * P:(j + 1) * P],
                                                   v_t[:, (4 * i + j) * P:(4 * i + j + 1) * P], ident[:, :])
                    last.then_inc(v_t_done, 1)
                pe.wait_ge(c_in, 64 * p + 64)
                pe.wait_ge(gemm_read[G], 2 * p + (2 * N_G_FOX + 2))
                for a in range(18):
                    if a < 16:
                        scores(p, a)
                    if a == 1:
                        pe.wait_ge(v_rows_done, 2 * p + 2)
                    if 1 <= a <= 16:
                        transpose_probs(p, a - 1)
                    if a >= 2:
                        attend_values(p, a - 2)
                if more:
                    for t in range(2):
                        gemm(U, 2 * p + (N_U_FOX + 2), t)
                pe.wait_ge(o_norm, p + 1)
                for i in range(2):
                    for j in range(4):
                        last = nc.tensor.transpose(ps[:, 4 + i, j * P:(j + 1) * P],
                                                   o_rows[:, 4 * i + j, :, :].rearrange("p a b -> p (a b)"), ident[:, :])
                    last.then_inc(o_t, 1)
                if more:
                    for t in range(2):
                        gemm(G, p + (N_G_FOX + 1), t)
                pe.wait_ge(h_ready, 2 * p + (2 * M_MIX + 2))
                down_all(p + M_MIX, 0, True)
                if more:
                    for t in range(2):
                        gemm(U, 2 * p + (N_U_FOX + 3), t)
                pe.wait_ge(down_read, 16 * p + (16 * (M_MIX + 1) + RING))

            with pe.Fori(0, FOX_PAIRS - 1) as p:
                fox_pair(p, True)
            fox_pair(FOX_PAIRS - 1, False)

            st = g_step
            with pe.Fori(0, GLA_PAIRS) as g:
                for i in range(2):
                    for j in range(4):
                        last = mm(ps[:, 4 + i, j * P:(j + 1) * P], gate_low[0:RANK + 1, (4 * i + j) * P:(4 * i + j + 1) * P],
                                  w_g2[0:RANK + 1, ds(g * P, P)], start=True, stop=True)
                    last.then_inc(st["gate"], 1)
                for slot, n in ((G, 3 * g + N_G_GLA), (U, 3 * g + N_U_GLA)):
                    for t in range(2):
                        gemm(slot, n, t)
                pe.wait_ge(st["la"], 2 * g + 2)
                for i in range(2):
                    for j in range(4):
                        last = mm(ps[:, 4 + i, j * P:(j + 1) * P], la[:, 4 * i + j, :], tri_blk[:, :], start=True, stop=True)
                    last.then_inc(st["b"], 1)
                for i in range(2):
                    mm(ps[:, 6 + i, :], tri_suf[:, :], la[:, 4 * i:4 * i + 4, :].rearrange("p a b -> p (a b)"),
                       start=True, stop=True).then_inc(st["suf"], 1)
                pe.wait_ge(st["eb"], 4 * g + 4)
                pe.wait_ge(gemm_read[U], 6 * g + (2 * N_U_GLA + 2))
                for i in range(2):
                    for j in range(4):
                        last = nc.tensor.transpose(ps[:, 4 + i, j * P:(j + 1) * P],
                                                   k_inv[:, (4 * i + j) * P:(4 * i + j + 1) * P], ident[:, :])
                    last.then_inc(st["kt"], 1)
                for hd in range(2):
                    rows = slice(hd * GLA_C, (hd + 1) * GLA_C)
                    for slot, nn in ((G, N_G_GLA), (U, N_U_GLA)):
                        for t in range(2):
                            gemm(slot, 3 * g + (nn + 1 + hd), t)
                    pe.wait_ge(gemm_read[G], 6 * g + (2 * N_G_GLA + 2 * hd + 4))
                    pe.wait_ge(st["kdec"], 2 * g + 2)
                    for i in range(2):
                        for j in range(4):
                            last = nc.tensor.transpose(ps[:, 4 + i, j * P:(j + 1) * P],
                                                       gv_t[:, (4 * i + j) * P:(4 * i + j + 1) * P], ident[:, :])
                        last.then_inc(st["vt"], 1)
                    pe.wait_ge(st["qdec"], g + 1)
                    for i in range(2):
                        for j in range(4 * i, 4 * i + 4):
                            tile = slice(j * P, (j + 1) * P)
                            last = mm(ps[:, i, (j % 4) * P:(j % 4 + 1) * P], k_inv[rows, tile], q_dec[rows, tile],
                                      start=True, stop=True)
                        last.then_inc(st["att"], 1)
                    pe.wait_ge(st["vrows"], 4 * g + (2 * hd + 2))
                    pe.wait_ge(gemm_read[U], 6 * g + (2 * N_U_GLA + 2 * hd + 4))
                    plain(pe)
                    for n in range(NC - 1):
                        r = slice((n % 2) * GLA_C, (n % 2 + 1) * GLA_C)
                        if n == 8:
                            pe.wait_ge(st["att_read"], 8 * g + (4 * hd + 4))
                            plain(pe)
                        last = mm(kv_psum(rows, n), k_dec[r, n // 2, rows],
                                  gv_rows[r, n // 2, :], start=True, stop=True)
                        if n in (7, NC - 2):
                            last.then_inc(st["kv"], 1)
                    pe.wait_ge(st["att_mask"], 4 * g + (2 * hd + 2))
                    pe.wait_ge(st["state"], 4 * g + (2 * hd + 2))
                    for j in range(NT):
                        acc = ps[:, 4 + j // 4, (j % 4) * P:(j % 4 + 1) * P]
                        mm(acc, gv_rows[:, j, :], att_t[:, j, :], start=True, stop=False)
                        for n in (2 * j, 2 * j + 1):
                            if n > 0:
                                last = mm(acc[:, (n % 2) * GLA_C:(n % 2 + 1) * GLA_C], states[rows, n, :],
                                          q_dec[rows, n * GLA_C:(n + 1) * GLA_C], start=False, stop=n % 2 == 1)
                        if j % 4 == 3:
                            last.then_inc(st["o"], 1)
                    for t in range(2):
                        pe.wait_ge(st["osq"], 4 * g + (2 * hd + t + 1))
                        for j in range(4):
                            last = mm(ps[:, 6 + t, j:j + 1], o_gla_sq[:, 4 * t + j, :], inv_d[:, 1:2], start=True, stop=True)
                        last.then_inc(st["stat"], 1)
                    for t in range(2):
                        pe.wait_ge(st["diag"], 4 * g + (2 * hd + t + 1))
                        mm(ps[:, 6 + t, :], ones[:, :], diag[:, :], start=True, stop=True).then_inc(st["spread"], 1)
                    m = 2 * g + (M_GLA + hd)
                    pe.wait_ge(h_ready, 4 * g + (2 * M_GLA + 2 * hd + 2))
                    down_all(m, 0, True)
                    pe.wait_ge(down_read, 32 * g + (16 * (M_GLA + hd + 1) + RING))

            for r in range(4):
                add_to_mean(2, 0, r)
            norms(2, [(G, N_G_MEM), (U, N_U_MEM)])

            ms = m_step
            for kk in range(KT // 2):
                if kk == 0:
                    pe.wait_ge(ms["norm"], 2)
                if kk >= 2:
                    pe.wait_ge(ms["ready"], kk - 1)
                for k in range(2):
                    for j in range(2):
                        last = nc.tensor.transpose(ps[:, 4 + kk % 2, (2 * k + j) * P:(2 * k + j + 1) * P],
                                                   mem_rows[:, j, (2 * kk + k) * P:(2 * kk + k + 1) * P], ident[:, :])
                last.then_inc(ms["t"], 1)
            pe.wait_ge(ms["ready"], 4)

            def gemm_mem(slot, n):
                pe.wait_ge(w_ready[slot], n + 1)
                pe.wait_ge(gemm_read[slot], 2 * n)
                for k in range(KT):
                    w, v, acc = w_tile(slot, k), (memt_hi[:, k, :], memt_lo[:, k, :]), ps[:, GEMM_BANK[slot], 0:MEM]
                    mm(acc, w[0], v[0], start=k == 0, stop=False)
                    a = mm(acc, w[0], v[1], start=False, stop=False)
                    b = mm(acc, w[1], v[0], start=False, stop=k == KT - 1)
                a.then_inc(gemm_done[slot], 1)
                b.then_inc(gemm_done[slot], 1)

            with pe.Fori(0, 4) as i:
                for s, nn in ((G, N_G_MEM), (U, N_U_MEM)):
                    gemm_mem(s, i + (nn + 1))
            with pe.Fori(0, 4) as i:
                for s, nn in ((G, N_G_MEM), (U, N_U_MEM)):
                    gemm_mem(s, i + (nn + 5))
                for s, nn in ((G, N_G_MEM), (U, N_U_MEM)):
                    pe.wait_ge(gemm_read[s], 2 * i + (2 * nn + 12))
                    for r in range(2):
                        last = nc.tensor.transpose(ps[:, 4 + s, r * P:(r + 1) * P], mem_vt[:, s, r * P:(r + 1) * P],
                                                   ident[:, :])
                    last.then_inc(ms["vt"], 1)
                pe.wait_ge(ms["vrows"], 4 * i + 4)

            def mem_head(h, more):
                for s, nn in ((G, N_G_MEM), (U, N_U_MEM)):
                    if isinstance(h, int) and h == 0:
                        continue
                    pe.wait_ge(gemm_read[s], 2 * h + (2 * nn + 18))
                for j in range(NT):
                    if j >= 4:
                        pe.wait_ge(ms["exp"], 8 * h + (j - 3))
                    for c in range(2):
                        last = mm(ps[:, j % 4, 0:MEM], q_mem[:, c, j * P:(j + 1) * P], mem_k[:, ds(2 * h + c, 1), :],
                                  start=c == 0, stop=c == 1)
                    last.then_inc(ms["score"], 1)
                for t in range(2):
                    pe.wait_ge(ms["scaled"], 8 * h + (4 * t + 4))
                    if t:
                        pe.wait_ge(ms["pt_read"], 4 * h + 2)
                    for blk in range(2):
                        for j in range(4):
                            last = nc.tensor.transpose(ps[:, 4 + blk, j * P:(j + 1) * P],
                                                       mem_p[:, j, blk * P:(blk + 1) * P], ident[:, :])
                    last.then_inc(ms["pt"], 1)
                    pe.wait_ge(ms["pt_read"], 4 * h + (2 * t + 2))
                    pe.wait_ge(ms["vh"], h + 1)
                    for c in range(2):
                        if t:
                            pe.wait_ge(h_ready, 4 * h + (2 * M_MEM + c + 1))
                        for blk in range(2):
                            last = mm(ps[:, 6 + c, :], mem_vh[:, blk, c * P:(c + 1) * P], mem_pt[:, blk, :],
                                      start=blk == 0, stop=blk == 1)
                        last.then_inc(ms["o"], 1)
                if more:
                    for s, nn in ((G, N_G_MEM), (U, N_U_MEM)):
                        for t in range(2):
                            pe.wait_ge(ms["exp"], 8 * h + 8)
                            gemm(s, h + (nn + 9), t)
                pe.wait_ge(h_ready, 4 * h + (2 * M_MEM + 4))
                for c in range(2):
                    down_all(2 * h + (M_MEM + c), 2 * c, True, 3 if c and not more else None)
                pe.wait_ge(down_read, 32 * h + (16 * (M_MEM + 2) + RING))

            with pe.Fori(0, MEM_H - 1) as h:
                mem_head(h, True)
            mem_head(MEM_H - 1, False)

            norms(3, [(G, N_G_FF2), (U, N_U_FF2)])
            ff(2)
            norms(4, [])
            pe.wait_ge(x_hi_done, 16 * 5)
            for j in range(NT):
                for b in range(2):
                    if j >= 2:
                        pe.wait_ge(out_read[b], j - 1)
                    for k in range(4):
                        last = nc.tensor.transpose(ps[:, 2 * (j % 2) + b, k * P:(k + 1) * P],
                                                   y[:, 4 * b + k, j * P:(j + 1) * P], ident[:, :])
                    last.then_inc(out_t, 1)

        @block.vector
        def _(dve):
            ve = nc.vector

            def split_lo(slot, n):
                dve.wait_ge(w_hi_done[slot], n + 1)
                ve.tensor_tensor(lo_tile(slot), raw_tile(slot), f32(hi_tile(slot)), ALU.subtract).then_inc(w_ready[slot], 1)

            def add_group(m, d, t, k):
                dve.wait_ge(down_done, 16 * m + (k + 1))
                ve.tensor_tensor(y[:, d, half(t)], y[:, d, half(t)], ps[:, 4 + k % 4, :], ALU.add).then_inc(down_read, 1)

            def add_all(m, by_half, stage=None):
                for k in range(16):
                    d, t = (k % 8, k // 8) if by_half else (k // 2, k % 2)
                    add_group(m, d, t, k)
                if stage:
                    mean(stage, 0, 0)
                    make_diag(stage, 0, 0)

            def mean(stage, kind, t):
                e = stat_event(stage, kind, t)
                dve.wait_ge(stat_done, 4 * e + 4)
                sums = ps[:, stat_bank(kind, t), 0:16].rearrange("p (r j) -> p j r", j=4)
                dve.drain()
                ve.tensor_reduce(out=mean4[:, 0:4], in_=sums, op=ALU.add, axis=AX.X)
                dve.drain()
                ve.tensor_scalar(mean4[:, 0:4], mean4[:, 0:4], EPS, None, ALU.add).then_inc(mean_done, 1)

            def make_diag(stage, kind, t):
                e = stat_event(stage, kind, t)
                dve.wait_ge(pow_done, e + 1)
                wait(dve, spread_done, e)
                ve.tensor_tensor(slot3(diag[:, :]), ident[:, :].unsqueeze(1).to_broadcast([P, 4, P]),
                                 rms4[:, 0:4].unsqueeze(2).to_broadcast([P, 4, P]), ALU.mult).then_inc(diag_done, 1)

            def low_x(stage, i):
                t, d = divmod(i, 8)
                src = ps[:, 4 + i % 2, :] if stage == 0 else x_new[:, i % 2, :]
                dve.wait_ge(x_hi_done, 16 * stage + i + 1)
                if stage == 0:
                    dve.wait_ge(sq_done, i + 1)
                ve.tensor_tensor(x_lo[:, d, half(t)], src, f32(x_hi[:, d, half(t)]),
                                 ALU.subtract).then_inc(x_ready, 1)

            def add_x_pair(stage, r):
                e = sq_event(stage, 1, 2 * r)
                dve.wait_ge(sq_done, e + 2)
                ve.tensor_tensor(sq[:, e % 4, :], sq[:, e % 4, :], sq[:, e % 4 + 1, :], ALU.add).then_inc(x_sq_added, 1)

            def norms(stage):
                for i in range(16):
                    t, d = divmod(i, 8)
                    if stage > 0:
                        if i >= 2:
                            dve.wait_ge(sq_done, sq_event(stage, 1, i) - 1)
                        dve.drain()
                        dve.wait_ge(y_scaled, 16 * (stage - 1) + i + 1)
                        dve.wait_ge(x_old, 16 * stage + i + 1)
                        ve.scalar_tensor_tensor(out=x_new[:, i % 2, :], in0=y[:, d, half(t)],
                                                scalar=gains[:, GAIN[POST[stage]], d:d + 1], in1=ps[:, 4 + i % 2, :],
                                                op0=ALU.mult, op1=ALU.add).then_inc(x_new_done, 1)
                        if stage < 4 and i >= 1:
                            low_x(stage, i - 1)
                        if i == 2:
                            mean(stage, 0, 1)
                        if i == 4:
                            make_diag(stage, 0, 1)
                    else:
                        low_x(stage, i)
                    if stage == 0 and i % 2:
                        add_x_pair(0, i // 2)
                    if stage > 0 and i % 2 and i >= 3:
                        add_x_pair(stage, (i - 3) // 2)
                    if i == 12:
                        mean(stage, 1, 0)
                    if i == 14 and stage < 4:
                        make_diag(stage, 1, 0)
                if 0 < stage < 4:
                    low_x(stage, 15)
                if stage > 0:
                    add_x_pair(stage, 7)
                mean(stage, 1, 1)
                if stage < 4:
                    make_diag(stage, 1, 1)

            def ff(which):
                f = FF[which]

                def chunk(c, parity, first=False, last=False):
                    nG, nU, m = f["nG"] + c, f["nU"] + c, f["m"] + c

                    def scale_gate(t):
                        wait(dve, silu_done, f["s"] + 2 * c + (t - 1))
                        dve.wait_ge(gemm_done[G], 2 * nG + (t + 1))
                        ve.tensor_tensor(gate[:, t, :], ps[:, t, :], rs[:, half(t)], ALU.mult).then_inc(gemm_read[G], 1)

                    def times_up(t):
                        dve.wait_ge(gemm_done[U], 2 * nU + (t + 1))
                        dve.wait_ge(gate_scaled, f["s"] + 2 * c + (t + 1))
                        ve.tensor_tensor(hidden[:, t, :], ps[:, 2 + t, :], gate_act[:, t, :],
                                         ALU.mult).then_inc(gemm_read[U], 1)

                    def low_hidden(t):
                        dve.wait_ge(h_hi_done, 2 * m + (t + 1))
                        ve.tensor_tensor(h_lo[parity][:, half(t)], hidden[:, t, :], f32(h_hi[parity][:, half(t)]),
                                         ALU.subtract).then_inc(h_ready, 1)

                    def add_groups(q):
                        if not first:
                            for k in range(4 * q, 4 * q + 4):
                                add_group(m - 1, k // 2, k % 2, k)

                    if first:
                        for t in range(2):
                            dve.wait_ge(rs_ready, stat_event(0 if which == 1 else 3, 1, t) + 1)
                            scale_gate(t)
                    else:
                        dve.drain()
                        scale_gate(0)
                        split_lo(U, nU)
                        add_groups(0)
                        split_lo(B, m - 1)
                        scale_gate(1)
                        add_groups(1)
                    if not last:
                        split_lo(G, nG + 1)
                    times_up(0)
                    split_lo(A, m)
                    low_hidden(0)
                    add_groups(2)
                    times_up(1)
                    low_hidden(1)
                    add_groups(3)

                chunk(0, 0, first=True)
                dve.wait_ge(y_zero, 8 * (1 if which == 1 else 4))
                with dve.Fori(0, (FC - 2) // 2) as i:
                    chunk(i * 2 + 1, 1)
                    chunk(i * 2 + 2, 0)
                chunk(FC - 1, 1, last=True)
                split_lo(B, f["m"] + FC - 1)
                dve.drain()
                add_all(f["m"] + FC - 1, True, 1 if which == 1 else 4)

            dve.sem_inc(down_read, RING)
            dve.wait_ge(const_ready, 1)
            ve.tensor_copy(ident_r[:, :], ident[:, :])
            dve.wait_ge(gains_t, 1)
            ve.tensor_copy(gains[:, :, :].rearrange("p a k -> p (a k)"), ps[:, 6, 0:11 * KT])
            dve.drain()
            for name in ("ff1_post", "ff2_post"):
                g = gains[:, GAIN[name], :]
                ve.tensor_scalar(g, g, 0.5, None, ALU.mult)
            dve.drain().then_inc(const_ready, 1)
            split_lo(G, 0)
            split_lo(U, 0)
            norms(0)
            ff(1)
            split_lo(U, N_U_FOX)
            split_lo(G, N_G_MIX)
            norms(1)

            row = slice(32, 40)
            dve.wait_ge(g_step["consts"], 1)
            for t in range(2):
                dve.wait_ge(rs_ready, stat_event(1, 1, t) + 1)
                dve.wait_ge(gemm_done[G], 2 * N_G_MIX + t + 1)
                ve.tensor_tensor(gate_low[0:RANK, half(t)], ps[0:RANK, t, :], rs[0:RANK, half(t)], ALU.mult)
                ve.tensor_tensor(forget[row, half(t)], ps[row, t, :], rs[row, half(t)], ALU.mult).then_inc(gemm_read[G], 1)
            dve.drain()
            dve.wait_ge(small_in, 16 * 4)
            for t in range(2):
                ve.tensor_scalar(forget[row, half(t)], forget[row, half(t)], b_f[row, :], None, ALU.add).then_inc(ff_step, 1)
            def fox_q(n, t):
                dve.wait_ge(gemm_done[U], 2 * n + (t + 1))
                for i in range(2):
                    r = slice(i * FOX_D, (i + 1) * FOX_D)
                    last = ve.scalar_tensor_tensor(out=q_head[i][0:FOX_D, half(t)], in0=ps[r, 2 + t, :],
                                                   scalar=FOX_D ** -0.5, in1=rs[r, half(t)], op0=ALU.mult, op1=ALU.mult)
                last.then_inc(gemm_read[U], 1)

            def fox_k(n, t):
                dve.wait_ge(gemm_done[G], 2 * n + (t + 1))
                for i in range(2):
                    r = slice(i * FOX_D, (i + 1) * FOX_D)
                    last = ve.tensor_tensor(k_head[i][0:FOX_D, half(t)], ps[r, t, :], rs[r, half(t)], ALU.mult)
                last.then_inc(gemm_read[G], 1)

            def fox_v(n, t):
                dve.wait_ge(gemm_done[U], 2 * n + (t + 1))
                ve.tensor_tensor(v_t[:, half(t)], ps[:, 2 + t, :], rs[:, half(t)], ALU.mult).then_inc(gemm_read[U], 1)

            split_lo(G, N_G_FOX)
            for t in range(2):
                fox_q(N_U_FOX, t)
            dve.wait_ge(ff_step, 5)
            ve.scalar_tensor_tensor(out=forget_a[row, :], in0=forget[row, :], scalar=0.0, in1=forget_a[row, :], op0=ALU.min,
                                    op1=ALU.subtract).then_inc(ff_step, 1)
            split_lo(U, N_U_FOX + 1)
            for t in range(2):
                fox_k(N_G_FOX, t)
            dve.wait_ge(ff_step, 7)
            ve.tensor_copy(lf_rows[:, :, :].rearrange("p a b -> p (a b)"), ps[:, 4, 0:NT * FOX_H]).then_inc(ff_step, 1)
            dve.wait_ge(ff_step, 9)
            c_psum = ps[0:FOX_H, 6:8, :].rearrange("p a b -> p (a b)")
            ve.tensor_copy(c_sb[:, 0, :], c_psum).then_inc(ff_step, 1)
            ve.tensor_scalar(c_sb[:, 1, :], c_psum, -1.0, None, ALU.mult).then_inc(ff_step, 1)
            for t in range(2):
                fox_v(N_U_FOX + 1, t)

            def attend_fox(p, more):
                splits = {10: (A, p + M_MIX), 12: (B, p + M_MIX)}
                if more:
                    splits[6] = (U, 2 * p + (N_U_FOX + 2))
                    splits[8] = (G, p + (N_G_FOX + 1))
                for a in range(19):
                    if a in splits:
                        split_lo(*splits[a])
                    if a < 16:
                        hh, b = divmod(a, 8)
                        dve.wait_ge(score_done, 16 * p + (a + 1))
                        bank = 2 * (a % 2)
                        ve.tensor_reduce(out=neg_max[:, b, hh:hh + 1],
                                         in_=ps[:, bank:bank + 2, :].rearrange("p a b -> p (a b)")[:, 0:(b + 1) * P],
                                         op=ALU.max, axis=AX.X, negate=True).then_inc(max_done, 1)
                    if a >= 3:
                        h3, b3 = divmod(a - 3, 8)
                        ve.reciprocal(row_inv[:, b3, h3:h3 + 1], row_sum[:, b3, h3:h3 + 1])
                    if 1 <= a <= 16:
                        b1 = (a - 1) % 8
                        dve.wait_ge(pt_lo, 16 * p + a)
                        if a >= 3:
                            dve.wait_ge(o_done, 16 * p + (a - 2))
                        n = min(b1 + 1, 4)
                        ve.tensor_copy(probs_t[:, (a - 1) % 2, 0:n, :].rearrange("p a b -> p (a b)"),
                                       ps[:, 4, 0:n * P]).then_inc(pt_lo_read, 1)
                    if a >= 3:
                        dve.drain()
                        dve.wait_ge(o_done, 16 * p + (a - 2))
                        ve.tensor_scalar(o_rows[:, b3, h3, :], ps[:, 6 + (a - 3) % 2, 0:FOX_D], row_inv[:, b3, h3:h3 + 1],
                                         None, ALU.mult).then_inc(o_read, 1)

            def fox_pair(p, more):
                dve.drain()
                attend_fox(p, more)
                dve.wait_ge(o_sq_done, 16 * p + 16)
                ve.tensor_scalar(mean4[:, :], o_sq[:, :, :].rearrange("p a b -> p (a b)"), 1.0 / FOX_D, EPS, ALU.mult,
                                 ALU.add).then_inc(o_mean, 1)
                dve.wait_ge(o_pow, p + 1)
                o16 = o_rows[:, :, :, :].rearrange("p a b c -> p (a b) c")
                ve.tensor_tensor(o16, o16, rms4[:, :].unsqueeze(2).to_broadcast([P, 16, FOX_D]), ALU.mult).then_inc(o_norm, 1)
                if more:
                    for t in range(2):
                        fox_q(2 * p + (N_U_FOX + 2), t)
                    split_lo(U, 2 * p + (N_U_FOX + 3))
                gain = head_gains[:, 0, ds(p, 1)] if more else head_gains[:, 0, p:p + 1]
                for t in range(2):
                    dve.wait_ge(h_hi_done, 2 * p + (2 * M_MIX + t + 1))
                    ve.scalar_tensor_tensor(out=h_lo[0][:, half(t)], in0=ps[:, 4 + t, :], scalar=gain,
                                            in1=f32(h_hi[0][:, half(t)]), op0=ALU.mult, op1=ALU.subtract).then_inc(h_ready, 1)
                if more:
                    for t in range(2):
                        fox_k(p + (N_G_FOX + 1), t)
                dve.wait_ge(y_zero, 16)
                add_all(p + M_MIX, True)
                if more:
                    for t in range(2):
                        fox_v(2 * p + (N_U_FOX + 3), t)

            with dve.Fori(0, FOX_PAIRS - 1) as p:
                fox_pair(p, True)
            fox_pair(FOX_PAIRS - 1, False)

            st = g_step
            with dve.Fori(0, GLA_PAIRS) as g:
                dve.drain()
                split_lo(G, 3 * g + N_G_GLA)
                split_lo(U, 3 * g + N_U_GLA)
                for i in range(2):
                    dve.wait_ge(st["logsig"], 6 * g + (3 * i + 3))
                    ve.scalar_tensor_tensor(out=la[:, 4 * i:4 * i + 4, :].rearrange("p a b -> p (a b)"), in0=ps[:, 4 + i, :],
                                            scalar=0.0, in1=gate_a[:, half(i)], op0=ALU.min,
                                            op1=ALU.subtract).then_inc(st["la"], 1)
                for t in range(2):
                    dve.wait_ge(gemm_done[G], 6 * g + (2 * N_G_GLA + t + 1))
                    ve.scalar_tensor_tensor(out=q_dec[:, half(t)], in0=ps[:, t, :], scalar=GLA_C ** -0.5,
                                            in1=rs[:, half(t)], op0=ALU.mult, op1=ALU.mult).then_inc(gemm_read[G], 1)
                for t in range(2):
                    dve.wait_ge(gemm_done[U], 6 * g + (2 * N_U_GLA + t + 1))
                    ve.tensor_tensor(k_inv[:, half(t)], ps[:, 2 + t, :], rs[:, half(t)], ALU.mult).then_inc(gemm_read[U], 1)
                for i in range(2):
                    dve.wait_ge(st["kt"], 2 * g + (i + 1))
                    dve.wait_ge(st["esuf"], 2 * g + (i + 1))
                    tiles = slice(4 * i, 4 * i + 4)
                    ve.tensor_tensor(k_dec[:, tiles, :].rearrange("p a b -> p (a b)"), ps[:, 4 + i, :],
                                     e_suf[:, tiles, :].rearrange("p a b -> p (a b)"), ALU.mult).then_inc(st["kdec"], 1)
                dve.drain()
                ve.tensor_tensor(k_inv[:, :], k_inv[:, :], e_nb[:, :], ALU.mult)
                ve.tensor_copy(decay[:, :], e_b[:, :].rearrange("p (n c) -> p n c", c=GLA_C)[:, :, GLA_C - 1])
                ve.tensor_tensor(q_dec[:, :], q_dec[:, :], e_b[:, :], ALU.mult)
                dve.drain().then_inc(st["qdec"], 1)
                dve.wait_ge(st["zero"], g + 1)
                for hd in range(2):
                    rows = slice(hd * GLA_C, (hd + 1) * GLA_C)
                    split_lo(G, 3 * g + (N_G_GLA + 1 + hd))
                    split_lo(U, 3 * g + (N_U_GLA + 1 + hd))
                    for dst, slot, nn in ((gv_t, G, N_G_GLA), (r_act, U, N_U_GLA)):
                        for t in range(2):
                            dve.wait_ge(gemm_done[slot], 6 * g + (2 * nn + 2 * hd + 2 + t + 1))
                            ve.tensor_tensor(dst[:, half(t)], ps[:, GEMM_BANK[slot] + t, :], rs[:, half(t)],
                                             ALU.mult).then_inc(gemm_read[slot], 1)
                    for i in range(2):
                        dve.wait_ge(st["att"], 4 * g + (2 * hd + i + 1))
                        for r in range(2):
                            rr = slice(r * GLA_C, (r + 1) * GLA_C)
                            ve.tensor_copy(att_t[rr, 4 * i:4 * i + 4, rr], slot3(ps[rr, i, :])[:, :, rr]).then_inc(st["att_read"], 1)
                    for n in range(NC - 1):
                        kv = kv_psum(rows, n)
                        if n % 8 == 0:
                            dve.wait_ge(st["kv"], 4 * g + (2 * hd + n // 8 + 1))
                            plain(dve)
                        if n == 0:
                            s_next = ve.tensor_copy(states[rows, 1, :], kv)
                        else:
                            dve.drain()
                            s_next = ve.scalar_tensor_tensor(out=states[rows, n + 1, :], in0=states[rows, n, :],
                                                             scalar=decay[rows, n:n + 1], in1=kv, op0=ALU.mult, op1=ALU.add)
                        if n in (7, NC - 2):
                            s_next.then_inc(st["state"], 1)
                    for t in range(2):
                        dve.wait_ge(st["stat"], 4 * g + (2 * hd + t + 1))
                        ve.tensor_scalar(mean4[:, 0:4], ps[:, 6 + t, 0:4], EPS, None, ALU.add).then_inc(st["mean"], 1)
                        dve.wait_ge(st["pow"], 4 * g + (2 * hd + t + 1))
                        if t:
                            dve.wait_ge(st["spread"], 4 * g + (2 * hd + 1))
                        ve.tensor_tensor(slot3(diag[:, :]), ident[:, :].unsqueeze(1).to_broadcast([P, 4, P]),
                                         rms4[:, 0:4].unsqueeze(2).to_broadcast([P, 4, P]), ALU.mult).then_inc(st["diag"], 1)
                    split_lo(A, 2 * g + (M_GLA + hd))
                    split_lo(B, 2 * g + (M_GLA + hd))
                    for t in range(2):
                        dve.wait_ge(st["spread"], 4 * g + (2 * hd + t + 1))
                        dve.wait_ge(st["o_copy"], 4 * g + (2 * hd + t + 1))
                        ve.scalar_tensor_tensor(out=x_new[:, t, :], in0=o_gla[:, half(t)],
                                                scalar=head_gains[:, 1, ds(2 * g + hd, 1)], in1=ps[:, 6 + t, :],
                                                op0=ALU.mult, op1=ALU.mult)
                        dve.drain()
                        dve.wait_ge(st["silu"], 4 * g + (2 * hd + t + 1))
                        ve.tensor_tensor(x_new[:, t, :], x_new[:, t, :], r_act[:, half(t)], ALU.mult).then_inc(st["h"], 1)
                    for t in range(2):
                        dve.wait_ge(h_hi_done, 4 * g + (2 * M_GLA + 2 * hd + t + 1))
                        ve.tensor_tensor(h_lo[0][:, half(t)], x_new[:, t, :], f32(h_hi[0][:, half(t)]),
                                         ALU.subtract).then_inc(h_ready, 1)
                    add_all(2 * g + (M_GLA + hd), True)

            split_lo(G, N_G_MEM)
            split_lo(U, N_U_MEM)
            mean(2, 0, 0)
            make_diag(2, 0, 0)
            norms(2)

            ms = m_step

            def queries(h):
                for t in range(2):
                    for c, (s, nn) in enumerate(((G, N_G_MEM), (U, N_U_MEM))):
                        n = 2 * nn + t + 1 if h is None else 2 * h + (2 * nn + 18 + t + 1)
                        dve.wait_ge(gemm_done[s], n)
                        ve.tensor_tensor(q_mem[:, c, half(t)], ps[:, GEMM_BANK[s] + t, :], rs[:, half(t)],
                                         ALU.mult).then_inc(gemm_read[s], 1)

            dve.wait_ge(rs_ready, stat_event(2, 1, 1) + 1)
            queries(None)
            for s, nn in ((G, N_G_MEM), (U, N_U_MEM)):
                split_lo(s, nn + 1)
            dve.wait_ge(ms["sq"], 2)
            ve.tensor_scalar(mem_stat[:, 0:2], mem_stat[:, 0:2], 1.0 / D, EPS, ALU.mult, ALU.add).then_inc(ms["mean"], 1)
            dve.wait_ge(ms["pow"], 1)
            for j in range(2):
                ve.tensor_scalar(mem_rows[:, j, :], mem_rows[:, j, :], mem_stat[:, 2 + j:3 + j], None,
                                 ALU.mult).then_inc(ms["norm"], 1)
            for k in range(KT // 2):
                dve.wait_ge(ms["hi"], k + 1)
                part = slice(2 * k, 2 * k + 2)
                ve.tensor_tensor(memt_lo[:, part, :].rearrange("p a b -> p (a b)"), ps[:, 4 + k % 2, :],
                                 f32(memt_hi[:, part, :].rearrange("p a b -> p (a b)")), ALU.subtract).then_inc(ms["ready"], 1)
            with dve.Fori(0, 4) as i:
                for s, nn in ((G, N_G_MEM), (U, N_U_MEM)):
                    split_lo(s, i + (nn + 2))
            with dve.Fori(0, 4) as i:
                for s, nn in ((G, N_G_MEM), (U, N_U_MEM)):
                    dve.wait_ge(gemm_done[s], 2 * i + (2 * nn + 12))
                    for r in range(2):
                        ve.tensor_copy(mem_vt[:, s, r * P:(r + 1) * P],
                                       ps[:, GEMM_BANK[s], r * P:(r + 1) * P]).then_inc(gemm_read[s], 1)
                    split_lo(s, i + (nn + 6))
                dve.wait_ge(ms["vt"], 2 * i + 2)

            def mem_head(h, more):
                def maximum(j):
                    dve.wait_ge(ms["score"], 8 * h + (j + 1))
                    ve.tensor_reduce(out=mem_max[:, j:j + 1], in_=ps[:, j % 4, 0:MEM], op=ALU.max, axis=AX.X,
                                     negate=True).then_inc(ms["max"], 1)

                def divide(j):
                    dve.wait_ge(ms["exp"], 8 * h + (j + 1))
                    ve.reciprocal(mem_inv[:, j:j + 1], mem_sum[:, j:j + 1])
                    dve.drain()
                    ve.tensor_scalar(mem_p[:, j % 4, :], mem_p[:, j % 4, :], mem_inv[:, j:j + 1], None,
                                     ALU.mult).then_inc(ms["scaled"], 1)

                dve.drain()
                for j in range(4):
                    maximum(j)
                for j in range(4):
                    divide(j)
                    maximum(j + 4)
                for j in range(4, 8):
                    if j == 4:
                        for c in range(2):
                            low(h, 0, c)
                    divide(j)
                for c in range(2):
                    low(h, 1, c)
                if more:
                    split_lo(G, h + (N_G_MEM + 10))
                    split_lo(U, h + (N_U_MEM + 10))
                    queries(h)
                for c in range(2):
                    split_lo(A, 2 * h + (M_MEM + c))
                    split_lo(B, 2 * h + (M_MEM + c))
                    dve.wait_ge(y_zero, 24)
                    add_all(2 * h + (M_MEM + c), True, 3 if c and not more else None)

            def low(h, t, c):
                dve.wait_ge(h_hi_done, 4 * h + (2 * M_MEM + 2 * t + c + 1))
                ve.tensor_tensor(h_lo[2 * c][:, half(t)], ps[:, 6 + c, :], f32(h_hi[2 * c][:, half(t)]),
                                 ALU.subtract).then_inc(h_ready, 1)

            with dve.Fori(0, MEM_H - 1) as h:
                mem_head(h, True)
            mem_head(MEM_H - 1, False)

            norms(3)
            ff(2)
            norms(4)
            dve.wait_ge(pow_done, stat_event(4, 1, 1) + 1)
            for j in range(NT):
                dve.wait_ge(out_t, 2 * j + 2)
                if j >= 2:
                    dve.wait_ge(out_sent[j % 2], 16 * (j // 2))
                ve.tensor_scalar(out_rows[:, j % 2, HT:D], ps[:, 2 * (j % 2) + 1, :], rms8[:, j:j + 1], None,
                                 ALU.mult).then_inc(out_read[1], 1)


def kernel(**inputs):
    import numpy as np
    import concourse.bacc as bacc
    from concourse.bass_utils import run_bass_kernel_spmd

    nc = bacc.Bacc("TRN2", target_bir_lowering=False, num_devices=1)
    arrays, args = {}, []
    for name in NAMES:
        a = np.ascontiguousarray(inputs[name])
        arrays["in_" + name] = a
        args.append(nc.dram_tensor("in_" + name, a.shape, mybir.dt.from_np(a.dtype), kind="ExternalInput").ap())
    args.append(nc.dram_tensor("out_x", (1, T, D), F32, kind="ExternalOutput").ap())
    build_layer(nc, *args)
    r = run_bass_kernel_spmd(nc, [arrays], core_ids=[0])
    return r.results[0]["out_x"]


NAMES = ["x", "mem", "g_ff1_pre", "w_ff1_gate", "w_ff1_up", "w_ff1_down", "g_ff1_post",
         "g_mix_pre", "w_mix_in", "b_fox_f", "w_gla_g2", "b_gla_g", "g_fox_out", "g_gla_out",
         "w_mix_out", "g_mix_post", "g_mem_pre", "g_mem_src", "w_mem_q", "w_mem_kv", "w_mem_o",
         "g_mem_post", "g_ff2_pre", "w_ff2_gate", "w_ff2_up", "w_ff2_down", "g_ff2_post", "g_final"]
```

```python
import concourse.bass as bass
from concourse import mybir
from contextlib import ExitStack

F32 = mybir.dt.float32
F32R = mybir.dt.float32r
BF16 = mybir.dt.bfloat16
ALU = mybir.AluOpType
ACT = mybir.ActivationFunctionType
AX = mybir.AxisListType
ds = bass.ds

P = 128
D = 1024
T = 1024
HT = 512
KT = D // P
NT = T // P
D_FF = 2816
FC = D_FF // P
MEM = 256
EPS = 1e-6

FOX_H, FOX_D = 8, 64
OFF_FQ, OFF_FK, OFF_FV, OFF_FF = 0, 512, 1024, 1536
OFF_GQ = OFF_FF + FOX_H
OFF_GK = OFF_GQ + 256
OFF_GV = OFF_GK + 256
OFF_GG = OFF_GV + 512
RANK = 16
OFF_GR = OFF_GG + RANK
GLA_C = 64
NC = T // GLA_C
FOX_PAIRS, GLA_PAIRS, MEM_H = FOX_H // 2, 2, 4

N_G_MIX, N_U_MIX, M_MIX = FC, FC, FC
N_G_FOX, N_U_FOX = N_G_MIX + 1, N_U_MIX
N_G_GLA, N_U_GLA, M_GLA = N_G_FOX + FOX_PAIRS, N_U_FOX + 2 * FOX_PAIRS, M_MIX + FOX_PAIRS
N_G_MEM, N_U_MEM, M_MEM = N_G_GLA + 3 * GLA_PAIRS, N_U_GLA + 3 * GLA_PAIRS, M_GLA + 2 * GLA_PAIRS
N_G_FF2, N_U_FF2, M_FF2 = N_G_MEM + 12, N_U_MEM + 12, M_MEM + 8
G, U, A, B = range(4)
RING = 4


def build_layer(nc, x, mem, g_ff1_pre, w_ff1_gate, w_ff1_up, w_ff1_down, g_ff1_post,
                g_mix_pre, w_mix_in, b_fox_f, w_gla_g2, b_gla_g, g_fox_out, g_gla_out,
                w_mix_out, g_mix_post, g_mem_pre, g_mem_src, w_mem_q, w_mem_kv, w_mem_o,
                g_mem_post, g_ff2_pre, w_ff2_gate, w_ff2_up, w_ff2_down, g_ff2_post, g_final, out):
    ctx = ExitStack()
    with ctx:
        def sb(name, shape, dt=F32, where=None):
            return (where or ctx).enter_context(nc.sbuf_tensor(name, shape, dt))

        def sem(name):
            return ctx.enter_context(nc.semaphore(name))

        x_hi = sb("x_hi", [P, KT, T], F32R)
        x_lo = sb("x_lo", [P, KT, T], F32R)
        y = sb("y", [P, KT, T])
        raw = sb("raw", [P, 3, D])
        w_hi = sb("w_hi", [P, 3, D], F32R)
        w_lo = sb("w_lo", [P, 3, D], F32R)
        h_hi, h_lo = [sb("h_hi", [P, T], F32R)], [sb("h_lo", [P, T], F32R)]
        rs = sb("rs", [P, T])
        sq = sb("sq", [P, 4, HT])
        x_new = sb("x_new", [P, 2, HT])
        post_rs = sb("post_rs", [P, T])
        diag = sb("diag", [P, HT])
        ident = sb("ident", [P, P])
        ones = sb("ones", [P, P])
        ident_r = sb("ident_r", [P, P], F32R)
        mean4 = sb("mean4", [P, 16])
        rms4 = sb("rms4", [P, 16])
        rms8 = sb("rms8", [P, NT])
        minus_half = sb("minus_half", [P, 16])
        inv_d = sb("inv_d", [P, 2])
        gains = sb("gains", [P, 11, KT])
        GAIN = {n: i for i, n in enumerate(
            ["ff1_pre", "ff1_post", "mix_pre", "mix_post", "mem_pre", "mem_post", "ff2_pre", "ff2_post",
             "final", "mem_src"])}
        head_gains = gains[:, 10, :].rearrange("p (a k) -> p a k", a=2)
        w_g2 = sb("w_g2", [32, 256])
        b_f = sb("b_f", [40, 1])
        ps = ctx.enter_context(nc.psum_tensor("ps", [P, 8, HT], F32))
        c_rows = nc.dram_tensor("c_rows", [2, FOX_H, T], F32, kind="Internal").ap()

        with ExitStack() as s:
            h_hi.append(sb("h_hi_ff", [P, T], F32R, where=s))
            h_lo.append(sb("h_lo_ff", [P, T], F32R, where=s))
            gate = sb("gate", [P, 2, HT], where=s)
            gate_act = sb("gate_act", [P, 2, HT], where=s)
            hidden = sb("hidden", [P, 2, HT], where=s)
            out_rows = sb("out_rows", [P, 2, D], where=s)
        with ExitStack() as s:
            gate_low = sb("gate_low", [32, T], where=s)
            tri_blk = sb("tri_blk", [P, P], where=s)
            tri_suf = sb("tri_suf", [P, P], where=s)
            ident_b = sb("ident_b", [P, P], BF16, where=s)
            neg_mask = sb("neg_mask", [P, P], BF16, where=s)
            with ExitStack() as f:
                q_head = [sb(f"q_head{i}", [66, T], where=f) for i in range(2)]
                k_head = [sb(f"k_head{i}", [66, T], where=f) for i in range(2)]
                v_rows = sb("v_rows", [P, NT, P], where=f)
                probs = sb("probs", [P, 2, T], where=f)
                v_t = probs[:, 0, :]
                probs_t = sb("probs_t", [P, 2, NT, P], where=f)
                o_rows = x_new[:, :, :].rearrange("p a (t i d) -> p (a t) i d", i=2, d=FOX_D)
                row_sum = sb("row_sum", [P, NT, 2], where=f)
                row_inv = sb("row_inv", [P, NT, 2], where=f)
                neg_max = sb("neg_max", [P, NT, 2], where=f)
                o_sq = sb("o_sq", [P, NT, 2], where=f)
                o_junk = sb("o_junk", [P, FOX_D], where=f)
                lf_rows = sb("lf_rows", [P, NT, FOX_H], where=f)
                tri = v_rows[:, 0, :]
                forget = probs_t[0:40, 0, :, :].rearrange("p a b -> p (a b)")
                forget_a = probs_t[0:40, 1, :, :].rearrange("p a b -> p (a b)")
                c_sb = sq[0:FOX_H, :, :].rearrange("p (s a) t -> p s (a t)", s=2)
            with ExitStack() as f:
                la = sb("la", [P, NT, P], where=f)
                e_b = sb("e_b", [P, T], where=f)
                e_nb = sb("e_nb", [P, T], where=f)
                o_gla = sb("o_gla", [P, T], where=f)
                e_suf = sb("e_suf", [P, NT, P], where=f)
                q_dec = sb("q_dec", [P, T], where=f)
                k_inv = sb("k_inv", [P, T], where=f)
                k_dec = sb("k_dec", [P, NT, P], where=f)
                gv_rows = sb("gv_rows", [P, NT, P], where=f)
                states = sq[:, :, :].rearrange("p a (n c) -> p (a n) c", c=P)
                decay = sb("decay", [P, NC], where=f)
                gate_a = e_nb
                gla_diag = (diag[:, :], post_rs[:, 0:HT])
                gv_t = e_nb
                o_gla_sq = e_nb
                att_t = e_suf
                r_act = e_b
        with ExitStack() as s:
            mem_k = sb("mem_k", [P, KT, MEM], where=s)
            mem_v = sb("mem_v", [P, 2, D], where=s)
            q_mem = sb("q_mem", [P, 2, T], where=s)
            mem_stat = sb("mem_stat", [P, 4], where=s)
            with ExitStack() as f:
                mem_rows = mem_v
                memt_hi = sb("memt_hi", [P, KT, MEM], F32R, where=f)
                memt_lo = sb("memt_lo", [P, KT, MEM], F32R, where=f)
                mem_vt = x_new[:, :, 0:MEM]
            with ExitStack() as f:
                h_hi.append(sb("h_hi_mem", [P, T], F32R, where=f))
                h_lo.append(sb("h_lo_mem", [P, T], F32R, where=f))
                mem_vh = sb("mem_vh", [P, 2, MEM], where=f)
                mem_p = sq[:, :, :].rearrange("p a (b c) -> p (a b) c", c=MEM)
                mem_pt = sb("mem_pt", [P, 2, HT], where=f)
                mem_max = sb("mem_max", [P, NT], where=f)
                mem_sum = sb("mem_sum", [P, NT], where=f)
                mem_inv = sb("mem_inv", [P, NT], where=f)

        const_ready = sem("const_ready")
        passed = sem("passed")
        gain_in, gains_in = sem("gain_in"), sem("gains_in")
        gains_t = sem("gains_t")
        x_in = [sem("x_in_0"), sem("x_in_1")]
        raw_in = [sem(f"raw_in_{s}") for s in "guab"]
        small_in = sem("small_in")
        small_zero = sem("small_zero")
        w_scaled = [sem(f"w_scaled_{s}") for s in "gu"]
        w_hi_done = [sem(f"w_hi_done_{s}") for s in "guab"]
        w_ready = [sem(f"w_ready_{s}") for s in "guab"]
        gemm_done = [sem("gemm_done_g"), sem("gemm_done_u")]
        gemm_read = [sem("gemm_read_g"), sem("gemm_read_u")]
        down_done = sem("down_done")
        down_read = sem("down_read")
        silu_done = sem("silu_done")
        gate_scaled = sem("gate_scaled")
        h_hi_done = sem("h_hi_done")
        h_ready = sem("h_ready")
        y_zero = sem("y_zero")
        sq_done, sq_added, x_sq_added = sem("sq_done"), sem("sq_added"), sem("x_sq_added")
        stat_done, mean_done = sem("stat_done"), sem("mean_done")
        pow_done, diag_done, spread_done = sem("pow_done"), sem("diag_done"), sem("spread_done")
        rs_ready, y_scaled = sem("rs_ready"), sem("y_scaled")
        x_old = sem("x_old")
        x_new_done, x_hi_done, x_ready = sem("x_new_done"), sem("x_hi_done"), sem("x_ready")
        out_t = sem("out_t")
        out_sent = [sem("out_sent_even"), sem("out_sent_odd")]
        out_read = [sem("out_read_act"), sem("out_read_dve")]
        f_step = {n: sem("forget_" + n) for n in (
            "biased", "abs", "exp", "ln", "log_f", "log_f_t", "log_f_rows", "tile_sums", "c")}
        c_sent = sem("c_sent")
        c_in = sem("c_in")
        head_ones = sem("head_ones")
        v_t_done, v_rows_done = sem("v_t_done"), sem("v_rows_done")
        score_done, max_done, exp_done = sem("score_done"), sem("max_done"), sem("exp_done")
        pt_lo, pt_hi, pt_lo_read, pt_hi_read = sem("pt_lo"), sem("pt_hi"), sem("pt_lo_read"), sem("pt_hi_read")
        o_done, o_read, o_sq_done = sem("o_done"), sem("o_read"), sem("o_sq_done")
        o_mean, o_pow, o_norm, o_t = sem("o_mean"), sem("o_pow"), sem("o_norm"), sem("o_t")
        g_step = {n: sem("gla_" + n) for n in (
            "consts", "gate", "logsig", "la", "b", "suf", "eb", "esuf", "kt", "kdec",
            "vt", "vrows", "att", "att_read", "att_mask", "kv", "state", "o", "o_copy", "osq", "stat",
            "mean", "pow", "diag", "spread", "silu", "h", "qdec", "zero")}
        m_step = {n: sem("mem_" + n) for n in (
            "in", "sq", "mean", "pow", "norm", "t", "hi", "ready", "vt", "vrows", "vh",
            "score", "max", "exp", "scaled", "pt", "pt_read", "o")}

        GEMM_BANK = {G: 0, U: 2}

        def wait(eng, semaphore, value):
            if not (isinstance(value, int) and value <= 0):
                eng.wait_ge(semaphore, value)

        def plain(eng):
            eng.sem_inc(passed, 1)

        def raw_tile(slot):
            return raw[:, slot, :] if slot < 2 else raw[:, 2, (slot - A) * HT:(slot - A + 1) * HT]

        def hi_tile(slot):
            return w_hi[:, slot, :] if slot < 2 else w_hi[:, 2, (slot - A) * HT:(slot - A + 1) * HT]

        def lo_tile(slot):
            return w_lo[:, slot, :] if slot < 2 else w_lo[:, 2, (slot - A) * HT:(slot - A + 1) * HT]

        def f32(ap):
            return ap.bitcast(F32)

        def half(t):
            return slice(t * HT, (t + 1) * HT)

        def stat_event(stage, kind, t):
            return t if stage == 0 else 2 + 4 * (stage - 1) + 2 * kind + t

        def stat_bank(kind, t):
            return t if kind == 0 else 6 + t

        def kv_psum(rows, n):
            c = n // 2 % 4
            return ps[rows, (6 if n < 8 else 0) + n % 2, c * P:(c + 1) * P]

        def sq_event(stage, kind, i):
            return 8 * stat_event(stage, kind, 0) + i

        MEM_UNSCALED = 8
        FF = {1: dict(nG=0, nU=0, m=0, s=0, unscaled=0, pre="ff1_pre", gate=w_ff1_gate, up=w_ff1_up, down=w_ff1_down),
              2: dict(nG=N_G_FF2, nU=N_U_FF2, m=M_FF2, s=2 * FC, unscaled=MEM_UNSCALED, pre="ff2_pre",
                      gate=w_ff2_gate, up=w_ff2_up, down=w_ff2_down)}
        POST = {1: "ff1_post", 2: "mix_post", 3: "mem_post", 4: "ff2_post"}
        LAST_M = {1: FC - 1, 2: M_MEM - 1, 3: M_FF2 - 1, 4: M_FF2 + FC - 1}

        def cols(w, c0):
            return w[0].rearrange("(k p) n -> p k n", p=P)[:, :, c0]

        def slot3(ap):
            return ap.rearrange("p (k c) -> p k c", c=P)

        block = ctx.enter_context(nc.Block())

        @block.sync
        def _(sp):
            def load(slot, n, src):
                wait(sp, w_ready[slot], n)
                dst = raw_tile(slot) if slot >= A else slot3(raw_tile(slot))
                sp.dma_start(dst, src).then_inc(raw_in[slot], 16)

            def load_down(slot, m, w, row0):
                load(slot, m, w[0][ds(row0, P), (slot - A) * HT:(slot - A + 1) * HT])

            load(G, 0, cols(w_ff1_gate, ds(0, P)))
            load(U, 0, cols(w_ff1_up, ds(0, P)))
            for j in range(NT):
                sp.dma_start(y[:, j, :], x[0][j * P:(j + 1) * P, :]).then_inc(x_in[j // 4], 16)

            def load_gains():
                gain_rows = sq[:, 0, 0:P]
                sp.wait_ge(stat_done, 8)
                for name, src in (("ff1_pre", g_ff1_pre), ("ff1_post", g_ff1_post), ("mix_pre", g_mix_pre),
                                  ("mix_post", g_mix_post), ("mem_pre", g_mem_pre), ("mem_post", g_mem_post),
                                  ("ff2_pre", g_ff2_pre), ("ff2_post", g_ff2_post), ("mem_src", g_mem_src),
                                  ("final", g_final.unsqueeze(0))):
                    r = GAIN[name] * KT
                    sp.dma_start(gain_rows[r:r + KT, :], src[0].rearrange("(k p) -> k p", p=P)).then_inc(gains_in, 16)
                for i, src in enumerate((g_fox_out, g_gla_out)):
                    r = (10 + i // 2) * KT + 4 * i
                    sp.dma_start(gain_rows[r:r + 4, :], src[0].rearrange("(k p) -> k p", p=P)).then_inc(gains_in, 16)

            def ff(which):
                f = FF[which]

                def chunk(c, after_g):
                    if not (isinstance(c, int) and c == FC - 1):
                        load(U, f["nU"] + c + 1, cols(f["up"], ds((c + 1) * P, P)))
                    load_down(B, f["m"] + c, f["down"], c * P)
                    if after_g:
                        load(G, f["nG"] + c + 2, cols(f["gate"], ds((c + 2) * P, P)))
                    if not (isinstance(c, int) and c == FC - 1):
                        load_down(A, f["m"] + c + 1, f["down"], (c + 1) * P)

                load_down(A, f["m"], f["down"], 0)
                load(G, f["nG"] + 1, cols(f["gate"], ds(P, P)))
                chunk(0, True)
                if which == 1:
                    load_gains()
                with sp.Fori(0, (FC - 4) // 2) as i:
                    chunk(i * 2 + 1, True)
                    chunk(i * 2 + 2, True)
                chunk(FC - 3, True)
                chunk(FC - 2, False)
                chunk(FC - 1, False)

            ff(1)
            load(U, N_U_FOX, cols(w_mix_in, slice(OFF_FQ, OFF_FQ + P)))
            sp.dma_start(w_g2[0:RANK, :], w_gla_g2[0]).then_inc(small_in, 16)
            wait(sp, w_ready[G], N_G_MIX)
            sp.wait_ge(small_zero, 1)
            small = slot3(raw_tile(G))
            sp.dma_start(small[:, :, 0:RANK], cols(w_mix_in, slice(OFF_GG, OFF_GG + RANK))).then_inc(small_in, 16)
            sp.dma_start(small[:, :, 32:40], cols(w_mix_in, slice(OFF_FF, OFF_FF + FOX_H))).then_inc(raw_in[G], 16)
            sp.dma_start(w_g2[RANK:RANK + 1, :], b_gla_g).then_inc(small_in, 16)
            sp.dma_start(b_f[32:40, :], b_fox_f.rearrange("a h -> h a")).then_inc(small_in, 16)
            load(G, N_G_FOX, cols(w_mix_in, slice(OFF_FK, OFF_FK + P)))
            load(U, N_U_FOX + 1, cols(w_mix_in, slice(OFF_FV, OFF_FV + P)))
            sp.wait_ge(f_step["c"], 1)
            sp.dma_start(c_rows.rearrange("a h t -> h a t"), c_sb).then_inc(c_sent, 16)
            sp.wait_ge(c_sent, 16)
            sp.wait_ge(head_ones, 1)

            def load_c(head, i):
                sp.dma_start(q_head[i][64:65, :], c_rows[0, head, :]).then_inc(c_in, 16)
                sp.dma_start(k_head[i][65:66, :], c_rows[1, head, :]).then_inc(c_in, 16)

            for i in range(2):
                load_c(slice(i, i + 1), i)
            with sp.Fori(0, FOX_PAIRS - 1) as p:
                load(U, 2 * p + (N_U_FOX + 2), cols(w_mix_in, ds(p * P + (OFF_FQ + P), P)))
                load(G, p + (N_G_FOX + 1), cols(w_mix_in, ds(p * P + (OFF_FK + P), P)))
                load_down(A, p + M_MIX, w_mix_out, p * P)
                load_down(B, p + M_MIX, w_mix_out, p * P)
                load(U, 2 * p + (N_U_FOX + 3), cols(w_mix_in, ds(p * P + (OFF_FV + P), P)))
                sp.wait_ge(gemm_done[U], 4 * p + (2 * N_U_FOX + 6))
                for i in range(2):
                    load_c(ds(2 * p + (i + 2), 1), i)
            load(U, N_U_GLA, cols(w_mix_in, slice(OFF_GK, OFF_GK + P)))
            load(G, N_G_GLA, cols(w_mix_in, slice(OFF_GQ, OFF_GQ + P)))
            for s in (A, B):
                load_down(s, FOX_PAIRS - 1 + M_MIX, w_mix_out, (FOX_PAIRS - 1) * P)
            for g in range(GLA_PAIRS):
                for hd in range(2):
                    i = 2 * g + hd
                    load(G, N_G_GLA + 3 * g + 1 + hd, cols(w_mix_in, slice(OFF_GV + i * P, OFF_GV + (i + 1) * P)))
                    load(U, N_U_GLA + 3 * g + 1 + hd, cols(w_mix_in, slice(OFF_GR + i * P, OFF_GR + (i + 1) * P)))
                    for s in (A, B):
                        load_down(s, M_GLA + i, w_mix_out, i * P + FOX_H * FOX_D)
                if g + 1 < GLA_PAIRS:
                    c = (g + 1) * P
                    load(G, N_G_GLA + 3 * g + 3, cols(w_mix_in, slice(OFF_GQ + c, OFF_GQ + c + P)))
                    load(U, N_U_GLA + 3 * g + 3, cols(w_mix_in, slice(OFF_GK + c, OFF_GK + c + P)))

            load(G, N_G_MEM, cols(w_mem_q, slice(0, P)))
            load(U, N_U_MEM, cols(w_mem_q, slice(P, 2 * P)))
            sp.wait_ge(down_read, 16 * (M_MEM - 1) + (RING + 1))
            sp.dma_start(mem_rows[:, :, :], mem[0].rearrange("(j p) d -> p j d", p=P)).then_inc(m_step["in"], 16)
            with sp.Fori(0, 8) as i:
                load(G, i + (N_G_MEM + 1), cols(w_mem_kv, ds(i * 2 * P, P)))
                load(U, i + (N_U_MEM + 1), cols(w_mem_kv, ds(i * 2 * P + P, P)))

            load(G, N_G_MEM + 9, cols(w_mem_q, slice(2 * P, 3 * P)))
            load(U, N_U_MEM + 9, cols(w_mem_q, slice(3 * P, 4 * P)))

            def mem_head(h, next_g, next_u):
                for i in range(2):
                    for s in (A, B):
                        load_down(s, 2 * h + (M_MEM + i), w_mem_o, h * 2 * P + i * P)
                    if i == 0 and next_g is not None:
                        load(G, h + (N_G_MEM + 10), next_g)
                        load(U, h + (N_U_MEM + 10), next_u)

            with sp.Fori(0, MEM_H - 2) as h:
                mem_head(h, cols(w_mem_q, ds(h * 2 * P + 4 * P, P)), cols(w_mem_q, ds(h * 2 * P + 5 * P, P)))
            mem_head(MEM_H - 2, cols(w_ff2_gate, ds(0, P)), cols(w_ff2_up, ds(0, P)))
            mem_head(MEM_H - 1, None, None)

            ff(2)

            for j in range(NT):
                for r in out_read:
                    sp.wait_ge(r, j + 1)
                sp.dma_start(out[0][j * P:(j + 1) * P, :], out_rows[:, j % 2, :]).then_inc(out_sent[j % 2], 16)
            for done in out_sent:
                sp.wait_ge(done, 16 * NT // 2)

        @block.gpsimd
        def _(pool):
            gp = nc.gpsimd

            def scale(slot, n, gain):
                pool.wait_ge(raw_in[slot], 16 * n + 16)
                w = slot3(raw_tile(slot))
                gp.tensor_tensor(w, w, gains[:, GAIN[gain], :].unsqueeze(2).to_broadcast([P, KT, P]),
                                 ALU.mult).then_inc(w_scaled[slot], 1)

            def add_pair(stage, r):
                e = sq_event(stage, 0, 2 * r)
                pool.wait_ge(sq_done, e + 2)
                gp.tensor_tensor(sq[:, e % 4, :], sq[:, e % 4, :], sq[:, e % 4 + 1, :], ALU.add).then_inc(sq_added, 1)

            def inverse_root(stage, kind, t):
                e = stat_event(stage, kind, t)
                pool.wait_ge(mean_done, e + 1)
                dst = rms8[:, 4 * t:4 * t + 4] if (stage, kind) == (4, 1) else rms4[:, 0:4]
                gp.tensor_tensor(dst, mean4[:, 0:4], minus_half[:, 0:4], ALU.pow).then_inc(pow_done, 1)

            def scale_y(stage, i):
                t, d = divmod(i, 8)
                if d == 0:
                    pool.wait_ge(rs_ready, stat_event(stage, 0, t) + 1)
                part = y[:, d, half(t)]
                gp.tensor_tensor(part, part, post_rs[:, half(t)], ALU.mult).then_inc(y_scaled, 1)

            def zero_y(stage):
                pool.wait_ge(x_ready, 16 * stage + 16)
                for d in range(KT):
                    gp.memset(y[:, d, :], 0.0).then_inc(y_zero, 1)

            def norms(stage, next_g):
                if stage > 0:
                    for r in range(6):
                        add_pair(stage, r)
                        if r == 3:
                            inverse_root(stage, 0, 0)
                for i in range(16):
                    if stage > 0:
                        scale_y(stage, i)
                        if i < 2:
                            add_pair(stage, 6 + i)
                        if i == 4:
                            inverse_root(stage, 0, 1)
                    if i == 12 and stage == 2:
                        pool.wait_ge(m_step["mean"], 1)
                        gp.tensor_tensor(mem_stat[:, 2:4], mem_stat[:, 0:2], minus_half[:, 0:2],
                                         ALU.pow).then_inc(m_step["pow"], 1)
                    if i == 13:
                        inverse_root(stage, 1, 0)
                if next_g:
                    scale(G, *next_g)
                inverse_root(stage, 1, 1)

            gp.memset(ident[:, :], 0.0)
            gp.memset(ones[:, :], 1.0)
            gp.memset(minus_half[:, :], -0.5)
            gp.memset(inv_d[:, 0:1], 1.0 / D)
            gp.memset(inv_d[:, 1:2], 1.0 / P)
            pool.drain()
            gp.affine_select(out=ident[:, :], in_=ident[:, :], compare_op=ALU.not_equal, fill=1.0, base=0,
                             pattern=[[-1, P]], channel_multiplier=1)
            pool.drain().then_inc(const_ready, 1)

            def ff(which):
                f = FF[which]

                def chunk(c, nxt_u, nxt_g):
                    if nxt_g:
                        scale(G, f["nG"] + c + 1, f["pre"])
                    for t in range(2):
                        pool.wait_ge(silu_done, f["s"] + 2 * c + (t + 1))
                        gp.tensor_tensor(gate_act[:, t, :], gate_act[:, t, :], rs[:, half(t)],
                                         ALU.mult).then_inc(gate_scaled, 1)
                    if nxt_u:
                        scale(U, f["nU"] + c + 1, f["pre"])

                chunk(0, True, False)
                with pool.Fori(0, (FC - 2) // 2) as i:
                    chunk(i * 2 + 1, True, True)
                    chunk(i * 2 + 2, True, True)
                chunk(FC - 1, False, False)

            pool.wait_ge(const_ready, 2)
            scale(G, 0, "ff1_pre")
            scale(U, 0, "ff1_pre")
            norms(0, (1, "ff1_pre"))
            zero_y(0)
            ff(1)

            pool.wait_ge(w_ready[G], N_G_MIX)
            gp.memset(raw_tile(G), 0.0).then_inc(small_zero, 1)
            pool.wait_ge(const_ready, 3)
            scale(U, N_U_FOX, "mix_pre")
            pool.wait_ge(small_in, 16 * 4)
            scale(G, N_G_MIX, "mix_pre")
            norms(1, (N_G_FOX, "mix_pre"))
            gp.memset(gate_low[:, :], 1.0).then_inc(g_step["consts"], 1)
            gp.memset(tri, 1.0)
            gp.memset(tri_blk[:, :], 1.0 / 16)
            gp.memset(tri_suf[:, :], 1.0 / 16)
            gp.memset(ident_b[:, :], 0.0)
            gp.memset(neg_mask[:, :], 0.0)
            pool.drain()
            gp.affine_select(out=tri, in_=tri, compare_op=ALU.is_ge, fill=0.0, base=0,
                             pattern=[[1, P]], channel_multiplier=-1)
            gp.affine_select(out=tri_blk[:, :], in_=tri_blk[:, :], compare_op=ALU.is_ge, fill=0.0, base=0,
                             pattern=[[1, P]], channel_multiplier=-1)
            gp.affine_select(out=tri_suf[:, :], in_=tri_suf[:, :], compare_op=ALU.is_gt, fill=0.0, base=0,
                             pattern=[[-1, P]], channel_multiplier=1)
            gp.affine_select(out=ident_b[:, :], in_=ident_b[:, :], compare_op=ALU.not_equal, fill=1.0, base=0,
                             pattern=[[-1, P]], channel_multiplier=1)
            gp.affine_select(out=neg_mask[:, :], in_=neg_mask[:, :], compare_op=ALU.is_ge, fill=-1e30, base=0,
                             pattern=[[-1, P]], channel_multiplier=1)
            pool.drain()
            gp.memset(tri_blk[0:GLA_C, GLA_C:P], 0.0)
            gp.memset(tri_suf[GLA_C:P, 0:GLA_C], 0.0)
            pool.drain().then_inc(g_step["consts"], 1)
            scale(U, N_U_FOX + 1, "mix_pre")
            pool.drain()
            for i in range(2):
                gp.memset(q_head[i][64:66, :], 1.0)
                gp.memset(k_head[i][64:66, :], 1.0)
            pool.drain().then_inc(head_ones, 1)
            zero_y(1)

            def fox_root(p):
                pool.wait_ge(o_mean, p + 1)
                gp.tensor_tensor(rms4[:, :], mean4[:, :], minus_half[:, :], ALU.pow).then_inc(o_pow, 1)

            with pool.Fori(0, FOX_PAIRS - 1) as p:
                scale(U, 2 * p + (N_U_FOX + 2), "mix_pre")
                scale(G, p + (N_G_FOX + 1), "mix_pre")
                scale(U, 2 * p + (N_U_FOX + 3), "mix_pre")
                fox_root(p)
            scale(U, N_U_GLA, "mix_pre")
            scale(G, N_G_GLA, "mix_pre")
            fox_root(FOX_PAIRS - 1)
            for g in range(GLA_PAIRS):
                scale(G, N_G_GLA + 3 * g + 1, "mix_pre")
                scale(U, N_U_GLA + 3 * g + 1, "mix_pre")
                for hd in range(2):
                    if hd == 0:
                        pool.wait_ge(g_step["kdec"], 2 * g + 2)
                        gp.memset(att_t[:, :, :], 0.0).then_inc(g_step["zero"], 1)
                    pool.wait_ge(g_step["att_read"], 8 * g + 4 * hd + 4)
                    for r in range(2):
                        pool.drain()
                        part = att_t[r * GLA_C:(r + 1) * GLA_C, :, r * GLA_C:(r + 1) * GLA_C]
                        gp.affine_select(out=part, in_=part, compare_op=ALU.is_ge, fill=0.0, base=0,
                                         pattern=[[0, NT], [1, GLA_C]],
                                         channel_multiplier=-1).then_inc(g_step["att_mask"], 1)
                    pool.drain()
                    if hd == 0 or g + 1 < GLA_PAIRS:
                        scale(G, N_G_GLA + 3 * g + 2 + hd, "mix_pre")
                        scale(U, N_U_GLA + 3 * g + 2 + hd, "mix_pre")
                    for t in range(2):
                        pool.wait_ge(g_step["mean"], 4 * g + 2 * hd + t + 1)
                        part = slice(4 * t, 4 * t + 4)
                        gp.tensor_tensor(rms4[:, part], mean4[:, part], minus_half[:, part],
                                         ALU.pow).then_inc(g_step["pow"], 1)

            scale(G, N_G_MEM, "mem_pre")
            scale(U, N_U_MEM, "mem_pre")
            norms(2, None)
            zero_y(2)

            def mem_head(h, more):
                gain = "mem_pre" if more else "ff2_pre"
                scale(G, h + (N_G_MEM + 9), gain)
                scale(U, h + (N_U_MEM + 9), gain)
                pool.wait_ge(m_step["vrows"], 16 + 4)
                wait(pool, m_step["o"], 4 * h)
                gp.tensor_copy(mem_vh[:, :, :], mem_v[:, :, ds(h * MEM, MEM)]).then_inc(m_step["vh"], 1)

            mem_head(0, True)
            with pool.Fori(1, MEM_H - 1) as h:
                mem_head(h, True)
            mem_head(MEM_H - 1, False)

            norms(3, (N_G_FF2 + 1, "ff2_pre"))
            zero_y(3)
            ff(2)
            norms(4, None)

        @block.scalar
        def _(act):
            sc = nc.scalar
            act.dma_start(sq[0:KT, 0, 0:P], g_ff1_pre[0].rearrange("(k p) -> k p", p=P)).then_inc(gain_in, 16)

            def free_of(slot, n, eng):
                if slot < A:
                    wait(eng, gemm_done[slot], 2 * n)
                else:
                    wait(eng, down_done, 16 * n)

            def split_hi(slot, n, early=False, unscaled=0):
                if slot < A and unscaled is not None:
                    act.wait_ge(w_scaled[slot], n + (1 - unscaled))
                else:
                    act.wait_ge(raw_in[slot], 16 * n + 16)
                if early:
                    act.wait_ge(down_done, 16 * n - 8)
                else:
                    free_of(slot, n, act)
                sc.activation(hi_tile(slot), raw_tile(slot), ACT.Copy).then_inc(w_hi_done[slot], 1)

            def square(e, src):
                wait(act, stat_done, e // 2 - 1)
                sc.activation(sq[:, e % 4, :], src, ACT.Square).then_inc(sq_done, 1)

            def y_squares(stage):
                m = LAST_M[stage]
                if stage == 1:
                    act.wait_ge(gains_t, 2)
                for i in range(16):
                    if i == 12:
                        keep_rs(stage, 0, 0)
                    act.wait_ge(down_read, 16 * m + i + 1 + RING)
                    square(sq_event(stage, 0, i), y[:, i % 8, half(i // 8)])

            def new_x(stage, i):
                t, d = divmod(i, 8)
                if stage == 0:
                    act.wait_ge(x_old, i + 1)
                    src = ps[:, 4 + i % 2, :]
                else:
                    act.wait_ge(x_new_done, 16 * (stage - 1) + i + 1)
                    src = x_new[:, i % 2, :]
                if stage < 4:
                    sc.activation(x_hi[:, d, half(t)], src, ACT.Copy).then_inc(x_hi_done, 1)
                else:
                    sc.activation(y[:, d, half(t)], src, ACT.Copy,
                                  scale=gains[:, GAIN["final"], d:d + 1]).then_inc(x_hi_done, 1)
                square(sq_event(stage, 1, i), src)

            def keep_rs(stage, kind, t):
                act.wait_ge(spread_done, stat_event(stage, kind, t) + 1)
                sc.activation((post_rs, rs)[kind][:, half(t)], ps[:, stat_bank(kind, t), :],
                              ACT.Copy).then_inc(rs_ready, 1)

            def write_out(j):
                act.wait_ge(pow_done, stat_event(4, 1, j // 4) + 1)
                act.wait_ge(out_t, 2 * j + 1)
                if j >= 2:
                    act.wait_ge(out_sent[j % 2], 16 * (j // 2))
                sc.activation(out_rows[:, j % 2, 0:HT], ps[:, 2 * (j % 2), :], ACT.Copy,
                              scale=rms8[:, j:j + 1]).then_inc(out_read[0], 1)

            def high_mem(k):
                act.wait_ge(m_step["t"], k // 2 + 1)
                sc.activation(memt_hi[:, k, :], ps[:, 4 + k // 2 % 2, (k % 2) * MEM:(k % 2 + 1) * MEM], ACT.Copy,
                              scale=gains[:, GAIN["mem_src"], k:k + 1]).then_inc(m_step["hi"], 1)

            def norms(stage, next_g, unscaled=0):
                if stage > 0:
                    y_squares(stage)
                for i in range(16):
                    new_x(stage, i)
                    if stage == 4 and i >= 13:
                        write_out(i - 13)
                    if stage == 2 and i in (6, 9):
                        j, ms = (i - 6) // 3, m_step
                        act.wait_ge(ms["in"], 16)
                        wait(act, ms["sq"], j)
                        sc.activation(mem_k[:, 0:4, :].rearrange("p a b -> p (a b)"), mem_rows[:, j, :], ACT.Square,
                                      accum_out=mem_stat[:, j:j + 1]).then_inc(ms["sq"], 1)
                    if stage == 2 and i in (14, 15):
                        act.wait_ge(m_step["pow"], 1)
                        j = i - 14
                        sc.activation(mem_rows[:, j, :], mem_rows[:, j, :], ACT.Copy,
                                      scale=mem_stat[:, 2 + j:3 + j]).then_inc(m_step["norm"], 1)
                    if stage > 0 and i == 5:
                        keep_rs(stage, 0, 1)
                if stage < 4:
                    keep_rs(stage, 1, 0)
                    split_hi(G, next_g, unscaled=unscaled)
                if stage == 2:
                    for k in range(4):
                        high_mem(k)
                if stage < 4:
                    keep_rs(stage, 1, 1)

            def ff(which):
                f = FF[which]

                def chunk(c, parity, first=False, last=False):
                    nG, nU, m = f["nG"] + c, f["nU"] + c, f["m"] + c
                    if not first:
                        split_hi(U, nU, unscaled=f["unscaled"])
                    for t in range(2):
                        act.wait_ge(gemm_read[G], 2 * nG + (t + 1))
                        if not first:
                            act.wait_ge(gemm_read[U], 2 * nU + (t - 1))
                        sc.activation(gate_act[:, t, :], gate[:, t, :], ACT.Silu).then_inc(silu_done, 1)
                        if t == 0 and not first:
                            split_hi(B, m - 1)
                    if not first and not last:
                        split_hi(G, nG + 1, unscaled=f["unscaled"])
                    split_hi(A, m, early=not first)
                    for t in range(2):
                        act.wait_ge(gemm_read[U], 2 * nU + (t + 1))
                        sc.activation(h_hi[parity][:, half(t)], hidden[:, t, :], ACT.Copy).then_inc(h_hi_done, 1)

                chunk(0, 0, first=True)
                with act.Fori(0, (FC - 2) // 2) as i:
                    chunk(i * 2 + 1, 1)
                    chunk(i * 2 + 2, 0)
                chunk(FC - 1, 1, last=True)
                split_hi(B, f["m"] + FC - 1)

            split_hi(G, 0)
            split_hi(U, 0)
            norms(0, 1)
            ff(1)
            split_hi(U, N_U_FOX)
            split_hi(G, N_G_MIX)
            norms(1, N_G_FOX)
            row = slice(32, 40)
            act.wait_ge(f_step["biased"], 2)
            sc.activation(forget_a[row, :], forget[row, :], ACT.Abs).then_inc(f_step["abs"], 1)
            act.wait_ge(f_step["abs"], 1)
            sc.activation(forget_a[row, :], forget_a[row, :], ACT.Exp, scale=-1.0).then_inc(f_step["exp"], 1)
            act.wait_ge(f_step["exp"], 1)
            sc.activation(forget_a[row, :], forget_a[row, :], ACT.Ln, bias=1.0).then_inc(f_step["ln"], 1)
            split_hi(U, N_U_FOX + 1)

            def attend_fox(p):
                for i in range(2):
                    act.wait_ge(v_t_done, 2 * p + (i + 1))
                    sc.activation(v_rows[:, 4 * i:4 * i + 4, :].rearrange("p a b -> p (a b)"), ps[:, 4 + i, :],
                                  ACT.Copy).then_inc(v_rows_done, 1)
                splits = {4: (U, 2 * p + (N_U_FOX + 2)), 6: (G, p + (N_G_FOX + 1)),
                          8: (A, p + M_MIX), 10: (B, p + M_MIX)}
                for a in range(19):
                    if a in splits:
                        split_hi(*splits[a])
                    hh, b = divmod(a, 8)
                    if a < 16:
                        act.wait_ge(max_done, 16 * p + (a + 1))
                        if a >= 2:
                            act.wait_ge(pt_lo, 16 * p + (a - 1))
                        if a >= 6 and (a - 2) % 8 >= 4:
                            act.wait_ge(pt_hi, 8 * p + 4 * ((a - 2) // 8) + ((a - 2) % 8 - 3))
                        L = (b + 1) * P
                        bank = 2 * (a % 2)
                        sc.activation(probs[:, a % 2, 0:L],
                                      ps[:, bank:bank + 2, :].rearrange("p a b -> p (a b)")[:, 0:L], ACT.Exp,
                                      bias=neg_max[:, b, hh:hh + 1], scale=1.0,
                                      accum_out=row_sum[:, b, hh:hh + 1]).then_inc(exp_done, 1)
                    if 1 <= a <= 16 and (a - 1) % 8 >= 4:
                        h1, b1 = divmod(a - 1, 8)
                        act.wait_ge(pt_hi, 8 * p + (4 * h1 + b1 - 3))
                        if a - 1 >= 2:
                            act.wait_ge(o_done, 16 * p + (a - 2))
                        sc.activation(probs_t[:, (a - 1) % 2, 4:b1 + 1, :].rearrange("p a b -> p (a b)"),
                                      ps[:, 5, 0:(b1 - 3) * P], ACT.Copy).then_inc(pt_hi_read, 1)
                    if a >= 3:
                        h3, b3 = divmod(a - 3, 8)
                        act.wait_ge(o_read, 16 * p + (a - 2))
                        if a > 3:
                            act.wait_ge(o_sq_done, 16 * p + (a - 3))
                        sc.activation(o_junk[:, :], o_rows[:, b3, h3, :], ACT.Square,
                                      accum_out=o_sq[:, b3, h3:h3 + 1]).then_inc(o_sq_done, 1)

            def log_sigmoid(g):
                for i in range(2):
                    la_h, st = gate_a[:, half(i)], g_step
                    act.wait_ge(st["gate"], 2 * g + i + 1)
                    sc.activation(la_h, ps[:, 2 + i, :], ACT.Abs).then_inc(st["logsig"], 1)
                    act.wait_ge(st["logsig"], 6 * g + 3 * i + 1)
                    sc.activation(la_h, la_h, ACT.Exp, scale=-1.0).then_inc(st["logsig"], 1)
                    act.wait_ge(st["logsig"], 6 * g + 3 * i + 2)
                    sc.activation(la_h, la_h, ACT.Ln, bias=1.0).then_inc(st["logsig"], 1)

            def fox_pair(p, more):
                attend_fox(p)
                if more:
                    split_hi(U, 2 * p + (N_U_FOX + 3))
                else:
                    log_sigmoid(0)
                for t in range(2):
                    act.wait_ge(o_t, 2 * p + (t + 1))
                    act.wait_ge(down_done, 16 * p + 16 * M_MIX)
                    plain(act)
                    gain = head_gains[:, 0, ds(p, 1)] if more else head_gains[:, 0, p:p + 1]
                    sc.activation(h_hi[0][:, half(t)], ps[:, 4 + t, :], ACT.Copy, scale=gain).then_inc(h_hi_done, 1)

            with act.Fori(0, FOX_PAIRS - 1) as p:
                fox_pair(p, True)
            fox_pair(FOX_PAIRS - 1, False)

            for g in range(GLA_PAIRS):
                st = g_step
                split_hi(G, N_G_GLA + 3 * g + 1)
                for i in range(2):
                    act.wait_ge(st["b"], 2 * g + i + 1)
                    sc.activation(e_b[:, half(i)], ps[:, 4 + i, :], ACT.Exp).then_inc(st["eb"], 1)
                    sc.activation(e_nb[:, half(i)], ps[:, 4 + i, :], ACT.Exp, scale=-1.0).then_inc(st["eb"], 1)
                for i in range(2):
                    act.wait_ge(st["suf"], 2 * g + i + 1)
                    sc.activation(e_suf[:, 4 * i:4 * i + 4, :].rearrange("p a b -> p (a b)"), ps[:, 6 + i, :],
                                  ACT.Exp).then_inc(st["esuf"], 1)
                split_hi(U, N_U_GLA + 3 * g + 1)
                for hd in range(2):
                    e, more = 4 * g + 2 * hd, g + 1 < GLA_PAIRS or hd == 0
                    for i in range(2):
                        act.wait_ge(st["vt"], e + i + 1)
                        sc.activation(gv_rows[:, 4 * i:4 * i + 4, :].rearrange("p a b -> p (a b)"), ps[:, 4 + i, :],
                                      ACT.Copy).then_inc(st["vrows"], 1)
                    if more:
                        split_hi(G, N_G_GLA + 3 * g + 2 + hd)
                    split_hi(A, M_GLA + 2 * g + hd)
                    split_hi(B, M_GLA + 2 * g + hd)
                    for t in range(2):
                        act.wait_ge(gemm_read[U], 2 * (N_U_GLA + 3 * g + 1 + hd) + t + 1)
                        sc.activation(r_act[:, half(t)], r_act[:, half(t)], ACT.Silu).then_inc(st["silu"], 1)
                    for t in range(2):
                        act.wait_ge(st["o"], e + t + 1)
                        sc.activation(o_gla[:, half(t)], ps[:, 4 + t, :], ACT.Copy).then_inc(st["o_copy"], 1)
                        sc.activation(o_gla_sq[:, half(t)], ps[:, 4 + t, :], ACT.Square).then_inc(st["osq"], 1)
                    if more:
                        split_hi(U, N_U_GLA + 3 * g + 2 + hd)
                        if hd:
                            log_sigmoid(g + 1)
                    for t in range(2):
                        act.wait_ge(st["h"], e + t + 1)
                        sc.activation(h_hi[0][:, half(t)], x_new[:, t, :], ACT.Copy).then_inc(h_hi_done, 1)

            split_hi(G, N_G_MEM)
            split_hi(U, N_U_MEM)
            norms(2, N_G_MEM + 1, unscaled=None)
            split_hi(U, N_U_MEM + 1, unscaled=None)
            ms = m_step
            for k in range(4, KT):
                high_mem(k)
            with act.Fori(0, 4) as i:
                for s, nn in ((G, N_G_MEM), (U, N_U_MEM)):
                    act.wait_ge(gemm_done[s], 2 * i + (2 * nn + 4))
                    plain(act)
                    for r in range(2):
                        sc.activation(mem_k[:, ds(2 * i + s, 1), r * P:(r + 1) * P], ps[:, GEMM_BANK[s], r * P:(r + 1) * P],
                                      ACT.Copy, scale=1.0 / 16).then_inc(gemm_read[s], 1)
                    split_hi(s, i + (nn + 2), unscaled=None)

            def values(i, unscaled):
                for s, nn in ((G, N_G_MEM), (U, N_U_MEM)):
                    split_hi(s, i + (nn + 6), unscaled=unscaled)
                for s, nn in ((G, N_G_MEM), (U, N_U_MEM)):
                    act.wait_ge(ms["vt"], 2 * i + (s + 1))
                    plain(act)
                    for r in range(2):
                        col = i * 2 * P + s * P
                        sc.activation(mem_v[:, r, slice(col, col + P) if isinstance(i, int) else ds(col, P)],
                                      ps[:, 4 + s, r * P:(r + 1) * P], ACT.Copy).then_inc(ms["vrows"], 1)

            act.sem_inc(ms["vrows"], 4)
            with act.Fori(0, 3) as i:
                values(i, None)
            values(3, MEM_UNSCALED)

            def mem_head(h, more):
                def exponential(j):
                    act.wait_ge(ms["max"], 8 * h + (j + 1))
                    sc.activation(mem_p[:, j, :], ps[:, j, 0:MEM], ACT.Exp, bias=mem_max[:, j:j + 1],
                                  scale=1.0, accum_out=mem_sum[:, j:j + 1]).then_inc(ms["exp"], 1)

                def probs_leave(t):
                    act.wait_ge(ms["pt"], 2 * h + (t + 1))
                    if t:
                        act.wait_ge(ms["o"], 4 * h + 2)
                    for blk in range(2):
                        sc.activation(mem_pt[:, blk, :], ps[:, 4 + blk, :], ACT.Copy).then_inc(ms["pt_read"], 1)

                def high(t):
                    for c in range(2):
                        act.wait_ge(ms["o"], 4 * h + (2 * t + c + 1))
                        act.wait_ge(down_done, 32 * h + 16 * M_MEM)
                        sc.activation(h_hi[2 * c][:, half(t)], ps[:, 6 + c, :], ACT.Copy).then_inc(h_hi_done, 1)

                for j in range(NT):
                    exponential(j)
                for s in (A, B):
                    split_hi(s, 2 * h + M_MEM)
                probs_leave(0)
                high(0)
                probs_leave(1)
                high(1)
                if more:
                    split_hi(G, h + (N_G_MEM + 10), unscaled=MEM_UNSCALED)
                    split_hi(U, h + (N_U_MEM + 10), unscaled=MEM_UNSCALED)
                split_hi(A, 2 * h + (M_MEM + 1), early=more)
                split_hi(B, 2 * h + (M_MEM + 1))

            with act.Fori(0, MEM_H - 1) as h:
                mem_head(h, True)
            mem_head(MEM_H - 1, False)

            norms(3, N_G_FF2 + 1, unscaled=MEM_UNSCALED)
            ff(2)
            norms(4, None)
            for j in range(3, NT):
                write_out(j)

        @block.tensor
        def _(pe):
            mm = nc.tensor.matmul

            def product(acc, w, v, first, last):
                mm(acc, w[0], v[0], start=first, stop=False)
                mm(acc, w[0], v[1], start=False, stop=False)
                return mm(acc, w[1], v[0], start=False, stop=last)

            def x_tile(k, t):
                return x_hi[:, k, half(t)], x_lo[:, k, half(t)]

            def w_tile(slot, k):
                return tuple(w[:, slot, k * P:(k + 1) * P] for w in (w_hi, w_lo))

            def gemm(slot, n, t):
                if t == 0:
                    pe.wait_ge(w_ready[slot], n + 1)
                wait(pe, gemm_read[slot], 2 * n + (t - 1))
                for k in range(KT):
                    last = product(ps[:, GEMM_BANK[slot] + t, :], w_tile(slot, k), x_tile(k, t), k == 0, k == KT - 1)
                last.then_inc(gemm_done[slot], 1)

            def down_group(m, h_slot, d, t, k):
                pe.wait_ge(w_ready[A if d < 4 else B], m + 1)
                pe.wait_ge(h_ready, 2 * m + (t + 1))
                pe.wait_ge(down_read, 16 * m + (k + 1))
                w = w_hi[:, 2, d * P:(d + 1) * P], w_lo[:, 2, d * P:(d + 1) * P]
                v = h_hi[h_slot][:, half(t)], h_lo[h_slot][:, half(t)]
                product(ps[:, 4 + k % 4, :], w, v, True, True).then_inc(down_done, 1)

            def add_to_mean(stage, kind, r):
                t, q = divmod(r, 4)
                e = sq_event(stage, kind, 2 * r)
                if kind == 0:
                    pe.wait_ge(sq_added, 8 * (stage - 1) + r + 1)
                else:
                    pe.wait_ge(x_sq_added, 8 * stage + r + 1)
                for j in range(4):
                    last = mm(ps[:, stat_bank(kind, t), 4 * q + j:4 * q + j + 1], sq[:, e % 4, j * P:(j + 1) * P],
                              inv_d[:, 0:1], start=True, stop=True)
                last.then_inc(stat_done, 1)

            def spread(stage, kind, t):
                pe.wait_ge(diag_done, stat_event(stage, kind, t) + 1)
                mm(ps[:, stat_bank(kind, t), :], ones[:, :], diag[:, :], start=True, stop=True).then_inc(spread_done, 1)

            def down_all(m, h_slot, by_half, stage=None):
                for k in range(16):
                    d, t = (k % 8, k // 8) if by_half else (k // 2, k % 2)
                    down_group(m, h_slot, d, t, k)
                    if stage and k >= 12:
                        add_to_mean(stage, 0, k - 12)

            def old_x(stage, i):
                t, d = divmod(i, 8)
                if i >= 2:
                    if stage == 0:
                        pe.wait_ge(x_ready, i - 1)
                    else:
                        pe.wait_ge(x_new_done, 16 * (stage - 1) + i - 1)
                bank = ps[:, 4 + i % 2, :]
                if stage == 0:
                    if d == 0:
                        pe.wait_ge(x_in[t], 16 * 4)
                    for j in range(4):
                        last = nc.tensor.transpose(bank[:, j * P:(j + 1) * P], y[:, 4 * t + j, d * P:(d + 1) * P], ident[:, :])
                    last.then_inc(x_old, 1)
                else:
                    mm(bank, ident_r[:, :], x_hi[:, d, half(t)], start=True, stop=False)
                    mm(bank, ident_r[:, :], x_lo[:, d, half(t)], start=False, stop=True).then_inc(x_old, 1)

            def transpose_mem(kk):
                ms = m_step
                pe.wait_ge(ms["norm"], 2)
                if kk >= 2:
                    pe.wait_ge(ms["ready"], kk - 1)
                for k in range(2):
                    for j in range(2):
                        last = nc.tensor.transpose(ps[:, 4 + kk % 2, (2 * k + j) * P:(2 * k + j + 1) * P],
                                                   mem_rows[:, j, (2 * kk + k) * P:(2 * kk + k + 1) * P], ident[:, :])
                last.then_inc(ms["t"], 1)

            def rows_out(j):
                pe.wait_ge(x_hi_done, 16 * 4 + 8 * (j // 4 + 1))
                for b in range(2):
                    if j >= 2:
                        pe.wait_ge(out_read[b], j - 1)
                    for k in range(4):
                        last = nc.tensor.transpose(ps[:, 2 * (j % 2) + b, k * P:(k + 1) * P],
                                                   y[:, 4 * b + k, j * P:(j + 1) * P], ident[:, :])
                    last.then_inc(out_t, 1)

            def norms(stage, first):
                if stage > 0:
                    pe.wait_ge(down_read, 16 * (LAST_M[stage] + 1) + RING)
                for i in range(2):
                    old_x(stage, i)
                if stage > 0:
                    spread(stage, 0, 0)
                    for r in (4, 5):
                        add_to_mean(stage, 0, r)
                for i in range(16):
                    if i + 2 < 16:
                        old_x(stage, i + 2)
                    t, k = divmod(i, 8)
                    if stage > 0 and i < 2:
                        add_to_mean(stage, 0, 6 + i)
                    if i % 2 and i >= 3:
                        add_to_mean(stage, 1, (i - 3) // 2)
                    if first:
                        pe.wait_ge(x_ready, 16 * stage + i + 1)
                    for slot, n in first:
                        if i == 0:
                            pe.wait_ge(w_ready[slot], n + 1)
                        if k == 0:
                            wait(pe, gemm_read[slot], 2 * n + (t - 1))
                            if stage > 0:
                                pe.wait_ge(rs_ready, stat_event(stage, 0, t) + 1)
                        last = product(ps[:, GEMM_BANK[slot] + t, :], w_tile(slot, k), x_tile(k, t),
                                       k == 0, k == KT - 1)
                        if k == KT - 1:
                            last.then_inc(gemm_done[slot], 1)
                    if stage > 0 and i == 4:
                        spread(stage, 0, 1)
                    if stage == 4 and i >= 13:
                        rows_out(i - 13)
                    if i == 15 and stage < 4:
                        spread(stage, 1, 0)
                add_to_mean(stage, 1, 7)
                if stage == 2:
                    pe.wait_ge(x_new_done, 16 * stage)
                    for kk in (0, 1):
                        transpose_mem(kk)
                if stage < 4:
                    spread(stage, 1, 1)

            def ff(which):
                f = FF[which]

                def chunk(c, parity):
                    m = f["m"] + c - 1
                    for q in range(4):
                        slot, t = (G, U)[q // 2], q % 2
                        gemm(slot, (f["nG"] if slot == G else f["nU"]) + c, t)
                        for k in range(4 * q, 4 * q + 4):
                            down_group(m, 1 - parity, k // 2, k % 2, k)

                with pe.Fori(0, (FC - 2) // 2) as i:
                    chunk(i * 2 + 1, 1)
                    chunk(i * 2 + 2, 0)
                chunk(FC - 1, 1)
                for s in (G, U):
                    pe.wait_ge(gemm_read[s], 2 * (f["nG" if s == G else "nU"] + FC))
                if which == 1:
                    pe.wait_ge(gains_in, 16 * 12)
                    rows = slice(0, 11 * KT)
                    nc.tensor.transpose(ps[:, 2, rows], sq[rows, 0, 0:P], ident[rows, rows]).then_inc(gains_t, 1)
                down_all(f["m"] + FC - 1, 1, True, 1 if which == 1 else 4)

            pe.wait_ge(const_ready, 1)
            pe.wait_ge(gain_in, 16)
            nc.tensor.transpose(ps[:, 6, 0:KT], sq[0:KT, 0, 0:P], ident[0:KT, 0:KT]).then_inc(gains_t, 1)
            pe.wait_ge(const_ready, 2)
            norms(0, [(G, 0), (U, 0)])
            ff(1)
            norms(1, [(G, N_G_MIX), (U, N_U_FOX)])

            for t in range(2):
                gemm(G, N_G_FOX, t)
            pe.wait_ge(f_step["log_f"], 1)
            for j in range(NT):
                last = nc.tensor.transpose(ps[:, 4, j * FOX_H:(j + 1) * FOX_H], forget_a[32:40, j * P:(j + 1) * P],
                                           ident[32:40, 32:40])
            last.then_inc(f_step["log_f_t"], 1)
            pe.wait_ge(f_step["log_f_rows"], 1)
            pe.wait_ge(g_step["consts"], 2)
            for j in range(NT):
                last = mm(ps[0:FOX_H, 6 + j // 4, (j % 4) * P:(j % 4 + 1) * P], lf_rows[:, j, :], tri,
                          start=True, stop=True)
            last.then_inc(f_step["tile_sums"], 1)
            for t in range(2):
                gemm(U, N_U_FOX + 1, t)
            pe.wait_ge(f_step["c"], 1)

            def scores(p, a):
                hh, b = divmod(a, 8)
                if a >= 2:
                    pe.wait_ge(exp_done, 16 * p + (a - 1))
                width = (b + 1) * P
                q = q_head[hh][0:66, b * P:(b + 1) * P]
                for t in range((width + HT - 1) // HT):
                    w = min(HT, width - t * HT)
                    diagonal = (t + 1) * HT >= width
                    mm(ps[:, 2 * (a % 2) + t, 0:w], q, k_head[hh][0:66, t * HT:t * HT + w], start=True, stop=not diagonal)
                    if diagonal:
                        mm(ps[:, 2 * (a % 2) + t, w - P:w], ident_b[:, :], neg_mask[:, :], start=False,
                           stop=True).then_inc(score_done, 1)

            def transpose_probs(p, a):
                hh, b = divmod(a, 8)
                pe.wait_ge(exp_done, 16 * p + (a + 1))
                for i in range(b // 4 + 1):
                    if i == 0 and a > 0:
                        pe.wait_ge(pt_lo_read, 16 * p + a)
                    if i == 1 and (a > 4):
                        pe.wait_ge(pt_hi_read, 8 * p + (4 * hh + b - 4))
                    for j in range(4 * i, min(4 * i + 4, b + 1)):
                        last = nc.tensor.transpose(ps[:, 4 + i, (j % 4) * P:(j % 4 + 1) * P],
                                                   probs[:, a % 2, j * P:(j + 1) * P], ident[:, :])
                    last.then_inc(pt_hi if i else pt_lo, 1)

            def attend_values(p, a):
                hh, b = divmod(a, 8)
                pe.wait_ge(pt_lo_read, 16 * p + (a + 1))
                if b >= 4:
                    pe.wait_ge(pt_hi_read, 8 * p + (4 * hh + b - 3))
                if a >= 2:
                    pe.wait_ge(o_read, 16 * p + (a - 1))
                for j in range(b + 1):
                    last = mm(ps[:, 6 + a % 2, 0:FOX_D], probs_t[:, a % 2, j, :],
                              v_rows[:, j, hh * FOX_D:(hh + 1) * FOX_D], start=j == 0, stop=j == b)
                last.then_inc(o_done, 1)

            def gates(g):
                for i in range(2):
                    for j in range(4):
                        last = mm(ps[:, 2 + i, j * P:(j + 1) * P], gate_low[0:RANK + 1, (4 * i + j) * P:(4 * i + j + 1) * P],
                                  w_g2[0:RANK + 1, g * P:(g + 1) * P], start=True, stop=True)
                    last.then_inc(g_step["gate"], 1)

            def fox_pair(p, more):
                pe.wait_ge(c_in, 64 * p + 64)
                pe.wait_ge(gemm_read[G], 2 * p + (2 * N_G_FOX + 2))
                scores(p, 0)
                pe.wait_ge(gemm_read[U], 4 * p + (2 * N_U_FOX + 4))
                pe.wait_ge(down_read, 16 * p + (16 * M_MIX + RING))
                for i in range(2):
                    for j in range(4):
                        last = nc.tensor.transpose(ps[:, 4 + i, j * P:(j + 1) * P],
                                                   v_t[:, (4 * i + j) * P:(4 * i + j + 1) * P], ident[:, :])
                    last.then_inc(v_t_done, 1)
                for a in range(18):
                    if 1 <= a < 16:
                        scores(p, a)
                    if a == 1:
                        pe.wait_ge(v_rows_done, 2 * p + 2)
                    if 1 <= a <= 16:
                        transpose_probs(p, a - 1)
                    if a >= 2:
                        attend_values(p, a - 2)
                if more:
                    for t in range(2):
                        gemm(U, 2 * p + (N_U_FOX + 2), t)
                else:
                    gates(0)
                    for t in range(2):
                        gemm(G, N_G_GLA, t)
                pe.wait_ge(o_norm, p + 1)
                for i in range(2):
                    for j in range(4):
                        last = nc.tensor.transpose(ps[:, 4 + i, j * P:(j + 1) * P],
                                                   o_rows[:, 4 * i + j, :, :].rearrange("p a b -> p (a b)"), ident[:, :])
                    last.then_inc(o_t, 1)
                if more:
                    for t in range(2):
                        gemm(G, p + (N_G_FOX + 1), t)
                else:
                    pe.wait_ge(g_step["la"], 2)
                    for t in range(2):
                        gemm(U, N_U_GLA, t)
                pe.wait_ge(h_ready, 2 * p + (2 * M_MIX + 2))
                down_all(p + M_MIX, 0, True)
                if more:
                    for t in range(2):
                        gemm(U, 2 * p + (N_U_FOX + 3), t)

            with pe.Fori(0, FOX_PAIRS - 1) as p:
                fox_pair(p, True)
            fox_pair(FOX_PAIRS - 1, False)

            st = g_step
            pe.wait_ge(down_read, 16 * M_GLA + RING)
            for g in range(GLA_PAIRS):
                for i in range(2):
                    for j in range(4):
                        last = mm(ps[:, 4 + i, j * P:(j + 1) * P], la[:, 4 * i + j, :], tri_blk[:, :], start=True, stop=True)
                    last.then_inc(st["b"], 1)
                for i in range(2):
                    mm(ps[:, 6 + i, :], tri_suf[:, :], la[:, 4 * i:4 * i + 4, :].rearrange("p a b -> p (a b)"),
                       start=True, stop=True).then_inc(st["suf"], 1)
                gemm(G, N_G_GLA + 3 * g + 1, 0)
                pe.wait_ge(st["eb"], 4 * g + 4)
                pe.wait_ge(gemm_read[U], 2 * (N_U_GLA + 3 * g + 1))
                for i in range(2):
                    for j in range(4):
                        last = nc.tensor.transpose(ps[:, 4 + i, j * P:(j + 1) * P],
                                                   k_inv[:, (4 * i + j) * P:(4 * i + j + 1) * P], ident[:, :])
                    last.then_inc(st["kt"], 1)
                gemm(G, N_G_GLA + 3 * g + 1, 1)
                for hd in range(2):
                    rows = slice(hd * GLA_C, (hd + 1) * GLA_C)
                    e, more = 4 * g + 2 * hd, g + 1 < GLA_PAIRS or hd == 0
                    pe.wait_ge(gemm_read[G], 2 * (N_G_GLA + 3 * g + 2 + hd))
                    pe.wait_ge(st["kdec"], 2 * g + 2)
                    for i in range(2):
                        for j in range(4):
                            last = nc.tensor.transpose(ps[:, 4 + i, j * P:(j + 1) * P],
                                                       gv_t[:, (4 * i + j) * P:(4 * i + j + 1) * P], ident[:, :])
                        last.then_inc(st["vt"], 1)
                    pe.wait_ge(st["qdec"], g + 1)
                    for i in range(2):
                        for j in range(4 * i, 4 * i + 4):
                            tile = slice(j * P, (j + 1) * P)
                            last = mm(ps[:, i, (j % 4) * P:(j % 4 + 1) * P], k_inv[rows, tile], q_dec[rows, tile],
                                      start=True, stop=True)
                        last.then_inc(st["att"], 1)
                    pe.wait_ge(st["vrows"], e + 2)
                    pe.wait_ge(st["esuf"], 2 * g + 2)
                    for n in range(NC - 1):
                        r = slice((n % 2) * GLA_C, (n % 2 + 1) * GLA_C)
                        if n == 8:
                            pe.wait_ge(st["att_read"], 8 * g + 4 * hd + 4)
                        last = mm(kv_psum(rows, n), k_dec[r, n // 2, rows],
                                  gv_rows[r, n // 2, :], start=True, stop=True)
                        if n in (7, NC - 2):
                            last.then_inc(st["kv"], 1)
                    for t in range(2):
                        gemm(U, N_U_GLA + 3 * g + 1 + hd, t)
                    pe.wait_ge(st["att_mask"], e + 2)
                    pe.wait_ge(st["state"], e + 2)
                    for j in range(NT):
                        acc = ps[:, 4 + j // 4, (j % 4) * P:(j % 4 + 1) * P]
                        mm(acc, gv_rows[:, j, :], att_t[:, j, :], start=True, stop=False)
                        for n in (2 * j, 2 * j + 1):
                            if n > 0:
                                last = mm(acc[:, (n % 2) * GLA_C:(n % 2 + 1) * GLA_C], states[rows, n, :],
                                          q_dec[rows, n * GLA_C:(n + 1) * GLA_C], start=False, stop=n % 2 == 1)
                        if j % 4 == 3:
                            last.then_inc(st["o"], 1)
                    for t in range(2):
                        pe.wait_ge(st["osq"], e + t + 1)
                        for j in range(4):
                            last = mm(ps[:, 6 + t, j:j + 1], o_gla_sq[:, (4 * t + j) * P:(4 * t + j + 1) * P],
                                      inv_d[:, 1:2], start=True, stop=True)
                        last.then_inc(st["stat"], 1)
                    if more and hd:
                        pe.wait_ge(gemm_read[U], 2 * (N_U_GLA + 3 * g + 3))
                        gates(g + 1)
                    if more:
                        gemm(G, N_G_GLA + 3 * g + 2 + hd, 0)
                    for t in range(2):
                        pe.wait_ge(st["diag"], e + t + 1)
                        mm(ps[:, 6 + t, :], ones[:, :], gla_diag[t], start=True, stop=True).then_inc(st["spread"], 1)
                    if more:
                        gemm(G, N_G_GLA + 3 * g + 2 + hd, 1)
                    if more and hd:
                        pe.wait_ge(st["la"], 2 * g + 4)
                        for t in range(2):
                            gemm(U, N_U_GLA + 3 * g + 3, t)
                    m = M_GLA + 2 * g + hd
                    pe.wait_ge(h_ready, 2 * m + 2)
                    down_all(m, 0, True, None if more else 2)
                    if more:
                        pe.wait_ge(down_read, 16 * (m + 1) + RING)

            norms(2, [(G, N_G_MEM), (U, N_U_MEM)])

            ms = m_step
            for kk in (2, 3):
                transpose_mem(kk)
            pe.wait_ge(ms["ready"], 4)

            def gemm_mem(slot, n):
                pe.wait_ge(w_ready[slot], n + 1)
                pe.wait_ge(gemm_read[slot], 2 * n)
                for k in range(KT):
                    w, v, acc = w_tile(slot, k), (memt_hi[:, k, :], memt_lo[:, k, :]), ps[:, GEMM_BANK[slot], 0:MEM]
                    mm(acc, w[0], v[0], start=k == 0, stop=False)
                    a = mm(acc, w[0], v[1], start=False, stop=False)
                    b = mm(acc, w[1], v[0], start=False, stop=k == KT - 1)
                a.then_inc(gemm_done[slot], 1)
                b.then_inc(gemm_done[slot], 1)

            with pe.Fori(0, 4) as i:
                for s, nn in ((G, N_G_MEM), (U, N_U_MEM)):
                    gemm_mem(s, i + (nn + 1))
            with pe.Fori(0, 4) as i:
                for s, nn in ((G, N_G_MEM), (U, N_U_MEM)):
                    gemm_mem(s, i + (nn + 5))
                pe.wait_ge(ms["vrows"], 4 * i + 4)
                for s, nn in ((G, N_G_MEM), (U, N_U_MEM)):
                    pe.wait_ge(gemm_read[s], 2 * i + (2 * nn + 12))
                    for r in range(2):
                        last = nc.tensor.transpose(ps[:, 4 + s, r * P:(r + 1) * P], mem_vt[:, s, r * P:(r + 1) * P],
                                                   ident[:, :])
                    last.then_inc(ms["vt"], 1)

            def mem_head(h, more):
                for s, nn in ((G, N_G_MEM), (U, N_U_MEM)):
                    pe.wait_ge(gemm_read[s], 2 * h + (2 * nn + 18))
                for j in range(NT):
                    if j == 4:
                        pe.wait_ge(ms["vrows"], 16 + 4)
                        pe.wait_ge(down_read, 32 * h + (16 * M_MEM + RING))
                    for c in range(2):
                        last = mm(ps[:, j, 0:MEM], q_mem[:, c, j * P:(j + 1) * P], mem_k[:, ds(2 * h + c, 1), :],
                                  start=c == 0, stop=c == 1)
                    last.then_inc(ms["score"], 1)

                def next_q(slot, t):
                    if more:
                        pe.wait_ge(ms["exp"], 8 * h + (GEMM_BANK[slot] + t + 1))
                        gemm(slot, h + ((N_G_MEM if slot == G else N_U_MEM) + 9), t)

                def transposes(t):
                    pe.wait_ge(ms["scaled"], 8 * h + (4 * t + 4))
                    if t:
                        pe.wait_ge(ms["pt_read"], 4 * h + 2)
                    else:
                        pe.wait_ge(ms["exp"], 8 * h + 8)
                    for blk in range(2):
                        for j in range(4):
                            last = nc.tensor.transpose(ps[:, 4 + blk, j * P:(j + 1) * P],
                                                       mem_p[:, 4 * t + j, blk * P:(blk + 1) * P], ident[:, :])
                    last.then_inc(ms["pt"], 1)

                def values(t):
                    pe.wait_ge(ms["pt_read"], 4 * h + (2 * t + 2))
                    pe.wait_ge(ms["vh"], h + 1)
                    for c in range(2):
                        if t:
                            pe.wait_ge(h_ready, 4 * h + (2 * M_MEM + c + 1))
                        for blk in range(2):
                            last = mm(ps[:, 6 + c, :], mem_vh[:, blk, c * P:(c + 1) * P], mem_pt[:, blk, :],
                                      start=blk == 0, stop=blk == 1)
                        last.then_inc(ms["o"], 1)

                next_q(G, 0)
                transposes(0)
                next_q(G, 1)
                values(0)
                transposes(1)
                next_q(U, 0)
                values(1)
                next_q(U, 1)
                pe.wait_ge(h_ready, 4 * h + (2 * M_MEM + 4))
                down_all(2 * h + M_MEM, 0, not more)
                down_all(2 * h + (M_MEM + 1), 2, not more, None if more else 3)

            with pe.Fori(0, MEM_H - 1) as h:
                mem_head(h, True)
            mem_head(MEM_H - 1, False)

            norms(3, [(G, N_G_FF2), (U, N_U_FF2)])
            ff(2)
            norms(4, [])
            for j in range(3, NT):
                rows_out(j)

        @block.vector
        def _(dve):
            ve = nc.vector

            def split_lo(slot, n):
                dve.wait_ge(w_hi_done[slot], n + 1)
                ve.tensor_tensor(lo_tile(slot), raw_tile(slot), f32(hi_tile(slot)), ALU.subtract).then_inc(w_ready[slot], 1)

            def add_group(m, d, t, k):
                dve.wait_ge(down_done, 16 * m + (k + 1))
                ve.tensor_tensor(y[:, d, half(t)], y[:, d, half(t)], ps[:, 4 + k % 4, :], ALU.add).then_inc(down_read, 1)

            def add_all(m, by_half, stage=None, next_a=None):
                for k in range(16):
                    if next_a is not None and k == 12:
                        split_lo(A, next_a)
                    d, t = (k % 8, k // 8) if by_half else (k // 2, k % 2)
                    add_group(m, d, t, k)
                if stage:
                    mean(stage, 0, 0)
                    make_diag(stage, 0, 0)

            def mean(stage, kind, t):
                e = stat_event(stage, kind, t)
                dve.wait_ge(stat_done, 4 * e + 4)
                sums = ps[:, stat_bank(kind, t), 0:16].rearrange("p (r j) -> p j r", j=4)
                dve.drain()
                ve.tensor_reduce(out=mean4[:, 0:4], in_=sums, op=ALU.add, axis=AX.X)
                dve.drain()
                ve.tensor_scalar(mean4[:, 0:4], mean4[:, 0:4], EPS, None, ALU.add).then_inc(mean_done, 1)

            def make_diag(stage, kind, t):
                e = stat_event(stage, kind, t)
                dve.wait_ge(pow_done, e + 1)
                wait(dve, spread_done, e)
                ve.tensor_tensor(slot3(diag[:, :]), ident[:, :].unsqueeze(1).to_broadcast([P, 4, P]),
                                 rms4[:, 0:4].unsqueeze(2).to_broadcast([P, 4, P]), ALU.mult).then_inc(diag_done, 1)

            def low_x(stage, i):
                t, d = divmod(i, 8)
                src = ps[:, 4 + i % 2, :] if stage == 0 else x_new[:, i % 2, :]
                dve.wait_ge(x_hi_done, 16 * stage + i + 1)
                if stage == 0:
                    dve.wait_ge(sq_done, i + 1)
                ve.tensor_tensor(x_lo[:, d, half(t)], src, f32(x_hi[:, d, half(t)]),
                                 ALU.subtract).then_inc(x_ready, 1)

            def add_x_pair(stage, r):
                e = sq_event(stage, 1, 2 * r)
                dve.wait_ge(sq_done, e + 2)
                ve.tensor_tensor(sq[:, e % 4, :], sq[:, e % 4, :], sq[:, e % 4 + 1, :], ALU.add).then_inc(x_sq_added, 1)

            def write_out(j):
                dve.wait_ge(pow_done, stat_event(4, 1, j // 4) + 1)
                dve.wait_ge(out_t, 2 * j + 2)
                if j >= 2:
                    dve.wait_ge(out_sent[j % 2], 16 * (j // 2))
                ve.tensor_scalar(out_rows[:, j % 2, HT:D], ps[:, 2 * (j % 2) + 1, :], rms8[:, j:j + 1], None,
                                 ALU.mult).then_inc(out_read[1], 1)

            def norms(stage, next_g):
                for i in range(16):
                    t, d = divmod(i, 8)
                    if stage > 0:
                        if i >= 2:
                            dve.wait_ge(sq_done, sq_event(stage, 1, i) - 1)
                        dve.drain()
                        dve.wait_ge(y_scaled, 16 * (stage - 1) + i + 1)
                        dve.wait_ge(x_old, 16 * stage + i + 1)
                        ve.scalar_tensor_tensor(out=x_new[:, i % 2, :], in0=y[:, d, half(t)],
                                                scalar=gains[:, GAIN[POST[stage]], d:d + 1], in1=ps[:, 4 + i % 2, :],
                                                op0=ALU.mult, op1=ALU.add).then_inc(x_new_done, 1)
                        if stage < 4 and i >= 1:
                            low_x(stage, i - 1)
                        if i == 2:
                            mean(stage, 0, 1)
                        if i == 4:
                            make_diag(stage, 0, 1)
                    else:
                        low_x(stage, i)
                    if stage == 0 and i % 2:
                        add_x_pair(0, i // 2)
                    if stage > 0 and i % 2 and i >= 3:
                        add_x_pair(stage, (i - 3) // 2)
                    if stage == 2 and i == 11:
                        dve.wait_ge(m_step["sq"], 2)
                        ve.tensor_scalar(mem_stat[:, 0:2], mem_stat[:, 0:2], 1.0 / D, EPS, ALU.mult,
                                         ALU.add).then_inc(m_step["mean"], 1)
                    if i == 12:
                        mean(stage, 1, 0)
                    if stage == 4 and i >= 14:
                        write_out(i - 14)
                    if i == 14 and stage < 4:
                        make_diag(stage, 1, 0)
                if 0 < stage < 4:
                    low_x(stage, 15)
                if stage > 0:
                    add_x_pair(stage, 7)
                if stage == 4:
                    write_out(2)
                if next_g:
                    split_lo(G, next_g)
                mean(stage, 1, 1)
                if stage < 4:
                    make_diag(stage, 1, 1)

            def ff(which):
                f = FF[which]

                def chunk(c, parity, first=False, last=False):
                    nG, nU, m = f["nG"] + c, f["nU"] + c, f["m"] + c

                    def scale_gate(t):
                        wait(dve, silu_done, f["s"] + 2 * c + (t - 1))
                        dve.wait_ge(gemm_done[G], 2 * nG + (t + 1))
                        ve.tensor_tensor(gate[:, t, :], ps[:, t, :], rs[:, half(t)], ALU.mult).then_inc(gemm_read[G], 1)

                    def times_up(t):
                        dve.wait_ge(gemm_done[U], 2 * nU + (t + 1))
                        dve.wait_ge(gate_scaled, f["s"] + 2 * c + (t + 1))
                        ve.tensor_tensor(hidden[:, t, :], ps[:, 2 + t, :], gate_act[:, t, :],
                                         ALU.mult).then_inc(gemm_read[U], 1)

                    def low_hidden(t):
                        dve.wait_ge(h_hi_done, 2 * m + (t + 1))
                        ve.tensor_tensor(h_lo[parity][:, half(t)], hidden[:, t, :], f32(h_hi[parity][:, half(t)]),
                                         ALU.subtract).then_inc(h_ready, 1)

                    def add_groups(q):
                        if not first:
                            for k in range(4 * q, 4 * q + 4):
                                add_group(m - 1, k // 2, k % 2, k)

                    if first:
                        for t in range(2):
                            dve.wait_ge(rs_ready, stat_event(0 if which == 1 else 3, 1, t) + 1)
                            scale_gate(t)
                    else:
                        dve.drain()
                        scale_gate(0)
                        split_lo(U, nU)
                        add_groups(0)
                        split_lo(B, m - 1)
                        scale_gate(1)
                        add_groups(1)
                    if not first and not last:
                        split_lo(G, nG + 1)
                    times_up(0)
                    split_lo(A, m)
                    low_hidden(0)
                    add_groups(2)
                    times_up(1)
                    low_hidden(1)
                    add_groups(3)

                chunk(0, 0, first=True)
                dve.wait_ge(y_zero, 8 * (1 if which == 1 else 4))
                with dve.Fori(0, (FC - 2) // 2) as i:
                    chunk(i * 2 + 1, 1)
                    chunk(i * 2 + 2, 0)
                chunk(FC - 1, 1, last=True)
                split_lo(B, f["m"] + FC - 1)
                if which == 1:
                    dve.wait_ge(gains_t, 2)
                    ve.tensor_copy(gains[:, :, :].rearrange("p a k -> p (a k)"), ps[:, 2, 0:11 * KT])
                    dve.drain()
                    for name in ("ff1_post", "ff2_post"):
                        g = gains[:, GAIN[name], :]
                        ve.tensor_scalar(g, g, 0.5, None, ALU.mult)
                    dve.drain().then_inc(const_ready, 1)
                dve.drain()
                add_all(f["m"] + FC - 1, True, 1 if which == 1 else 4)

            dve.sem_inc(down_read, RING)
            dve.wait_ge(const_ready, 1)
            ve.tensor_copy(ident_r[:, :], ident[:, :])
            dve.wait_ge(gains_t, 1)
            ve.tensor_copy(gains[:, GAIN["ff1_pre"], :], ps[:, 6, 0:KT])
            dve.drain().then_inc(const_ready, 1)
            split_lo(G, 0)
            split_lo(U, 0)
            norms(0, 1)
            ff(1)
            split_lo(U, N_U_FOX)
            split_lo(G, N_G_MIX)
            norms(1, N_G_FOX)

            row = slice(32, 40)
            dve.wait_ge(g_step["consts"], 1)
            for t in range(2):
                dve.wait_ge(rs_ready, stat_event(1, 1, t) + 1)
                dve.wait_ge(gemm_done[G], 2 * N_G_MIX + t + 1)
                ve.tensor_tensor(gate_low[0:RANK, half(t)], ps[0:RANK, t, :], rs[0:RANK, half(t)], ALU.mult)
                ve.tensor_tensor(forget[row, half(t)], ps[row, t, :], rs[row, half(t)], ALU.mult).then_inc(gemm_read[G], 1)
            dve.drain()
            dve.wait_ge(small_in, 16 * 4)
            for t in range(2):
                ve.tensor_scalar(forget[row, half(t)], forget[row, half(t)], b_f[row, :], None, ALU.add).then_inc(f_step["biased"], 1)
            def fox_q(n, t):
                dve.wait_ge(gemm_done[U], 2 * n + (t + 1))
                for i in range(2):
                    r = slice(i * FOX_D, (i + 1) * FOX_D)
                    last = ve.scalar_tensor_tensor(out=q_head[i][0:FOX_D, half(t)], in0=ps[r, 2 + t, :],
                                                   scalar=FOX_D ** -0.5, in1=rs[r, half(t)], op0=ALU.mult, op1=ALU.mult)
                last.then_inc(gemm_read[U], 1)

            def fox_k(n, t):
                dve.wait_ge(gemm_done[G], 2 * n + (t + 1))
                for i in range(2):
                    r = slice(i * FOX_D, (i + 1) * FOX_D)
                    last = ve.tensor_tensor(k_head[i][0:FOX_D, half(t)], ps[r, t, :], rs[r, half(t)], ALU.mult)
                last.then_inc(gemm_read[G], 1)

            def fox_v(n, t):
                dve.wait_ge(gemm_done[U], 2 * n + (t + 1))
                ve.tensor_tensor(v_t[:, half(t)], ps[:, 2 + t, :], rs[:, half(t)], ALU.mult).then_inc(gemm_read[U], 1)

            for t in range(2):
                fox_q(N_U_FOX, t)
            dve.wait_ge(f_step["ln"], 1)
            ve.scalar_tensor_tensor(out=forget_a[row, :], in0=forget[row, :], scalar=0.0, in1=forget_a[row, :], op0=ALU.min,
                                    op1=ALU.subtract).then_inc(f_step["log_f"], 1)
            split_lo(U, N_U_FOX + 1)
            for t in range(2):
                fox_k(N_G_FOX, t)
            dve.wait_ge(f_step["log_f_t"], 1)
            ve.tensor_copy(lf_rows[:, :, :].rearrange("p a b -> p (a b)"), ps[:, 4, 0:NT * FOX_H]).then_inc(f_step["log_f_rows"], 1)
            dve.wait_ge(f_step["tile_sums"], 1)
            c_psum = ps[0:FOX_H, 6:8, :].rearrange("p a b -> p (a b)")
            for j in range(NT):
                tile = slice(j * P, (j + 1) * P)
                if j == 0:
                    ve.tensor_copy(c_sb[:, 0, tile], c_psum[:, tile])
                else:
                    ve.tensor_scalar(c_sb[:, 0, tile], c_psum[:, tile], c_sb[:, 0, j * P - 1:j * P], None, ALU.add)
                dve.drain()
            ve.tensor_scalar(c_sb[:, 1, :], c_sb[:, 0, :], -1.0, None, ALU.mult).then_inc(f_step["c"], 1)
            for t in range(2):
                fox_v(N_U_FOX + 1, t)

            def attend_fox(p):
                splits = {6: (U, 2 * p + (N_U_FOX + 2)), 8: (G, p + (N_G_FOX + 1)),
                          10: (A, p + M_MIX), 12: (B, p + M_MIX)}
                for a in range(19):
                    if a in splits:
                        split_lo(*splits[a])
                    if a < 16:
                        hh, b = divmod(a, 8)
                        dve.wait_ge(score_done, 16 * p + (a + 1))
                        bank = 2 * (a % 2)
                        ve.tensor_reduce(out=neg_max[:, b, hh:hh + 1],
                                         in_=ps[:, bank:bank + 2, :].rearrange("p a b -> p (a b)")[:, 0:(b + 1) * P],
                                         op=ALU.max, axis=AX.X, negate=True).then_inc(max_done, 1)
                    if a >= 3:
                        h3, b3 = divmod(a - 3, 8)
                        ve.reciprocal(row_inv[:, b3, h3:h3 + 1], row_sum[:, b3, h3:h3 + 1])
                    if 1 <= a <= 16:
                        b1 = (a - 1) % 8
                        dve.wait_ge(pt_lo, 16 * p + a)
                        if a >= 3:
                            dve.wait_ge(o_done, 16 * p + (a - 2))
                        n = min(b1 + 1, 4)
                        ve.tensor_copy(probs_t[:, (a - 1) % 2, 0:n, :].rearrange("p a b -> p (a b)"),
                                       ps[:, 4, 0:n * P]).then_inc(pt_lo_read, 1)
                    if a >= 3:
                        dve.drain()
                        dve.wait_ge(o_done, 16 * p + (a - 2))
                        ve.tensor_scalar(o_rows[:, b3, h3, :], ps[:, 6 + (a - 3) % 2, 0:FOX_D], row_inv[:, b3, h3:h3 + 1],
                                         None, ALU.mult).then_inc(o_read, 1)

            def log_a(g):
                for i in range(2):
                    dve.wait_ge(g_step["logsig"], 6 * g + 3 * i + 3)
                    ve.scalar_tensor_tensor(out=la[:, 4 * i:4 * i + 4, :].rearrange("p a b -> p (a b)"), in0=ps[:, 2 + i, :],
                                            scalar=0.0, in1=gate_a[:, half(i)], op0=ALU.min,
                                            op1=ALU.subtract).then_inc(g_step["la"], 1)

            def gla_q(g, t):
                n = N_G_GLA + 3 * g
                dve.wait_ge(gemm_done[G], 2 * n + t + 1)
                ve.scalar_tensor_tensor(out=q_dec[:, half(t)], in0=ps[:, t, :], scalar=GLA_C ** -0.5,
                                        in1=rs[:, half(t)], op0=ALU.mult, op1=ALU.mult).then_inc(gemm_read[G], 1)

            def gla_out(slot, n, dst):
                for t in range(2):
                    dve.wait_ge(gemm_done[slot], 2 * n + t + 1)
                    ve.tensor_tensor(dst[:, half(t)], ps[:, GEMM_BANK[slot] + t, :], rs[:, half(t)],
                                     ALU.mult).then_inc(gemm_read[slot], 1)

            def fox_pair(p, more):
                dve.drain()
                attend_fox(p)
                dve.wait_ge(o_sq_done, 16 * p + 16)
                ve.tensor_scalar(mean4[:, :], o_sq[:, :, :].rearrange("p a b -> p (a b)"), 1.0 / FOX_D, EPS, ALU.mult,
                                 ALU.add).then_inc(o_mean, 1)
                dve.wait_ge(o_pow, p + 1)
                o16 = o_rows[:, :, :, :].rearrange("p a b c -> p (a b) c")
                ve.tensor_tensor(o16, o16, rms4[:, :].unsqueeze(2).to_broadcast([P, 16, FOX_D]), ALU.mult).then_inc(o_norm, 1)
                if more:
                    for t in range(2):
                        fox_q(2 * p + (N_U_FOX + 2), t)
                    split_lo(U, 2 * p + (N_U_FOX + 3))
                else:
                    for t in range(2):
                        gla_q(0, t)
                    log_a(0)
                gain = head_gains[:, 0, ds(p, 1)] if more else head_gains[:, 0, p:p + 1]
                for t in range(2):
                    dve.wait_ge(h_hi_done, 2 * p + (2 * M_MIX + t + 1))
                    ve.scalar_tensor_tensor(out=h_lo[0][:, half(t)], in0=ps[:, 4 + t, :], scalar=gain,
                                            in1=f32(h_hi[0][:, half(t)]), op0=ALU.mult, op1=ALU.subtract).then_inc(h_ready, 1)
                if more:
                    for t in range(2):
                        fox_k(p + (N_G_FOX + 1), t)
                else:
                    gla_out(U, N_U_GLA, k_inv)
                dve.wait_ge(y_zero, 16)
                add_all(p + M_MIX, True)
                if more:
                    for t in range(2):
                        fox_v(2 * p + (N_U_FOX + 3), t)

            with dve.Fori(0, FOX_PAIRS - 1) as p:
                fox_pair(p, True)
            fox_pair(FOX_PAIRS - 1, False)

            st = g_step
            for g in range(GLA_PAIRS):
                split_lo(G, N_G_GLA + 3 * g + 1)
                for i in range(2):
                    dve.wait_ge(st["kt"], 2 * g + i + 1)
                    dve.wait_ge(st["esuf"], 2 * g + i + 1)
                    tiles = slice(4 * i, 4 * i + 4)
                    ve.tensor_tensor(k_dec[:, tiles, :].rearrange("p a b -> p (a b)"), ps[:, 4 + i, :],
                                     e_suf[:, tiles, :].rearrange("p a b -> p (a b)"), ALU.mult).then_inc(st["kdec"], 1)
                dve.drain()
                ve.tensor_tensor(k_inv[:, :], k_inv[:, :], e_nb[:, :], ALU.mult)
                ve.tensor_copy(decay[:, :], e_b[:, :].rearrange("p (n c) -> p n c", c=GLA_C)[:, :, GLA_C - 1])
                ve.tensor_tensor(q_dec[:, :], q_dec[:, :], e_b[:, :], ALU.mult)
                dve.drain().then_inc(st["qdec"], 1)
                gla_out(G, N_G_GLA + 3 * g + 1, gv_t)
                dve.wait_ge(st["zero"], g + 1)
                for hd in range(2):
                    rows = slice(hd * GLA_C, (hd + 1) * GLA_C)
                    e, more = 4 * g + 2 * hd, g + 1 < GLA_PAIRS or hd == 0
                    m = M_GLA + 2 * g + hd
                    if hd == 0:
                        split_lo(U, N_U_GLA + 3 * g + 1)
                    for i in range(2):
                        dve.wait_ge(st["att"], e + i + 1)
                        for r in range(2):
                            rr = slice(r * GLA_C, (r + 1) * GLA_C)
                            ve.tensor_copy(att_t[rr, 4 * i:4 * i + 4, rr], slot3(ps[rr, i, :])[:, :, rr]).then_inc(st["att_read"], 1)
                    for n in range(NC - 1):
                        kv = kv_psum(rows, n)
                        if n % 8 == 0:
                            dve.wait_ge(st["kv"], e + n // 8 + 1)
                        if n == 0:
                            s_next = ve.tensor_copy(states[rows, 1, :], kv)
                        else:
                            dve.drain()
                            s_next = ve.scalar_tensor_tensor(out=states[rows, n + 1, :], in0=states[rows, n, :],
                                                             scalar=decay[rows, n:n + 1], in1=kv, op0=ALU.mult, op1=ALU.add)
                        if n in (7, NC - 2):
                            s_next.then_inc(st["state"], 1)
                    gla_out(U, N_U_GLA + 3 * g + 1 + hd, r_act)
                    if more:
                        split_lo(G, N_G_GLA + 3 * g + 2 + hd)
                    split_lo(A, m)
                    split_lo(B, m)
                    for t in range(2):
                        dve.wait_ge(st["stat"], e + t + 1)
                        ve.tensor_scalar(mean4[:, 4 * t:4 * t + 4], ps[:, 6 + t, 0:4], EPS, None, ALU.add).then_inc(st["mean"], 1)
                    for t in range(2):
                        dve.wait_ge(st["pow"], e + t + 1)
                        ve.tensor_tensor(slot3(gla_diag[t]), ident[:, :].unsqueeze(1).to_broadcast([P, 4, P]),
                                         rms4[:, 4 * t:4 * t + 4].unsqueeze(2).to_broadcast([P, 4, P]), ALU.mult).then_inc(st["diag"], 1)
                    if more:
                        split_lo(U, N_U_GLA + 3 * g + 2 + hd)
                        if hd:
                            log_a(g + 1)
                    for t in range(2):
                        dve.wait_ge(st["spread"], e + t + 1)
                        dve.wait_ge(st["o_copy"], e + t + 1)
                        ve.scalar_tensor_tensor(out=x_new[:, t, :], in0=o_gla[:, half(t)],
                                                scalar=head_gains[:, 1, 2 * g + hd:2 * g + hd + 1], in1=ps[:, 6 + t, :],
                                                op0=ALU.mult, op1=ALU.mult)
                        dve.drain()
                        dve.wait_ge(st["silu"], e + t + 1)
                        ve.tensor_tensor(x_new[:, t, :], x_new[:, t, :], r_act[:, half(t)], ALU.mult).then_inc(st["h"], 1)
                    for t in range(2):
                        dve.wait_ge(h_hi_done, 2 * m + t + 1)
                        ve.tensor_tensor(h_lo[0][:, half(t)], x_new[:, t, :], f32(h_hi[0][:, half(t)]),
                                         ALU.subtract).then_inc(h_ready, 1)
                    if more and hd:
                        for t in range(2):
                            gla_q(g + 1, t)
                        gla_out(U, N_U_GLA + 3 * g + 3, k_inv)
                    elif more:
                        gla_out(G, N_G_GLA + 3 * g + 2, gv_t)
                    dve.drain()
                    add_all(m, True, None if more else 2)

            split_lo(G, N_G_MEM)
            split_lo(U, N_U_MEM)
            norms(2, N_G_MEM + 1)

            ms = m_step

            def queries(h, s, t):
                nn = N_G_MEM if s == G else N_U_MEM
                dve.wait_ge(gemm_done[s], 2 * nn + t + 1 if h is None else 2 * h + (2 * nn + 18 + t + 1))
                ve.tensor_tensor(q_mem[:, s, half(t)], ps[:, GEMM_BANK[s] + t, :], rs[:, half(t)],
                                 ALU.mult).then_inc(gemm_read[s], 1)

            def low_mem(k):
                dve.wait_ge(ms["hi"], 2 * (k // 2) + 2)
                low = ve.scalar_tensor_tensor(out=memt_lo[:, k, :], in0=ps[:, 4 + k // 2 % 2, (k % 2) * MEM:(k % 2 + 1) * MEM],
                                              scalar=gains[:, GAIN["mem_src"], k:k + 1], in1=f32(memt_hi[:, k, :]),
                                              op0=ALU.mult, op1=ALU.subtract)
                if k % 2:
                    low.then_inc(ms["ready"], 1)

            for k in range(4):
                low_mem(k)
            dve.wait_ge(rs_ready, stat_event(2, 1, 1) + 1)
            for t in range(2):
                for s in (G, U):
                    queries(None, s, t)
            split_lo(U, N_U_MEM + 1)
            for k in range(4, KT):
                low_mem(k)
            with dve.Fori(0, 4) as i:
                for s, nn in ((G, N_G_MEM), (U, N_U_MEM)):
                    split_lo(s, i + (nn + 2))
            with dve.Fori(0, 4) as i:
                for s, nn in ((G, N_G_MEM), (U, N_U_MEM)):
                    dve.wait_ge(gemm_done[s], 2 * i + (2 * nn + 12))
                    for r in range(2):
                        ve.tensor_copy(mem_vt[:, s, r * P:(r + 1) * P],
                                       ps[:, GEMM_BANK[s], r * P:(r + 1) * P]).then_inc(gemm_read[s], 1)
                    split_lo(s, i + (nn + 6))

            def mem_head(h, more):
                def maximum(j):
                    dve.wait_ge(ms["score"], 8 * h + (j + 1))
                    ve.tensor_reduce(out=mem_max[:, j:j + 1], in_=ps[:, j, 0:MEM], op=ALU.max, axis=AX.X,
                                     negate=True).then_inc(ms["max"], 1)

                def divide(j):
                    dve.wait_ge(ms["exp"], 8 * h + (j + 1))
                    ve.reciprocal(mem_inv[:, j:j + 1], mem_sum[:, j:j + 1])
                    dve.drain()
                    ve.tensor_scalar(mem_p[:, j, :], mem_p[:, j, :], mem_inv[:, j:j + 1], None,
                                     ALU.mult).then_inc(ms["scaled"], 1)

                dve.drain()
                for j in range(8):
                    maximum(j)
                for j in range(8):
                    divide(j)
                if more:
                    queries(h, G, 0)
                for s in (A, B):
                    split_lo(s, 2 * h + M_MEM)
                if more:
                    queries(h, G, 1)
                for c in range(2):
                    low(h, 0, c)
                if more:
                    queries(h, U, 0)
                for c in range(2):
                    low(h, 1, c)
                if more:
                    queries(h, U, 1)
                if more:
                    split_lo(G, h + (N_G_MEM + 10))
                    split_lo(U, h + (N_U_MEM + 10))
                dve.wait_ge(y_zero, 24)
                add_all(2 * h + M_MEM, not more, next_a=2 * h + (M_MEM + 1))
                split_lo(B, 2 * h + (M_MEM + 1))
                add_all(2 * h + (M_MEM + 1), not more, None if more else 3)

            def low(h, t, c):
                dve.wait_ge(h_hi_done, 4 * h + (2 * M_MEM + 2 * t + c + 1))
                ve.tensor_tensor(h_lo[2 * c][:, half(t)], ps[:, 6 + c, :], f32(h_hi[2 * c][:, half(t)]),
                                 ALU.subtract).then_inc(h_ready, 1)

            with dve.Fori(0, MEM_H - 1) as h:
                mem_head(h, True)
            mem_head(MEM_H - 1, False)

            norms(3, N_G_FF2 + 1)
            ff(2)
            norms(4, None)
            for j in range(3, NT):
                write_out(j)


def kernel(**inputs):
    import numpy as np
    import concourse.bacc as bacc
    from concourse.bass_utils import run_bass_kernel_spmd

    nc = bacc.Bacc("TRN2", target_bir_lowering=False, num_devices=1)
    arrays, args = {}, []
    for name in NAMES:
        a = np.ascontiguousarray(inputs[name])
        arrays["in_" + name] = a
        args.append(nc.dram_tensor("in_" + name, a.shape, mybir.dt.from_np(a.dtype), kind="ExternalInput").ap())
    args.append(nc.dram_tensor("out_x", (1, T, D), F32, kind="ExternalOutput").ap())
    build_layer(nc, *args)
    r = run_bass_kernel_spmd(nc, [arrays], core_ids=[0])
    return r.results[0]["out_x"]


NAMES = ["x", "mem", "g_ff1_pre", "w_ff1_gate", "w_ff1_up", "w_ff1_down", "g_ff1_post",
         "g_mix_pre", "w_mix_in", "b_fox_f", "w_gla_g2", "b_gla_g", "g_fox_out", "g_gla_out",
         "w_mix_out", "g_mix_post", "g_mem_pre", "g_mem_src", "w_mem_q", "w_mem_kv", "w_mem_o",
         "g_mem_post", "g_ff2_pre", "w_ff2_gate", "w_ff2_up", "w_ff2_down", "g_ff2_post", "g_final"]
```
